# Optimizing a Trainium2 kernel written in Bass

```python
import math
import jax
import jax.numpy as jnp
from jax import lax
import numpy as np

D_MODEL = 1024
BATCH = 1
SEQ = 256
DEPTH = 1

GRID_W = 64
CTX_LEN = 256
EPS = 1e-6

GLA_HEADS = 4
GLA_DK = 64
GLA_DV = 128
GLA_QK = GLA_HEADS * GLA_DK
GLA_V = GLA_HEADS * GLA_DV
GLA_RANK = 16
GLA_GATE_NORM = 16.0
GLA_CHUNK = 16

SSD_HEADDIM = 64
SSD_INNER = 512
SSD_HEADS = SSD_INNER // SSD_HEADDIM
SSD_GROUPS = 2
SSD_HEADS_PER_GROUP = SSD_HEADS // SSD_GROUPS
SSD_STATE = 128
SSD_CHUNK = 128
SSD_CONV_DIM = SSD_INNER + 2 * SSD_GROUPS * SSD_STATE
SSD_CONV_K = 3

MIX_WIDTH = GLA_V + SSD_INNER

IN_SPLITS = (GLA_QK, GLA_QK, GLA_V, GLA_V, GLA_RANK, SSD_INNER, SSD_CONV_DIM, SSD_HEADS)
IN_DIM = sum(IN_SPLITS)
IN_OFFSETS = tuple(int(o) for o in np.cumsum(IN_SPLITS)[:-1])

N_EXPERTS = 32
TOP_K = 4
D_FF = 1024
SWIGLU_LIMIT = 7.0
SWIGLU_ALPHA = 1.702
MOE_BLOCK = 256

kernel_name = "hybrid_gla_ssd_moe_prefix_dit"

def rmsnorm(x, w):
    x32 = x.astype(jnp.float32)
    y = x32 * lax.rsqrt(jnp.mean(x32 * x32, axis=-1, keepdims=True) + EPS)
    return (y * w.astype(jnp.float32)).astype(x.dtype)

def modulate(h, shift, scale):
    return h * (1.0 + scale) + shift

def _identity(a):
    return a

def _flip(a):
    return jnp.flip(a, axis=1)

def gla_scan(q, k, v, log_a, s0):
    Bsz, L, H, DK = q.shape
    DV = v.shape[-1]
    C = GLA_CHUNK
    n = L // C
    qc = q.reshape(Bsz, n, C, H, DK).astype(jnp.float32)
    kc = k.reshape(Bsz, n, C, H, DK).astype(jnp.float32)
    vc = v.reshape(Bsz, n, C, H, DV).astype(jnp.float32)
    b = jnp.cumsum(log_a.reshape(Bsz, n, C, H, DK).astype(jnp.float32), axis=2)
    b_last = b[:, :, -1]
    mask = jnp.tril(jnp.ones((C, C), dtype=bool))[:, :, None, None]
    decay = jnp.exp(jnp.where(mask, b[:, :, :, None] - b[:, :, None], -jnp.inf))
    scores = jnp.einsum('bnihd,bnijhd,bnjhd->bnhij', qc, decay, kc)
    o_intra = jnp.einsum('bnhij,bnjhv->bnihv', scores, vc)
    q_dec = qc * jnp.exp(b)
    k_dec = kc * jnp.exp(b_last[:, :, None] - b)
    u = jnp.einsum('bnjhd,bnjhv->bnhdv', k_dec, vc)

    def step(S, inp):
        qd, uc, a_tot = inp
        o = jnp.einsum('bihd,bhdv->bihv', qd, S)
        return S * a_tot[..., None] + uc, o

    s_fin, o_inter = lax.scan(step, s0, (jnp.moveaxis(q_dec, 1, 0), jnp.moveaxis(u, 1, 0),
                                         jnp.moveaxis(jnp.exp(b_last), 1, 0)))
    o = o_intra + jnp.moveaxis(o_inter, 0, 1)
    return o.reshape(Bsz, L, H, DV).astype(v.dtype), s_fin

def ssd_scan(xh, dt, A, Bm, Cm, s0):
    Bsz, L, G, R, P = xh.shape
    N = Bm.shape[-1]
    C = SSD_CHUNK
    n = L // C
    dt32 = dt.astype(jnp.float32)
    a = (dt32 * A).reshape(Bsz, n, C, G, R)
    xdt = (xh.astype(jnp.float32) * dt32[..., None]).reshape(Bsz, n, C, G, R, P)
    Bc = Bm.reshape(Bsz, n, C, G, N).astype(jnp.float32)
    Cc = Cm.reshape(Bsz, n, C, G, N).astype(jnp.float32)
    acum = jnp.cumsum(a, axis=2)
    mask = jnp.tril(jnp.ones((C, C), dtype=bool))[:, :, None, None]
    seg = jnp.exp(jnp.where(mask, acum[:, :, :, None] - acum[:, :, None], -jnp.inf))
    cb = jnp.einsum('bnigs,bnjgs->bnijg', Cc, Bc)
    y_diag = jnp.einsum('bnijg,bnijgr,bnjgrp->bnigrp', cb, seg, xdt)
    a_last = acum[:, :, -1]
    w_state = jnp.exp(a_last[:, :, None] - acum)
    u = jnp.einsum('bnjgs,bnjgr,bnjgrp->bngrps', Bc, w_state, xdt)
    c_dec = jnp.exp(acum)

    def step(S, inp):
        cn, cd, uc, a_tot = inp
        o = jnp.einsum('bigs,bigr,bgrps->bigrp', cn, cd, S)
        return S * a_tot[..., None, None] + uc, o

    s_fin, y_off = lax.scan(step, s0, (jnp.moveaxis(Cc, 1, 0), jnp.moveaxis(c_dec, 1, 0),
                                       jnp.moveaxis(u, 1, 0), jnp.moveaxis(jnp.exp(a_last), 1, 0)))
    y = y_diag + jnp.moveaxis(y_off, 0, 1)
    return y.reshape(Bsz, L, G, R, P).astype(xh.dtype), s_fin

def gla_heads(q, k, v):
    Bsz, L, _ = q.shape
    return (q.reshape(Bsz, L, GLA_HEADS, GLA_DK) * (GLA_DK ** -0.5),
            k.reshape(Bsz, L, GLA_HEADS, GLA_DK),
            v.reshape(Bsz, L, GLA_HEADS, GLA_DV))

def gla_log_decay(gk_low, w_up, b_up):
    Bsz, L, _ = gk_low.shape
    g = jax.nn.log_sigmoid((gk_low @ w_up + b_up).astype(jnp.float32)) / GLA_GATE_NORM
    return g.reshape(Bsz, L, GLA_HEADS, GLA_DK)

def gla_output(o, g, w_norm):
    Bsz, L = o.shape[:2]
    y = rmsnorm(o, w_norm) * jax.nn.silu(g.reshape(Bsz, L, GLA_HEADS, GLA_DV))
    return y.reshape(Bsz, L, GLA_V)

def gla_mixer(p, pc, w_gk_up, b_gk, w_norm, with_ctx):
    q, k, v, g, gk_low = p
    qc, kc, vc, gc, gkc_low = pc
    ql, kl, vl = gla_heads(q, k, v)
    qx, kx, vx = gla_heads(qc, kc, vc)
    s0 = jnp.zeros((qx.shape[0], GLA_HEADS, GLA_DK, GLA_DV), jnp.float32)
    o_lat, o_ctx = None, None
    for d in range(2):
        f = _identity if d == 0 else _flip
        ld_c = gla_log_decay(gkc_low, w_gk_up[d], b_gk[d])
        ld_l = gla_log_decay(gk_low, w_gk_up[d], b_gk[d])
        oc, sc = gla_scan(f(qx), f(kx), f(vx), f(ld_c), s0)
        ol, _ = gla_scan(f(ql), f(kl), f(vl), f(ld_l), sc)
        o_lat = f(ol) if o_lat is None else o_lat + f(ol)
        o_ctx = f(oc) if o_ctx is None else o_ctx + f(oc)
    y = gla_output(o_lat, g, w_norm)
    yc = gla_output(o_ctx, gc, w_norm) if with_ctx else None
    return y, yc

def conv_latent(xbc, w, b):
    Bsz, L, Ch = xbc.shape
    rows = L // GRID_W
    y = lax.conv_general_dilated(xbc.reshape(Bsz, rows, GRID_W, Ch), w[:, :, None, :], (1, 1), 'SAME',
                                 dimension_numbers=('NHWC', 'HWIO', 'NHWC'), feature_group_count=Ch)
    return jax.nn.silu(y.reshape(Bsz, L, Ch) + b)

def conv_context(xbc, w, b):
    Ch = xbc.shape[-1]
    y = lax.conv_general_dilated(xbc, w[1][:, None, :], (1,), 'SAME',
                                 dimension_numbers=('NWC', 'WIO', 'NWC'), feature_group_count=Ch)
    return jax.nn.silu(y + b)

def ssd_heads(xbc_act):
    Bsz, L, _ = xbc_act.shape
    xs, Bm, Cm = jnp.split(xbc_act, [SSD_INNER, SSD_INNER + SSD_GROUPS * SSD_STATE], axis=-1)
    return (xs.reshape(Bsz, L, SSD_GROUPS, SSD_HEADS_PER_GROUP, SSD_HEADDIM),
            Bm.reshape(Bsz, L, SSD_GROUPS, SSD_STATE),
            Cm.reshape(Bsz, L, SSD_GROUPS, SSD_STATE))

def ssd_output(y, z, w_norm):
    Bsz, L = y.shape[:2]
    u = (y.reshape(Bsz, L, SSD_INNER) * jax.nn.silu(z)).reshape(Bsz, L, SSD_GROUPS, SSD_INNER // SSD_GROUPS)
    return rmsnorm(u, w_norm.reshape(SSD_GROUPS, SSD_INNER // SSD_GROUPS)).reshape(Bsz, L, SSD_INNER)

def ssd_mixer(p, pc, conv_w, conv_b, dt_bias, A_log, D_skip, w_norm, with_ctx):
    z, xbc, dt_raw = p
    zc, xbcc, dtc_raw = pc
    xl, Bl, Cl = ssd_heads(conv_latent(xbc, conv_w, conv_b))
    xc, Bc, Cc = ssd_heads(conv_context(xbcc, conv_w, conv_b))
    Dg = D_skip.reshape(SSD_GROUPS, SSD_HEADS_PER_GROUP, 1)
    y_lat = Dg * xl
    y_ctx = Dg * xc
    gr = (SSD_GROUPS, SSD_HEADS_PER_GROUP)
    s0 = jnp.zeros((xc.shape[0], SSD_GROUPS, SSD_HEADS_PER_GROUP, SSD_HEADDIM, SSD_STATE), jnp.float32)
    for d in range(2):
        f = _identity if d == 0 else _flip
        A = -jnp.exp(A_log[d].astype(jnp.float32)).reshape(gr)
        bias = dt_bias[d].astype(jnp.float32)
        dtl = jax.nn.softplus(dt_raw.astype(jnp.float32) + bias).reshape(dt_raw.shape[:2] + gr)
        dtc = jax.nn.softplus(dtc_raw.astype(jnp.float32) + bias).reshape(dtc_raw.shape[:2] + gr)
        yc, sc = ssd_scan(f(xc), f(dtc), A, f(Bc), f(Cc), s0)
        yl, _ = ssd_scan(f(xl), f(dtl), A, f(Bl), f(Cl), sc)
        y_lat = y_lat + f(yl)
        y_ctx = y_ctx + f(yc)
    y = ssd_output(y_lat, z, w_norm)
    yc_out = ssd_output(y_ctx, zc, w_norm) if with_ctx else None
    return y, yc_out

def moe_ffn(h, w_router, b_router, w_gate_up, b_gate_up, w_down, b_down):
    T, D = h.shape
    logits = (h @ w_router + b_router).astype(jnp.float32)
    top_val, top_idx = lax.top_k(logits, TOP_K)
    gates = jax.nn.softmax(top_val, axis=-1).astype(h.dtype)
    A_n = T * TOP_K
    flat_e = top_idx.reshape(-1).astype(jnp.int32)
    flat_tok = jnp.repeat(jnp.arange(T, dtype=jnp.int32), TOP_K)
    flat_w = gates.reshape(-1)
    order = jnp.argsort(flat_e)
    se, stok, sw = flat_e[order], flat_tok[order], flat_w[order]
    counts = jnp.bincount(flat_e, length=N_EXPERTS).astype(jnp.int32)
    padded = ((counts + MOE_BLOCK - 1) // MOE_BLOCK) * MOE_BLOCK
    start = jnp.cumsum(counts) - counts
    pend = jnp.cumsum(padded)
    pstart = pend - padded
    dest = pstart[se] + (jnp.arange(A_n, dtype=jnp.int32) - start[se])
    n_blocks = -(-A_n // MOE_BLOCK) + N_EXPERTS
    P = n_blocks * MOE_BLOCK
    tok_buf = jnp.full((P,), T, jnp.int32).at[dest].set(stok)
    w_buf = jnp.zeros((P,), h.dtype).at[dest].set(sw)
    blk_e = jnp.minimum(jnp.searchsorted(pend, jnp.arange(n_blocks, dtype=jnp.int32) * MOE_BLOCK,
                                         side='right'), N_EXPERTS - 1)
    h_pad = jnp.concatenate([h, jnp.zeros((1, D), h.dtype)], axis=0)

    def expert_block(args):
        e, toks, wts = args
        xb = h_pad[toks]
        gu = xb @ w_gate_up[e] + b_gate_up[e]
        gate, up = gu[:, :D_FF], gu[:, D_FF:]
        gate = jnp.minimum(gate, SWIGLU_LIMIT)
        up = jnp.clip(up, -SWIGLU_LIMIT, SWIGLU_LIMIT)
        glu = gate * jax.nn.sigmoid(SWIGLU_ALPHA * gate)
        y = ((up + 1.0) * glu) @ w_down[e] + b_down[e]
        return y * wts[:, None]

    y = lax.map(expert_block, (blk_e, tok_buf.reshape(n_blocks, MOE_BLOCK), w_buf.reshape(n_blocks, MOE_BLOCK)))
    out = jnp.zeros((T + 1, D), h.dtype).at[tok_buf].add(y.reshape(P, D).astype(h.dtype))
    return out[:T]

def setup_inputs(seed: int = 0) -> dict:
    key = jax.random.key(seed)
    ks = jax.random.split(key, 26)

    def nrm(k, shape, scale):
        return jax.random.normal(k, shape, jnp.float32) * scale

    dt0 = jnp.exp(jax.random.uniform(ks[13], (DEPTH, 2, SSD_HEADS), jnp.float32,
                                     minval=math.log(1e-3), maxval=math.log(1e-1)))
    return {
        "x": nrm(ks[0], (BATCH, SEQ, D_MODEL), 1.0),
        "c": nrm(ks[1], (BATCH, D_MODEL), 1.0),
        "ctx": nrm(ks[2], (BATCH, CTX_LEN, D_MODEL), 1.0),
        "c_ctx": nrm(ks[3], (D_MODEL,), 1.0),
        "w_mod": nrm(ks[4], (DEPTH, D_MODEL, 6 * D_MODEL), D_MODEL ** -0.5),
        "b_mod": nrm(ks[5], (DEPTH, 6 * D_MODEL), 0.02),
        "norm1": 1.0 + nrm(ks[6], (DEPTH, D_MODEL), 0.02),
        "w_in": nrm(ks[7], (DEPTH, D_MODEL, IN_DIM), D_MODEL ** -0.5),
        "gla_w_gk_up": nrm(ks[8], (DEPTH, 2, GLA_RANK, GLA_QK), GLA_RANK ** -0.5),
        "gla_b_gk": nrm(ks[9], (DEPTH, 2, GLA_QK), 0.1),
        "gla_norm": 1.0 + nrm(ks[10], (DEPTH, GLA_DV), 0.02),
        "ssd_conv_w": nrm(ks[11], (DEPTH, SSD_CONV_K, SSD_CONV_K, SSD_CONV_DIM), 1.0 / SSD_CONV_K),
        "ssd_conv_b": nrm(ks[12], (DEPTH, SSD_CONV_DIM), 0.02),
        "ssd_dt_bias": dt0 + jnp.log(-jnp.expm1(-dt0)),
        "ssd_A_log": jnp.log(jax.random.uniform(ks[14], (DEPTH, 2, SSD_HEADS), jnp.float32, minval=1.0, maxval=16.0)),
        "ssd_D": 1.0 + nrm(ks[15], (DEPTH, SSD_HEADS), 0.02),
        "ssd_norm": 1.0 + nrm(ks[16], (DEPTH, SSD_INNER), 0.02),
        "w_out": nrm(ks[17], (DEPTH, MIX_WIDTH, D_MODEL), MIX_WIDTH ** -0.5),
        "norm2": 1.0 + nrm(ks[18], (DEPTH, D_MODEL), 0.02),
        "w_router": nrm(ks[19], (DEPTH, D_MODEL, N_EXPERTS), D_MODEL ** -0.5),
        "b_router": nrm(ks[20], (DEPTH, N_EXPERTS), 0.01),
        "w_gate_up": nrm(ks[21], (DEPTH, N_EXPERTS, D_MODEL, 2 * D_FF), D_MODEL ** -0.5),
        "b_gate_up": nrm(ks[22], (DEPTH, N_EXPERTS, 2 * D_FF), 0.01),
        "w_down": nrm(ks[23], (DEPTH, N_EXPERTS, D_FF, D_MODEL), D_FF ** -0.5),
        "b_down": nrm(ks[24], (DEPTH, N_EXPERTS, D_MODEL), 0.01),
        "final_norm": 1.0 + nrm(ks[25], (D_MODEL,), 0.02),
    }

def reference(x, c, ctx, c_ctx, w_mod, b_mod, norm1, w_in, gla_w_gk_up, gla_b_gk, gla_norm,
              ssd_conv_w, ssd_conv_b, ssd_dt_bias, ssd_A_log, ssd_D, ssd_norm, w_out,
              norm2, w_router, b_router, w_gate_up, b_gate_up, w_down, b_down, final_norm):
    Bsz, L, D = x.shape
    xc = ctx
    for l in range(DEPTH):
        update_ctx = l < DEPTH - 1
        mod = (jax.nn.silu(c) @ w_mod[l] + b_mod[l])[:, None, :]
        mod_c = jax.nn.silu(c_ctx) @ w_mod[l] + b_mod[l]
        sh1, sc1, g1, sh2, sc2, g2 = jnp.split(mod, 6, axis=-1)
        sh1c, sc1c, g1c, sh2c, sc2c, g2c = jnp.split(mod_c, 6, axis=-1)
        h = modulate(rmsnorm(x, norm1[l]), sh1, sc1)
        hc = modulate(rmsnorm(xc, norm1[l]), sh1c, sc1c)
        p = jnp.split(h @ w_in[l], IN_OFFSETS, axis=-1)
        pc = jnp.split(hc @ w_in[l], IN_OFFSETS, axis=-1)
        y_gla, yc_gla = gla_mixer(p[:5], pc[:5], gla_w_gk_up[l], gla_b_gk[l], gla_norm[l], update_ctx)
        y_ssd, yc_ssd = ssd_mixer(p[5:], pc[5:], ssd_conv_w[l], ssd_conv_b[l], ssd_dt_bias[l],
                                  ssd_A_log[l], ssd_D[l], ssd_norm[l], update_ctx)
        x = x + g1 * (jnp.concatenate([y_gla, y_ssd], axis=-1) @ w_out[l])
        h2 = modulate(rmsnorm(x, norm2[l]), sh2, sc2).reshape(Bsz * L, D)
        if update_ctx:
            xc = xc + g1c * (jnp.concatenate([yc_gla, yc_ssd], axis=-1) @ w_out[l])
            h2c = modulate(rmsnorm(xc, norm2[l]), sh2c, sc2c).reshape(-1, D)
            f_all = moe_ffn(jnp.concatenate([h2, h2c], axis=0), w_router[l], b_router[l],
                            w_gate_up[l], b_gate_up[l], w_down[l], b_down[l])
            x = x + g2 * f_all[:Bsz * L].reshape(Bsz, L, D)
            xc = xc + g2c * f_all[Bsz * L:].reshape(xc.shape)
        else:
            f_lat = moe_ffn(h2, w_router[l], b_router[l], w_gate_up[l], b_gate_up[l], w_down[l], b_down[l])
            x = x + g2 * f_lat.reshape(Bsz, L, D)
    return rmsnorm(x, final_norm)


_drawn_inputs = setup_inputs


def setup_inputs(seed=0):
    import zlib

    import numpy as np

    out = dict(_drawn_inputs(seed))
    spreads = {}
    factors = {'gla_norm': 8.335,
     'ssd_D': 64.0,
     'ssd_norm': 3.351,
     'b_router': 5.273,
     'b_gate_up': 21.767,
     'b_down': 32.142,
     'final_norm': 7.738,
     'ssd_conv_b': 2.703,
     'norm2': 2.784}
    for name, (base, spread) in spreads.items():
        noise = np.random.default_rng([zlib.crc32(name.encode()), seed]).standard_normal(out[name].shape)
        drawn = base * np.exp(spread * noise) if base else spread * noise
        out[name] = jnp.asarray(drawn.astype(out[name].dtype))
    for name, factor in factors.items():
        out[name] = (out[name] * factor).astype(out[name].dtype)
    return out
```

```python
from contextlib import ExitStack

import concourse.bass as bass
from concourse import mybir

F32 = mybir.dt.float32
I32 = mybir.dt.int32
ALU = mybir.AluOpType
ACT = mybir.ActivationFunctionType
AX = mybir.AxisListType

P = 128
D = 1024
KC = D // P
T = 256
TX = 256
NT = T // P
EPS = 1e-6
GH, DK, DV = 4, 64, 128
RANK = 16
GATE_NORM = 16.0
BLK = 32
NB = T // BLK
CLAMP = 60.0
SH, HP, SG, NS = 8, 64, 2, 128
HPG = SH // SG
SI = SH * HP
GRID = 64
ROWS = T // GRID
NE = 32
FF = 1024
SLOTS = 64
NOV = 16
NJ = NE + NOV
LIMIT, ALPHA = 7.0, 1.702
UNIT = 2048
N_SMALL = 13
NSLOT = 12
FSLOT = 10
N_MOD1, N_IN, N_MOD2, N_OUT = 8, 12, 16, 4
N_FRONT = N_MOD1 + N_IN + N_MOD2 + N_OUT
SPAN = 384


def bc(ap, shape):
    return ap.to_broadcast(shape)


def overflow_tables(nc, v, S, step, cnt, RT, GT, JE, ovi, ov, no32, ones):
    V = nc.vector
    TT, TS, STT = V.tensor_tensor, V.tensor_scalar, V.scalar_tensor_tensor
    total = cnt[:, 2, :]
    extra, incl = cnt[:, 0, :], cnt[:, 1, :]
    step(TS(extra, total, SLOTS + 0.5, None, ALU.is_gt))
    for b in range(2, T // SLOTS):
        step.settle()
        step(STT(out=extra, in0=total, scalar=b * SLOTS + 0.5, in1=extra, op0=ALU.is_gt, op1=ALU.add))
    step.settle()
    step(V.tensor_tensor_scan(incl, bc(ones[:, 0:1], [P, NE]), extra, 0.0, ALU.mult, ALU.add))
    step.settle()
    step(TT(extra, incl, extra, ALU.subtract))
    q, own, w, base = ov
    row = lambda ap, n: bc(ap.rearrange("p (a e) -> p a e", a=1), [P, n, NE])
    number = bc(no32[:, 0:NOV].rearrange("p (i a) -> p i a", a=1), [P, NOV, NE])
    step.settle()
    step(TT(q, number, row(extra, NOV), ALU.subtract))
    step(TT(w, number, row(incl, NOV), ALU.subtract))
    step.settle()
    step(TS(own, q, 0.0, None, ALU.is_ge))
    step(TS(w, w, 0.0, None, ALU.is_lt))
    step(TS(base, q, 1.0, float(SLOTS), ALU.add, ALU.mult))
    step.settle()
    step(TT(own, own, w, ALU.mult))
    step.settle()
    step(TT(w, own, row(no32, NOV), ALU.mult))
    step.settle()
    step(V.tensor_reduce(JE[:, NE:NJ], w, AX.X, ALU.add))
    step.settle()
    step(V.tensor_copy(ovi[:, 0:NOV], JE[:, NE:NJ]))
    for t in range(2):
        step(TT(w, own, row(GT[:, t, 0:NE], NOV), ALU.mult))
        step.settle()
        step(V.tensor_reduce(GT[:, t, NE:NJ], w, AX.X, ALU.add))
        step.settle()
        step(TT(w, row(RT[:, t, 0:NE], NOV), base, ALU.subtract))
        step.settle()
        step(STT(out=w, in0=w, scalar=1.0, in1=own, op0=ALU.add, op1=ALU.mult))
        step.settle()
        step(V.tensor_reduce(RT[:, t, NE:NJ], w, AX.X, ALU.add))
        step.settle()
        step(TS(RT[:, t, NE:NJ], RT[:, t, NE:NJ], -1.0, None, ALU.add))
    V.tensor_copy(ovi[:, NOV:NOV + 1], incl[:, NE - 1:NE]).then_inc(S["ovtab"], 1)
    step.settle()


def layer_kernel(nc, A, out):
    with ExitStack() as ctx:
        def sb(name, cols, parts=P, dt=F32):
            return ctx.enter_context(nc.sbuf_tensor(name, [parts, cols], dt))[:]

        def sem(name):
            return ctx.enter_context(nc.semaphore(name))

        ring = sb("ring", NSLOT * UNIT)
        bank = [ctx.enter_context(nc.psum_tensor(f"bank{i}", [P, 512], F32))[:] for i in range(8)]

        def slot(i):
            return ring[:, i * UNIT:(i + 1) * UNIT]

        conv = ring[:, FSLOT * UNIT:].rearrange("p (m t) -> p m t", m=8)
        o_sb = ring[:, FSLOT * UNIT:FSLOT * UNIT + 1024]
        y_acc = ring[:, FSLOT * UNIT + 1024:FSLOT * UNIT + 2048]

        hA = sb("hA", 4096)
        hT = hA.rearrange("p (k t) -> p k t", k=KC)
        xs_tm = hA[:, 0:2048].rearrange("p (t c) -> p t c", t=4)
        xdt = hA[:, 2048:4096].rearrange("p (t d c) -> p t d c", t=2, d=2)
        brows = hA[0:NE, 0:3072]

        cB = sb("cB", 4096)
        xbc = cB.rearrange("p (m t) -> p m t", m=8)
        xw = cB[:, 0:2048].rearrange("p (t d c) -> p t d c", t=2, d=2)
        cbm = cB[:, 2048:2048 + 4 * SPAN].rearrange("p (d g c) -> p d g c", d=2, g=2)
        b_tm = cB[:, 3584:4096].rearrange("p (t g s) -> p t g s", t=2, g=2)
        mixT = cB[:, 0:2048].rearrange("p (k t) -> p k t", k=KC)
        h2 = cB[:, 2048:4096].rearrange("p (t c) -> p t c", t=NT)

        dB = sb("dB", 2048)
        k_fm = dB[:, 0:1024].rearrange("p (c t) -> p c t", c=2)
        q_fm = dB[:, 1024:1536].rearrange("p (c t) -> p c t", c=2)
        gk_fm = dB[0:RANK, 1536:2048]
        n2row = dB[:, 0:1024]
        fnrow = dB[:, 1024:2048]

        fB = sb("fB", 4096)
        vgz = fB[:, 0:3072].rearrange("p (t c) -> p t c", t=2)
        vx = fB[:, 3072:4096].rearrange("p (t c) -> p t c", t=2)
        h2T = fB[:, 0:2048].rearrange("p (k t) -> p k t", k=KC)

        gB = sb("gB", 4 * 2 * 257 + 2 * 1536)
        pre = gB[:, 0:2056].rearrange("p (n s t) -> p n s t", n=4, s=2)
        kv = [gB[:, 2056 + 1536 * i:2056 + 1536 * (i + 1)] for i in range(2)]
        soft = gB[:, 2056:2056 + 2048].rearrange("p (n t) -> p n t", n=4)
        sq = [gB[:, 512 * i:512 * (i + 1)] for i in range(2)]
        rstd1 = gB[:, 1024:1536]
        g1b, sh2b, w2b, g2b = (gB[:, 1024 * i:1024 * (i + 1)] for i in range(4))

        pB = sb("pB", 2560)
        ld = pB[:, 0:2048].rearrange("p (n t) -> p n t", n=4)
        pt = pB[:, 0:4 * SPAN].rearrange("p (d e c) -> p d e c", d=2, e=2)
        seg = [pB[:, SPAN * i:SPAN * (i + 1)] for i in range(4)]
        x_tm = pB[:, 0:2048].rearrange("p (t c) -> p t c", t=2)

        qv = [sb(f"qv{i}", 256) for i in range(2)]
        kx = [sb(f"kx{i}", 256) for i in range(2)]
        qd = sb("qd", 512).rearrange("p (d t) -> p d t", d=2)
        kxT = sb("kxT", 256)
        gS = sb("gS", 256).rearrange("p (d v) -> p d v", d=2)
        sS = sb("sS", 1024).rearrange("p (d c) -> p d c", d=2)
        mask = [sb(f"mask{d}", SPAN) for d in range(2)]
        upper, ones, lower = mask[0][:, 0:P], mask[0][:, P:2 * P], mask[1][:, 0:P]
        s_upper, s_lower, ident = sb("s_upper", P), sb("s_lower", P), sb("ident", P)
        slot_no = sb("slot_no", 2 * SLOTS)
        part_no = sb("part_no", SLOTS)
        no32 = slot_no[:, 0:NE]
        zeros = qv[0][:, 0:P]
        cs = sb("cs", KC * 32).rearrange("p (k c) -> p k c", k=KC)
        c_in = sb("c_in", KC * 2).rearrange("p (k c) -> p k c", k=KC)
        modrow = sb("modrow", 1024).rearrange("p (r c) -> p r c", r=2)
        modrow1 = pB[:, 2048:2560]
        modc = sb("modc", 32).rearrange("p (g c) -> p g c", g=16)
        bmodT, n1T = sb("bmodT", 16), sb("n1T", KC)
        bgk = sb("bgk", 4)
        wup = dB[0:RANK, 1024:1536].rearrange("r (d c) -> r d c", d=2)
        wgk = pB[:, 0:KC * RANK].rearrange("p (k c) -> p k c", k=KC)
        wdt = sb("wdt", KC * SH).rearrange("p (k c) -> p k c", k=KC)
        convw = sb("convw", 72).rearrange("p (m j) -> p m j", m=8)
        convb = sb("convb", 8)
        gnrow, snrow = sb("gnrow", DV), pB[:, 2048:2560]
        d_row, dtb, negA = sb("d_row", SH), sb("dtb", 16), sb("negA", 16)
        dtb3, negA3 = (v.rearrange("p (d h) -> p d h", d=2) for v in (dtb, negA))
        dtr = sb("dtr", 4 * SH).rearrange("p (t h) -> p t h", t=4)
        dta = sb("dta", 64).rearrange("p (t d h) -> p t d h", t=4, d=2)
        dtt = sb("dtt", 64).rearrange("p (t d h) -> p t d h", t=4, d=2)
        a_tm = sb("a_tm", 64).rearrange("p (t d h) -> p t d h", t=4, d=2)
        acol = sb("acol", 64).rearrange("p (t d h) -> p t d h", t=4, d=2)
        eac = sb("eac", 64).rearrange("p (t d h) -> p t d h", t=4, d=2)
        stat = sb("stat", 32)
        wr = gS.rearrange("p d v -> p (d v)").rearrange("p (k e) -> p k e", k=KC)
        brrow = sb("brrow", NE)
        lg = fB[:, 3776:3840].rearrange("p (t e) -> p t e", t=2)
        top8 = fB[:, 3840:3856].rearrange("p (t e) -> p t e", t=2)
        rt = [kxT[:, 64 * i:64 * i + 64].rearrange("p (t e) -> p t e", t=2) for i in range(4)]
        RT, GT = (qv[1][:, i * 2 * (NJ + 1):(i + 1) * 2 * (NJ + 1)].rearrange("p (t j) -> p t j", t=2) for i in range(2))
        JE = sb("JE", NJ + 1)
        cnt = fB[:, 3856:3952].rearrange("p (i e) -> p i e", i=3)
        ovi = sb("ovi", NOV + 1, dt=I32)
        S_j = fB[:, 2048:2176].rearrange("p (t s) -> p t s", t=2)
        SG_j = fB[:, 2176:2432].rearrange("p (t s) -> p t s", t=2)
        SGT = fB[:, 2432:2688].rearrange("p (t c) -> p t c", t=2)
        xg = fB[:, 2688:3200].rearrange("p (k s) -> p k s", k=KC)
        gm = fB[:, 3200:3712]
        sig = sS.rearrange("p d c -> p (d c)")[:, 0:512]
        act = sS.rearrange("p d c -> p (d c)")[:, 512:1024]
        actT = modrow.rearrange("p r c -> p (r c)")[:, 0:512].rearrange("p (q c) -> p q c", q=4)
        ysb = modrow.rearrange("p r c -> p (r c)")[:, 512:1024]
        job_sel = fB[0:NE, 3712:3776]
        ov = [fB[:, 0:512], fB[:, 512:1024], fB[:, 1024:1536], fB[:, 1536:2048]]
        ov = [v.rearrange("p (i e) -> p i e", i=NOV) for v in ov]

        loaded = [sem(f"slot{i}_loaded") for i in range(NSLOT)]
        names = """mod1_used mod2_used cT_in xT_in small_in late_in consts zeroed cs_ready row1_ready
        sq_ready sq_summed sum_done rinv_ready rstd_ready xh_ready h_ready
        fm_done fm_evac gate_done gate_read soft_arg soft_ready
        tm_done tm_evac misc_filled misc_read conv_ready conv_act
        dt_ready dt_exp dt_sp kvarg_ready exp_ready kvmul_ready
        score_done pt_ready o_done o_copied
        sn_in eac_ready negA_ready rb_done arg_ready segexp_ready segm_ready segm_used ydiag_done
        row2_ready rows_ready silu_ready gst sst gsq ssq mix_ready ex_ready ex_done h2_ready sel_made xw_ready seg0
        op_done op_read xnew_ready nsq nst
        s_ready sg_ready sgt_ready sel_ready gather_done xg_ready gu_done gm_ready sig_ready
        act_ready actT_done actT_ready sel_used y_ready sgt_done scat_done moe_used moe_done up_read
        ovtab fsq fst out_ready stored dve act pool mr""".split()
        S = {n: sem(n) for n in names}

        class Steps:

            def __init__(self, eng, sm):
                self.eng, self.sm, self.n = eng, sm, 0

            def __call__(self, ins):
                self.n += 1
                ins.then_inc(self.sm, 1)

            def settle(self):
                self.eng.wait_ge(self.sm, self.n)

        MISC = (bank[2], bank[7])
        M_MODT, M_CB, M_B = 0, 1, 3
        M_GLA = 4
        M_X = 12
        M_ACOL = 16
        M_ST = 17
        M_YOFF = 19
        M_ROWS = 23
        M_MIXT = 31
        M_H2T = 35
        M_LOG = 39
        M_RANK = 40

        def in_item_bank(i):
            return bank[3 + i % 2]

        FM = [("gk", 0, True)] + [("xbc", m, m < 6) for m in range(8)] + [("k", 0, True), ("k", 1, True),
                                                                       ("q", 0, False), ("q", 1, False)]
        TM = [("dt", 0, 0), ("v", 0, 0), ("v", 0, 1), ("v", 1, 0), ("v", 1, 1),
              ("g", 0, 0), ("g", 1, 0), ("z", 0, 0), ("z", 1, 0)]
        U_IN = N_MOD1
        U_MOD2 = U_IN + N_IN
        U_OUT = U_MOD2 + N_MOD2

        def consumed(u):
            if u < U_IN:
                return S["mod1_used"], u + 1
            if u < U_IN + 6:
                return S["fm_done"], 2 * (u - U_IN) + 3
            if u < U_MOD2:
                return S["tm_done"], (3, 5, 6, 7, 8, 9)[u - U_IN - 6]
            if u < U_OUT:
                return S["mod2_used"], u - U_MOD2 + 1
            return S["op_done"], 4

        def front_slot(u):
            return slot(u % FSLOT)

        def await_unit(eng, u):
            eng.wait_ge(loaded[u % FSLOT], 16 * (u // FSLOT + 1))

        GU = A["w_gate_up"].rearrange("e (k p) f -> e k p f", p=P)
        DN = A["w_down"].rearrange("e (i k p) f -> e i p k f", p=P, k=2)

        block = ctx.enter_context(nc.Block())

        @block.sync
        def _(sp):
            sp.dma_start(c_in, A["c2"].rearrange("k p c -> p k c")).then_inc(S["cT_in"], 16)

            def front_unit(u):
                if u >= FSLOT:
                    sp.wait_ge(*consumed(u - FSLOT))
                dst = front_slot(u)
                if u < U_IN:
                    src = A["w_mod"][u * P:(u + 1) * P, 0:UNIT]
                elif u < U_MOD2:
                    src = A["w_in"][u - U_IN]
                elif u < U_OUT:
                    r, k = divmod(u - U_MOD2, KC)
                    src = A["w_mod"][k * P:(k + 1) * P, (r + 1) * UNIT:(r + 2) * UNIT]
                else:
                    i = u - U_OUT
                    src = A["w_out"][2 * i * P:2 * (i + 1) * P, :].rearrange("(k p) n -> p k n", p=P)
                    dst = dst.rearrange("p (k n) -> p k n", k=2)
                sp.dma_start(dst, src).then_inc(loaded[u % FSLOT], 16)

            for u in range(4):
                front_unit(u)
            sp.dma_start(hT[:, :, 0:T], A["xT"].rearrange("k p t -> p k t")).then_inc(S["xT_in"], 16)
            sp.dma_start(hT[:, :, T:T + TX], A["ctxT"].rearrange("k p t -> p k t")).then_inc(S["xT_in"], 16)
            for u in range(4, N_FRONT):
                front_unit(u)

            def expert_unit(i, gate_up, down):
                dst = slot(i)
                if i < KC:
                    sp.dma_start(dst, gate_up[i]).then_inc(loaded[i], 16)
                else:
                    sp.dma_start(dst.rearrange("p (k n) -> p k n", k=2), down[i - KC]).then_inc(loaded[i], 16)

            for i in range(NSLOT):
                if i < FSLOT:
                    sp.wait_ge(*consumed(N_FRONT - FSLOT + i))
                else:
                    sp.wait_ge(S["mix_ready"], 2)
                expert_unit(i, GU[0], DN[0])

            def dyn(e):
                return (GU[bass.ds(e, 1)].rearrange("e k p f -> (e k) p f"),
                        DN[bass.ds(e, 1)].rearrange("e i p k f -> (e i) p k f"))

            with sp.Fori(1, NE) as j:
                g, d = dyn(j)
                for i in range(NSLOT):
                    sp.wait_ge(S["moe_used"], NSLOT * j + (i + 1 - NSLOT))
                    expert_unit(i, g, d)
            sp.wait_ge(S["ovtab"], 1)
            n = sp.value_load(ovi[0:1, NOV:NOV + 1], min_val=0, max_val=NOV)
            with sp.Fori(NE, NJ) as j:
                with sp.If(n > j - NE):
                    e = sp.value_load(ovi[0:1, bass.ds(j - NE, 1)], min_val=0, max_val=NE - 1)
                    g, d = dyn(e)
                    for i in range(NSLOT):
                        sp.wait_ge(S["moe_used"], NSLOT * j + (i + 1 - NSLOT))
                        expert_unit(i, g, d)
            for t in range(NT):
                sp.wait_ge(S["out_ready"], t + 1)
                sp.dma_start(out[0, t * P:(t + 1) * P, :], x_tm[:, t, :]).then_inc(S["stored"], 16)
            sp.wait_ge(S["stored"], 16 * NT)

        @block.gpsimd
        def _(pool):
            step = Steps(pool, S["pool"])
            small = [(bmodT, A["bmodT"]), (n1T, A["n1T"]), (bgk, A["bgk"]), (wup, A["wup"]),
                     (wgk, A["wgk"].rearrange("k p c -> p k c")), (wdt, A["wdt"].rearrange("k p c -> p k c")),
                     (convw, A["convw"]), (convb, A["convb"]),
                     (gnrow, A["gla_norm"].partition_broadcast(P)),
                     (d_row, A["ssd_D"].partition_broadcast(P)), (dtb, A["dtb"].partition_broadcast(P)),
                     (negA, A["alog"].partition_broadcast(P)),
                     (brrow, A["b_router"].partition_broadcast(P))]
            assert len(small) == N_SMALL
            for dst, src in small:
                pool.dma_start(dst, src).then_inc(S["small_in"], 16)
            nc.gpsimd.memset(cs, 0.0).then_inc(S["zeroed"], 1)
            for m in mask:
                step(nc.gpsimd.memset(m, 1.0))
            step(nc.gpsimd.memset(ident, 0.0))
            step(nc.gpsimd.memset(modrow, 0.0))
            step(nc.gpsimd.iota(
                slot_no.rearrange("p (a s) -> p a s", a=2), [[0, 2], [1, SLOTS]], base=0, channel_multiplier=0,
                allow_small_or_imprecise_dtypes=True))
            step(nc.gpsimd.iota(part_no, [[0, SLOTS]], base=0, channel_multiplier=1,
                                allow_small_or_imprecise_dtypes=True))
            step(nc.gpsimd.iota(JE, [[1, NJ + 1]], base=0, channel_multiplier=0, allow_small_or_imprecise_dtypes=True))
            step.settle()
            for d, sgn in ((0, 1), (1, -1)):
                for b in (0, 2):
                    v = mask[d][:, b * P:(b + 1) * P]
                    step(nc.gpsimd.affine_select(out=v, in_=v, compare_op=ALU.is_ge, fill=0.0, base=0,
                                                 pattern=[[sgn, P]], channel_multiplier=-sgn))
            step(nc.gpsimd.affine_select(out=ident, in_=ident, compare_op=ALU.not_equal, fill=1.0, base=0,
                                         pattern=[[-1, P]], channel_multiplier=1))
            step(nc.gpsimd.affine_select(out=s_upper, in_=ones, compare_op=ALU.is_gt, fill=0.0, base=0,
                                         pattern=[[1, P]], channel_multiplier=-1))
            step(nc.gpsimd.affine_select(out=s_lower, in_=ones, compare_op=ALU.is_gt, fill=0.0, base=0,
                                         pattern=[[-1, P]], channel_multiplier=1))
            step.settle()
            nc.gpsimd.memset(stat, 0.0).then_inc(S["consts"], 1)
            for g in range(4):
                pool.dma_start(modrow[32 * g:32 * g + 1], A["b_mod2"][:, g:g + 1, :].rearrange("r g c -> g r c")
                               ).then_inc(S["mr"], 16)
            pool.wait_ge(S["misc_filled"], M_MODT + 1)
            pool.dma_start(snrow, A["ssd_norm"].partition_broadcast(P)).then_inc(S["sn_in"], 16)
            pool.wait_ge(S["kvmul_ready"], 4)
            pool.wait_ge(S["o_done"], 2)
            pool.dma_start(wr, A["w_router"].rearrange("(k p) e -> p k e", p=P)).then_inc(S["late_in"], 16)
            pool.dma_start(n2row, A["norm2"].partition_broadcast(P)).then_inc(S["late_in"], 16)
            pool.dma_start(fnrow, A["final_norm"].partition_broadcast(P)).then_inc(S["late_in"], 16)
            pool.wait_ge(S["ydiag_done"], SH)
            pool.wait_ge(S["segm_ready"], 2 * SH)
            pool.dma_start(x_tm, A["x"].rearrange("(t p) c -> p t c", p=P)).then_inc(S["late_in"], 16)
            pool.wait_ge(S["ssq"], 1)
            pool.dma_start(brows, A["b_moe"]).then_inc(S["late_in"], 16)

        @block.scalar
        def _(sc):
            step = Steps(sc, S["act"])
            A_ = nc.scalar.activation
            sc.wait_ge(S["cT_in"], 16)
            sc.wait_ge(S["zeroed"], 1)
            A_(cs[:, :, 0:2], c_in, ACT.Silu).then_inc(S["cs_ready"], 1)
            sc.wait_ge(S["xT_in"], 32)
            for k in range(KC):
                if k >= 2:
                    sc.wait_ge(S["sq_summed"], k - 1)
                A_(sq[k % 2], hT[:, k, :], ACT.Square).then_inc(S["sq_ready"], 1)
            sc.wait_ge(S["rinv_ready"], 1)
            A_(rstd1, rstd1, ACT.Sqrt).then_inc(S["rstd_ready"], 1)
            for k in range(KC):
                for s in range(2):
                    sc.wait_ge(S["xh_ready"], 2 * k + s + 1)
                    v = hT[:, k, s * T:(s + 1) * T]
                    A_(v, v, ACT.Identity, bias=modc[:, k, s:s + 1]).then_inc(S["h_ready"], 1)

            def fm_evac(i):
                kind, m, with_ctx = FM[i]
                n = T + TX if with_ctx else T
                src = in_item_bank(i)
                sc.wait_ge(S["fm_done"], i + 1)
                if kind == "gk":
                    A_(gk_fm, src[0:RANK, 0:n], ACT.Copy).then_inc(S["fm_evac"], 1)
                elif kind == "xbc":
                    A_(xbc[:, m, 0:n], src[:, 0:n], ACT.Copy).then_inc(S["fm_evac"], 1)
                elif kind == "k":
                    A_(k_fm[:, m, :], src, ACT.Copy).then_inc(S["fm_evac"], 1)
                else:
                    A_(q_fm[:, m, :], src[:, 0:n], ACT.Copy, scale=DK ** -0.5).then_inc(S["fm_evac"], 1)

            def conv_silu(m):
                n = T + TX if m < 6 else T
                sc.wait_ge(S["conv_ready"], m + 1)
                A_(conv[:, m, 0:n], conv[:, m, 0:n], ACT.Silu).then_inc(S["conv_act"], 1)

            for i in range(3):
                fm_evac(i)
            sc.wait_ge(S["soft_arg"], 1)
            step(A_(soft, soft, ACT.Exp))
            step.settle()
            A_(soft, soft, ACT.Ln, bias=1.0).then_inc(S["soft_ready"], 1)
            for i in range(3, len(FM)):
                fm_evac(i)
                if i >= 5:
                    conv_silu(i - 5)

            def tm_evac(i):
                kind, half, c = TM[i]
                b = in_item_bank(len(FM) + i)
                sc.wait_ge(S["tm_done"], i + 1)
                if kind == "dt":
                    A_(dtr, b[:, 0:4 * SH].rearrange("p (t h) -> p t h", t=4), ACT.Copy).then_inc(S["tm_evac"], 1)
                    return
                col = {"v": 0, "g": 512, "z": 1024}[kind] + 256 * half
                dst = (vx if c else vgz)[:, :, col:col + 256]
                A_(dst, b.rearrange("p (t c) -> p t c", t=2), ACT.Copy).then_inc(S["tm_evac"], 1)

            tm_evac(0)
            sc.wait_ge(S["small_in"], 16 * N_SMALL)
            A_(negA, negA, ACT.Exp).then_inc(S["negA_ready"], 1)
            sc.wait_ge(S["dt_ready"], 1)
            step(A_(dtt, dtt, ACT.Exp))
            step.settle()
            A_(dtt, dtt, ACT.Ln, bias=1.0).then_inc(S["dt_sp"], 1)

            def decay_exps(n):
                d = n % 2
                b = n % 2
                up = 1.0 / GATE_NORM
                sc.wait_ge(S["kvarg_ready"], n + 1)
                sgn = -1.0 if d == 0 else 1.0
                A_(kv[b], kv[b], ACT.Exp, scale=sgn * up).then_inc(S["exp_ready"], 1)
                A_(qv[b], qv[b], ACT.Exp, scale=-sgn * up).then_inc(S["exp_ready"], 1)
                if n >= 2:
                    sc.wait_ge(S["o_done"], 1)
                if d == 0:
                    A_(qd[:, 0, :], pre[:, n, 0, 1:T + 1], ACT.Exp, scale=up).then_inc(S["exp_ready"], 1)
                    A_(kx[b], pre[:, n, 1, 1:TX + 1], ACT.Exp, scale=-up,
                       bias=stat[:, 16 + n:17 + n]).then_inc(S["exp_ready"], 1)
                else:
                    A_(qd[:, 1, :], pre[:, n, 0, 0:T], ACT.Exp, scale=-up,
                       bias=stat[:, 16 + n:17 + n]).then_inc(S["exp_ready"], 1)
                    A_(kx[b], pre[:, n, 1, 0:TX], ACT.Exp, scale=up).then_inc(S["exp_ready"], 1)

            def o_copy(c):
                sc.wait_ge(S["o_done"], c + 1)
                ov_ = o_sb.rearrange("p (t h v) -> p t h v", t=2, h=GH)
                for e in range(2):
                    src = bank[5 + e].rearrange("p (t c v) -> p t c v", t=2, c=2)[:, :, c, :]
                    A_(ov_[:, :, 2 * c + e, :], src, ACT.Copy).then_inc(S["o_copied"], 1)

            decay_exps(0)
            for i in range(1, 5):
                tm_evac(i)
            decay_exps(1)
            tm_evac(5)
            decay_exps(2)
            tm_evac(6)
            tm_evac(7)
            decay_exps(3)
            tm_evac(8)
            sc.wait_ge(S["misc_filled"], M_X + 4)
            o_copy(0)
            o_copy(1)
            sc.wait_ge(S["misc_read"], M_ACOL + 1)
            A_(eac, acol, ACT.Exp).then_inc(S["eac_ready"], 1)
            for i in range(2 * SH):
                sc.wait_ge(S["arg_ready"], i + 1)
                A_(seg[i % 4], seg[i % 4], ACT.Exp).then_inc(S["segexp_ready"], 1)
            sc.wait_ge(S["tm_evac"], len(TM))
            gz = vgz[:, :, 512:1536]
            A_(gz, gz, ACT.Silu).then_inc(S["silu_ready"], 1)
            sc.wait_ge(S["gst"], 1)
            A_(stat[:, 0:8], stat[:, 0:8], ACT.Sqrt).then_inc(S["gsq"], 1)
            sc.wait_ge(S["sst"], 1)
            A_(stat[:, 8:12], stat[:, 8:12], ACT.Sqrt).then_inc(S["ssq"], 1)
            for t in range(NT):
                sc.wait_ge(S["xnew_ready"], 2 * (t + 1))
                A_(fB[:, 1024:2048], x_tm[:, t, :], ACT.Square, accum_out=stat[:, 20 + t:21 + t]).then_inc(S["nsq"], 1)
                sc.wait_ge(S["nst"], t + 1)
                A_(stat[:, 22 + t:23 + t], stat[:, 22 + t:23 + t], ACT.Sqrt).then_inc(S["nsq"], 1)

            sc.wait_ge(S["ex_ready"], 1)
            A_(rt[3], rt[3], ACT.Exp).then_inc(S["ex_done"], 1)

            def xg_copy(j):
                sc.wait_ge(S["gather_done"], j + 1)
                A_(xg.rearrange("p k s -> p (k s)"), bank[3], ACT.Copy).then_inc(S["xg_ready"], 1)

            def job(j):
                xg_copy(j + 1)
                sc.wait_ge(S["gm_ready"], j + 1)
                A_(sig, gm, ACT.Sigmoid, scale=ALPHA).then_inc(S["sig_ready"], 1)
                sc.wait_ge(S["actT_done"], j + 2)
                A_(actT, bank[0].rearrange("p (q c) -> p q c", q=4), ACT.Copy).then_inc(S["actT_ready"], 1)
                sc.wait_ge(S["moe_used"], NSLOT * (j + 1))
                A_(ysb, bank[2], ACT.Copy).then_inc(S["y_ready"], 1)

            xg_copy(0)
            with sc.Fori(0, NE) as j:
                job(j)
            sc.wait_ge(S["ovtab"], 1)
            n = sc.value_load(ovi[0:1, NOV:NOV + 1], min_val=0, max_val=NOV)
            with sc.Fori(NE, NJ) as j:
                with sc.If(n > j - NE):
                    job(j)
            for t in range(NT):
                sc.wait_ge(S["fsq"], 2 * t + 1)
                A_(h2[:, t, :], x_tm[:, t, :], ACT.Square, accum_out=stat[:, 24 + t:25 + t]).then_inc(S["fst"], 1)
                sc.wait_ge(S["fsq"], 2 * t + 2)
                A_(stat[:, 26 + t:27 + t], stat[:, 26 + t:27 + t], ACT.Sqrt).then_inc(S["fst"], 1)

        @block.tensor
        def _(pe):
            mm = nc.tensor.matmul

            def misc_begin(i):
                if i >= 2:
                    pe.wait_ge(S["misc_read"], i - 1)
                return MISC[i % 2]

            def mod_unit(u, dst, k, used):
                await_unit(pe, u)
                w = front_slot(u)
                for g in range(4):
                    last = mm(dst[32 * g:32 * g + 32, :], cs[:, k, :], w[:, 512 * g:512 * (g + 1)],
                              start=(k == 0), stop=(k == KC - 1))
                last.then_inc(used, 1)

            pe.wait_ge(S["cs_ready"], 1)
            for k in range(KC):
                mod_unit(k, bank[0], k, S["mod1_used"])
            pe.wait_ge(S["consts"], 1)
            for k in range(KC):
                pe.wait_ge(S["sq_ready"], k + 1)
                mm(bank[1], ones, sq[k % 2], start=(k == 0), stop=(k == KC - 1)).then_inc(S["sq_summed"], 1)
            b = misc_begin(M_MODT)
            pe.wait_ge(S["row1_ready"], 1)
            for q in range(4):
                last = nc.tensor.transpose(b[:, q * P:(q + 1) * P], modrow1[:, q * P:(q + 1) * P], ident)
            last.then_inc(S["misc_filled"], 1)

            def fm_chunk(i):
                kind, m, with_ctx = FM[i]
                n = T + TX if with_ctx else T
                b = in_item_bank(i)
                u = U_IN + (i - 1) // 2
                if kind != "gk":
                    await_unit(pe, u)
                    w = front_slot(u).rearrange("p (k c) -> p k c", k=KC)[:, :, P * ((i - 1) % 2):P * ((i - 1) % 2) + P]
                else:
                    w = wgk
                    pe.wait_ge(S["small_in"], 16 * N_SMALL)
                if i >= 2:
                    pe.wait_ge(S["fm_evac"], i - 1)
                for k in range(KC):
                    if i == 0:
                        pe.wait_ge(S["h_ready"], 2 * (k + 1))
                    last = mm(b[0:w.shape[2], 0:n], w[:, k, :], hT[:, k, 0:n], start=(k == 0), stop=(k == KC - 1))
                last.then_inc(S["fm_done"], 1)

            def fm_unit(a):
                fm_chunk(a)
                fm_chunk(a + 1)

            fm_chunk(0)
            fm_unit(1)
            pe.wait_ge(S["fm_evac"], 1)
            for n in range(4):
                c, d = divmod(n, 2)
                if n >= 2:
                    pe.wait_ge(S["gate_read"], n - 1)
                mm(bank[5 + n % 2], wup[:, d, c * P:(c + 1) * P], gk_fm, start=True, stop=True
                   ).then_inc(S["gate_done"], 1)
            for a in range(3, len(FM), 2):
                fm_unit(a)

            def tm_item(i):
                kind, half, c = TM[i]
                n = len(FM) + i
                b = in_item_bank(n)
                if i == 0:
                    pe.wait_ge(S["fm_evac"], n - 1)
                elif i == 1:
                    pe.wait_ge(S["fm_evac"], n - 1)
                else:
                    pe.wait_ge(S["tm_evac"], i - 1)
                if kind == "dt":
                    for t in range(4):
                        for k in range(KC):
                            last = mm(b[:, SH * t:SH * (t + 1)], hT[:, k, t * P:(t + 1) * P], wdt[:, k, :],
                                      start=(k == 0), stop=(k == KC - 1))
                    last.then_inc(S["tm_done"], 1)
                    return
                u = U_IN + 6 + {"v": 0, "g": 2, "z": 4}[kind] + half
                await_unit(pe, u)
                w = front_slot(u).rearrange("p (k c) -> p k c", k=KC)
                for t in range(2):
                    for k in range(KC):
                        last = mm(b[:, 256 * t:256 * (t + 1)], hT[:, k, (2 * c + t) * P:(2 * c + t + 1) * P], w[:, k, :],
                                  start=(k == 0), stop=(k == KC - 1))
                last.then_inc(S["tm_done"], 1)

            tm_item(0)
            pe.wait_ge(S["conv_act"], 8)
            for g in range(SG):
                b = misc_begin(M_CB + g)
                for jt in range(2):
                    last = mm(b[:, 256 * jt:256 * (jt + 1)], conv[:, 4 + g, jt * P:(jt + 1) * P], conv[:, 6 + g, 0:T],
                              start=True, stop=True)
                last.then_inc(S["misc_filled"], 1)
            b = misc_begin(M_B)
            for t in range(2):
                for g in range(SG):
                    last = nc.tensor.transpose(b[:, (2 * t + g) * P:(2 * t + g + 1) * P],
                                               conv[:, 4 + g, (2 + t) * P:(3 + t) * P], ident)
            last.then_inc(S["misc_filled"], 1)

            def gla_scores(n):
                c, d = divmod(n, 2)
                kb, qb = kv[n % 2], qv[n % 2]
                pe.wait_ge(S["kvmul_ready"], n + 1)
                for e in range(2):
                    rows = slice(64 * e, 64 * e + 64)
                    b = bank[e]
                    if n >= 1:
                        pe.wait_ge(S["pt_ready"], 2 * (n - 1) + e + 1)
                    elif e == 0:
                        pe.wait_ge(S["row1_ready"], 1)
                    else:
                        pe.wait_ge(S["rinv_ready"], 1)
                    for blk in range(NB):
                        near = blk < 4 if d == 0 else blk >= 4
                        i4 = blk % 4
                        q = qb[rows, blk * BLK:(blk + 1) * BLK]
                        if near:
                            col = blk * BLK if d == 0 else 2 * P + i4 * BLK
                            if d == 0 and blk < 4:
                                col = blk * BLK
                            last = mm(b[:, col:col + BLK], kb[rows, i4 * P:(i4 + 1) * P], q, start=True, stop=True)
                        else:
                            for jt in range(2):
                                col = (1 + jt if d == 0 else jt) * P + i4 * BLK
                                last = mm(b[:, col:col + BLK],
                                          kb[rows, 512 + 256 * i4 + P * jt:512 + 256 * i4 + P * (jt + 1)], q,
                                          start=True, stop=True)
                    last.then_inc(S["score_done"], 1)
                b = misc_begin(M_GLA + 2 * n)
                for t in range(2):
                    last = nc.tensor.transpose(b[:, t * P:(t + 1) * P], kx[n % 2][:, t * P:(t + 1) * P], ident)
                last.then_inc(S["misc_filled"], 1)
                b = misc_begin(M_GLA + 2 * n + 1)
                pe.wait_ge(S["misc_read"], M_GLA + 2 * n + 1)
                pe.wait_ge(S["tm_evac"], 5)
                for e in range(2):
                    h = 2 * c + e
                    for t in range(2):
                        last = mm(b[64 * e:64 * e + 64, 0:DV], kxT[:, t * P + 64 * e:t * P + 64 * e + 64],
                                  vx[:, t, h * DV:(h + 1) * DV], start=(t == 0), stop=(t == 1))
                last.then_inc(S["misc_filled"], 1)

            def gla_out(c):
                pe.wait_ge(S["pt_ready"], 4 * (c + 1))
                pe.wait_ge(S["misc_read"], M_GLA + 4 * (c + 1))
                if c == 0:
                    pe.wait_ge(S["gate_read"], 4)
                for e in range(2):
                    h = 2 * c + e
                    rows = slice(64 * e, 64 * e + 64)
                    for t in range(2):
                        dst = bank[5 + e][:, (2 * t + c) * DV:(2 * t + c + 1) * DV]
                        terms = [(0, 0, 0), (1, 0, 0), (1, 1, 1)] if t == 0 else [(0, 0, 1), (0, 1, 2), (1, 1, 2)]
                        for x, (d, jt, s) in enumerate(terms):
                            mm(dst, pt[:, d, e, s * P:(s + 1) * P], vgz[:, jt, h * DV:(h + 1) * DV],
                               start=(x == 0), stop=False)
                        for d in range(2):
                            last = mm(dst, qd[rows, d, t * P:(t + 1) * P], gS[rows, d, :], start=False, stop=(d == 1))
                last.then_inc(S["o_done"], 1)

            for i in range(1, 5):
                tm_item(i)
            gla_scores(0)
            tm_item(5)
            gla_scores(1)
            tm_item(6)
            gla_out(0)
            gla_scores(2)
            tm_item(7)
            gla_scores(3)
            tm_item(8)
            gla_out(1)
            for t in range(4):
                b = misc_begin(M_X + t)
                for m in range(4):
                    last = nc.tensor.transpose(b[:, m * P:(m + 1) * P], conv[:, m, t * P:(t + 1) * P], ident)
                last.then_inc(S["misc_filled"], 1)

            b = misc_begin(M_ACOL)
            pe.wait_ge(S["dt_exp"], 1)
            for d in range(2):
                near, far = (upper, 0) if d == 0 else (lower, 1)
                for t in range(2):
                    dst = b[:, (t * 2 + d) * SH:(t * 2 + d + 1) * SH]
                    both = t != far
                    mm(dst, near, a_tm[:, t, d, :], start=True, stop=not both)
                    if both:
                        mm(dst, ones, a_tm[:, 1 - t, d, :], start=False, stop=True)
                near, far = (s_lower, 1) if d == 0 else (s_upper, 0)
                for t in range(2):
                    dst = b[:, ((2 + t) * 2 + d) * SH:((2 + t) * 2 + d + 1) * SH]
                    both = t != far
                    last = mm(dst, near, a_tm[:, 2 + t, d, :], start=True, stop=not both)
                    if both:
                        last = mm(dst, ones, a_tm[:, 3 - t, d, :], start=False, stop=True)
            last.then_inc(S["misc_filled"], 1)
            for d in range(2):
                b = misc_begin(M_ST + d)
                pe.wait_ge(S["xw_ready"], d + 1)
                for g in range(SG):
                    for t in range(2):
                        last = mm(b[:, 256 * g:256 * (g + 1)], b_tm[:, t, g, :], xw[:, t, d, 256 * g:256 * (g + 1)],
                                  start=(t == 0), stop=(t == 1))
                last.then_inc(S["misc_filled"], 1)
            for t in range(2):
                for d in range(2):
                    b = misc_begin(M_YOFF + 2 * t + d)
                    pe.wait_ge(S["misc_read"], M_ST + d + 1)
                    for g in range(SG):
                        last = mm(b[:, 256 * g:256 * (g + 1)], conv[:, 6 + g, t * P:(t + 1) * P],
                                  sS[:, d, 256 * g:256 * (g + 1)], start=True, stop=True)
                    last.then_inc(S["misc_filled"], 1)

            def row_sums(i):
                h, d = divmod(i, 2)
                b = bank[3 + i % 2]
                if i >= 2:
                    pe.wait_ge(S["arg_ready"], i - 1)
                elif i == 0:
                    pe.wait_ge(S["tm_evac"], len(TM))
                tri = (upper, lower)[d]
                a = [bc(a_tm[:, t, d, h:h + 1], [P, P]) for t in range(2)]
                for t in range(2):
                    dst = b[:, t * P:(t + 1) * P]
                    both = t == 1 - d
                    last = mm(dst, a[t], tri, start=True, stop=not both)
                    if both:
                        last = mm(dst, a[1 - t], ones, start=False, stop=True)
                last.then_inc(S["rb_done"], 1)

            def ssd_out(h):
                pe.wait_ge(S["segm_ready"], 2 * h + 2)
                if h == 0:
                    pe.wait_ge(S["o_copied"], 4)
                for t in range(2):
                    dst = bank[5 + t][:, h * HP:(h + 1) * HP]
                    terms = [(0, 0, 0), (1, 0, 0), (1, 1, 1)] if t == 0 else [(0, 0, 1), (0, 1, 2), (1, 1, 2)]
                    for x, (d, jt, s) in enumerate(terms):
                        last = mm(dst, seg[(2 * h + d) % 4][:, s * P:(s + 1) * P], xdt[:, jt, d, h * HP:(h + 1) * HP],
                                  start=(x == 0), stop=(x == 2))
                last.then_inc(S["ydiag_done"], 1)

            pe.wait_ge(S["pt_ready"], 8)
            row_sums(0)
            row_sums(1)
            for h in range(SH):
                for d in range(2):
                    m = 2 * h + d
                    mod_unit(U_MOD2 + m, bank[m // KC], m % KC, S["mod2_used"])
                if h < SH - 1:
                    row_sums(2 * h + 2)
                    row_sums(2 * h + 3)
                ssd_out(h)

            for i in range(8):
                b = misc_begin(M_ROWS + i)
                pe.wait_ge(S["row2_ready"], i // 4 + 1)
                g = 32 * (i % 4)
                mm(b, ones[g:g + 1, :], modrow[g:g + 1, i // 4, :], start=True, stop=True
                   ).then_inc(S["misc_filled"], 1)
            for r in range(4):
                t, half = divmod(r, 2)
                b = misc_begin(M_MIXT + r)
                pe.wait_ge(S["mix_ready"], half + 1)
                for q in range(4):
                    col = 512 + (4 * half + q) * P
                    last = nc.tensor.transpose(b[:, q * P:(q + 1) * P], vgz[:, t, col:col + P], ident)
                last.then_inc(S["misc_filled"], 1)
            for r in range(4):
                t, half = divmod(r, 2)
                b = bank[3 + r % 2]
                if r == 0:
                    pe.wait_ge(S["misc_read"], M_MIXT + 4)
                    pe.wait_ge(S["arg_ready"], 2 * SH)
                if r >= 2:
                    pe.wait_ge(S["op_read"], r - 1)
                for k in range(KC):
                    u = U_OUT + k // 2
                    await_unit(pe, u)
                    w = front_slot(u)[:, (k % 2) * 1024 + half * 512:(k % 2) * 1024 + half * 512 + 512]
                    last = mm(b, mixT[:, k, t * P:(t + 1) * P], w, start=(k == 0), stop=(k == KC - 1))
                last.then_inc(S["op_done"], 1)
            for r in range(4):
                t, half = divmod(r, 2)
                b = misc_begin(M_H2T + r)
                pe.wait_ge(S["h2_ready"], t + 1)
                for q in range(4):
                    k = 4 * half + q
                    last = nc.tensor.transpose(b[:, q * P:(q + 1) * P], h2[:, t, k * P:(k + 1) * P], ident)
                last.then_inc(S["misc_filled"], 1)
            b = misc_begin(M_LOG)
            pe.wait_ge(S["misc_read"], M_H2T + 4)
            for t in range(2):
                for k in range(KC):
                    last = mm(b[:, t * NE:(t + 1) * NE], h2T[:, k, t * P:(t + 1) * P], wr[:, k, :],
                              start=(k == 0), stop=(k == KC - 1))
            last.then_inc(S["misc_filled"], 1)
            b = misc_begin(M_RANK)
            pe.wait_ge(S["sel_made"], 1)
            sel = rt[0]
            mm(b[:, 0:NE], s_upper, sel[:, 0, :], start=True, stop=True)
            mm(b[:, NE:2 * NE], s_upper, sel[:, 1, :], start=True, stop=False)
            mm(b[:, NE:2 * NE], ones, sel[:, 0, :], start=False, stop=True)
            mm(b[:, 2 * NE:3 * NE], ones, sel[:, 0, :], start=True, stop=False)
            mm(b[:, 2 * NE:3 * NE], ones, sel[:, 1, :], start=False, stop=True).then_inc(S["misc_filled"], 1)

            def acc(t, half):
                return bank[4 + 2 * t + half]

            def gather(j):
                pe.wait_ge(S["s_ready"], j + 1)
                for k in range(KC):
                    for t in range(2):
                        last = mm(bank[3][:, k * SLOTS:(k + 1) * SLOTS], h2[:, t, k * P:(k + 1) * P], S_j[:, t, :],
                                  start=(t == 0), stop=(t == 1))
                last.then_inc(S["gather_done"], 1)

            pe.wait_ge(S["misc_read"], M_RANK + 1)
            for (t, half), primed in zip(((0, 0), (0, 1), (1, 0), (1, 1)), ("scat_done", "sgt_done", "actT_done", None)):
                ins = mm(acc(t, half), zeros, h2[:, 0, 0:512], start=True, stop=False, skip_group_check=True)
                if primed:
                    ins.then_inc(S[primed], 1)
            gather(0)
            pe.wait_ge(S["late_in"], 80)

            def scatter(jobs):
                pe.wait_ge(S["y_ready"], jobs + 1)
                pe.wait_ge(S["sgt_ready"], jobs + 1)
                for t in range(2):
                    for half in range(2):
                        rows = slice(64 * half, 64 * half + 64)
                        last = mm(acc(t, half), SGT[rows, t, :], ysb[rows, :], start=False, stop=False,
                                  skip_group_check=True)
                last.then_inc(S["scat_done"], 1)

            def job(j):
                pe.wait_ge(S["xg_ready"], j + 1)
                pe.wait_ge(S["sg_ready"], j + 1)
                for t in range(2):
                    last = nc.tensor.transpose(bank[3][:, t * P:(t + 1) * P], SG_j[:, t, :], ident)
                last.then_inc(S["sgt_done"], 1)
                for k in range(KC):
                    pe.wait_ge(loaded[k], 16 * (j + 1 + N_FRONT // FSLOT))
                    w = slot(k)
                    for b, col in ((bank[0], 0), (bank[1], FF)):
                        for half in range(2):
                            last = mm(b[64 * half:64 * half + 64, :], xg[:, k, :],
                                      w[:, col + 512 * half:col + 512 * half + 512], start=(k == 0), stop=False)
                    last.then_inc(S["moe_used"], 1)
                    if k == 1:
                        scatter(j)
                pe.wait_ge(S["sel_ready"], j + 1)
                for b, col in ((bank[0], 0), (bank[1], FF)):
                    for half in range(2):
                        last = mm(b[64 * half:64 * half + 64, :], job_sel, brows[:, col + 512 * half:col + 512 * half + 512],
                                  start=False, stop=True)
                last.then_inc(S["gu_done"], 1)
                gather_next(j)
                pe.wait_ge(S["act_ready"], j + 1)
                for q in range(4):
                    last = nc.tensor.transpose(bank[0][:, q * P:(q + 1) * P], act[:, q * P:(q + 1) * P], ident)
                last.then_inc(S["actT_done"], 1)
                for half in range(2):
                    last = mm(bank[2][64 * half:64 * half + 64, :], job_sel,
                              brows[:, 2 * FF + 512 * half:2 * FF + 512 * half + 512], start=True, stop=False)
                last.then_inc(S["sel_used"], 1)
                pe.wait_ge(S["actT_ready"], j + 1)
                for c in range(KC):
                    s = KC + c // 2
                    if c % 2 == 0:
                        front = N_FRONT // FSLOT if s < FSLOT else 0
                        pe.wait_ge(loaded[s], 16 * (j + 1 + front))
                    hh, q = divmod(c, 4)
                    for half in range(2):
                        last = mm(bank[2][64 * half:64 * half + 64, :], actT[:, q, 64 * hh:64 * hh + 64],
                                  slot(s)[:, (c % 2) * 1024 + 512 * half:(c % 2) * 1024 + 512 * half + 512],
                                  start=False, stop=(c == KC - 1))
                    if c % 2 == 1:
                        last.then_inc(S["moe_used"], 1)

            def gather_next(j):
                pe.wait_ge(S["sgt_ready"], j + 2)
                pe.wait_ge(S["s_ready"], j + 2)
                for k in range(KC):
                    for t in range(2):
                        last = mm(bank[3][:, k * SLOTS:(k + 1) * SLOTS], h2[:, t, k * P:(k + 1) * P], S_j[:, t, :],
                                  start=(t == 0), stop=(t == 1))
                last.then_inc(S["gather_done"], 1)

            with pe.Fori(0, NE) as j:
                job(j)
            pe.wait_ge(S["ovtab"], 1)
            n = pe.value_load(ovi[0:1, NOV:NOV + 1], min_val=0, max_val=NOV)
            with pe.Fori(NE, NJ) as j:
                with pe.If(n > j - NE):
                    job(j)
            scatter(n + NE)
            for t in range(2):
                for half in range(2):
                    last = mm(acc(t, half), zeros, h2[:, 0, 0:512], start=False, stop=True, skip_group_check=True)
            last.then_inc(S["moe_done"], 1)

        @block.vector
        def _(v):
            V = nc.vector
            step = Steps(v, S["dve"])
            TT, TS, STT = V.tensor_tensor, V.tensor_scalar, V.scalar_tensor_tensor

            def misc_wait(i):
                v.wait_ge(S["misc_filled"], i + 1)
                return MISC[i % 2]

            def misc_read(ins):
                ins.then_inc(S["misc_read"], 1)

            v.wait_ge(S["mod1_used"], KC)
            V.tensor_copy(modrow1, bank[0]).then_inc(S["row1_ready"], 1)
            v.wait_ge(S["sq_summed"], KC)
            step(TS(rstd1, bank[1], 1.0 / D, EPS, ALU.mult, ALU.add))
            step.settle()
            V.reciprocal(rstd1, rstd1).then_inc(S["rinv_ready"], 1)
            b = misc_wait(M_MODT).rearrange("p (q g c) -> p g q c", q=4, g=4)
            v.wait_ge(S["small_in"], 16 * N_SMALL)
            bm = bmodT.rearrange("p (g q) -> p g q", g=4)
            mc = modc.rearrange("p (g q) c -> p g q c", g=4)
            step(TT(mc[:, :, :, 0], b[:, :, :, 0], bm, ALU.add))
            misc_read(TT(mc[:, :, :, 1], b[:, :, :, 1], bm, ALU.add))
            v.wait_ge(S["misc_read"], 1)
            step.settle()
            step(TS(modc[:, 8:16, :], modc[:, 8:16, :], 1.0, None, ALU.add))
            step.settle()
            step(TT(modc[:, 8:16, :], modc[:, 8:16, :], bc(n1T.rearrange("p (k c) -> p k c", c=1), [P, KC, 2]), ALU.mult))
            step.settle()
            v.wait_ge(S["rstd_ready"], 1)
            for k in range(KC):
                for s in range(2):
                    x = hT[:, k, s * T:(s + 1) * T]
                    STT(out=x, in0=x, scalar=modc[:, 8 + k, s:s + 1], in1=rstd1[:, s * T:(s + 1) * T],
                        op0=ALU.mult, op1=ALU.mult).then_inc(S["xh_ready"], 1)
            v.wait_ge(S["xh_ready"], 2 * KC)
            step(V.memset(pre[:, :, :, 0:1], 0.0))

            def conv_chunk(m):
                v.wait_ge(S["fm_evac"], m + 2)
                x, y = xbc[:, m, :], conv[:, m, :]
                n = T + TX if m < 6 else T
                step(TS(y[:, 0:n], x[:, 0:n], convw[:, m, 4:5], convb[:, m:m + 1], ALU.mult, ALU.add))
                x3 = x[:, 0:T].rearrange("p (r c) -> p r c", r=ROWS)
                y3 = y[:, 0:T].rearrange("p (r c) -> p r c", r=ROWS)
                for tap in (0, 1, 2, 3, 5, 6, 7, 8):
                    dy, dx = tap // 3 - 1, tap % 3 - 1
                    r0, r1 = max(0, -dy), ROWS - max(0, dy)
                    c0, c1 = max(0, -dx), GRID - max(0, dx)
                    yo = y3[:, r0:r1, c0:c1]
                    xi = x3[:, r0 + dy:r1 + dy, c0 + dx:c1 + dx]
                    step.settle()
                    ins = STT(out=yo, in0=xi, scalar=convw[:, m, tap:tap + 1], in1=yo, op0=ALU.mult, op1=ALU.add)
                    if tap == 8:
                        ins.then_inc(S["conv_ready"], 1)
                    else:
                        step(ins)
                    if dy == 0 and m < 6:
                        yo = y[:, T + c0:T + TX - max(0, dx)]
                        xi = x[:, T + c0 + dx:T + TX - max(0, dx) + dx]
                        step(STT(out=yo, in0=xi, scalar=convw[:, m, tap:tap + 1], in1=yo, op0=ALU.mult, op1=ALU.add))

            conv_chunk(0)
            for n in range(4):
                v.wait_ge(S["gate_done"], n + 1)
                step(TS(ld[:, n, :], bank[5 + n % 2], bgk[:, n:n + 1], 0.0, ALU.add, ALU.min))
                TS(soft[:, n, :], bank[5 + n % 2], bgk[:, n:n + 1], 0.0, ALU.add, ALU.max).then_inc(S["gate_read"], 1)
            v.wait_ge(S["gate_read"], 4)
            step.settle()
            TT(soft, ld, soft, ALU.subtract).then_inc(S["soft_arg"], 1)
            conv_chunk(1)
            v.wait_ge(S["soft_ready"], 1)
            step.settle()
            step(TT(ld, ld, soft, ALU.subtract))
            step.settle()
            for n in range(4):
                for s in range(2):
                    step(V.tensor_tensor_scan(pre[:, n, s, 1:T + 1], bc(ones[:, 0:1], [P, T]),
                                              ld[:, n, s * T:(s + 1) * T], 0.0, ALU.mult, ALU.add))
            step.settle()
            for n in range(4):
                s = 1 if n % 2 == 0 else 0
                step(TS(stat[:, 16 + n:17 + n], pre[:, n, s, T:T + 1], 1.0 / GATE_NORM, None, ALU.mult))
            for m in range(2, 8):
                conv_chunk(m)

            v.wait_ge(S["tm_evac"], 1)
            for d in range(2):
                step(TT(dta[:, :, d, :], dtr, bc(dtb3[:, d:d + 1, :], [P, 4, SH]), ALU.add))
            step.settle()
            step(TS(dtt, dta, 0.0, None, ALU.min))
            step.settle()
            step(TS(dta, dta, 0.0, None, ALU.max))
            step.settle()
            TT(dtt, dtt, dta, ALU.subtract).then_inc(S["dt_ready"], 1)

            def args(n):
                d, b = n % 2, n % 2
                off = 1 if d == 0 else 0
                src = pre[:, n, 0, off:off + T]
                lim = CLAMP * GATE_NORM
                clip = (-lim, ALU.max) if d == 0 else (lim, ALU.min)
                if n >= 2:
                    v.wait_ge(S["score_done"], 2 * (n - 1))
                for blk in range(NB):
                    near = blk < 4 if d == 0 else blk >= 4
                    i4 = blk % 4
                    ref = pre[:, n, 0, blk * BLK + BLK // 2:blk * BLK + BLK // 2 + 1]
                    if near:
                        dst = kv[b][:, i4 * P:(i4 + 1) * P]
                        s = src[:, 0:P] if d == 0 else src[:, P:2 * P]
                    else:
                        dst = kv[b][:, 512 + i4 * 256:512 + (i4 + 1) * 256]
                        s = src
                    step(TS(dst, s, ref, clip[0], ALU.subtract, clip[1]))
                    last = TS(qv[b][:, blk * BLK:(blk + 1) * BLK], src[:, blk * BLK:(blk + 1) * BLK], ref,
                              -clip[0], ALU.subtract, ALU.min if d == 0 else ALU.max)
                    if blk < NB - 1:
                        step(last)
                last.then_inc(S["kvarg_ready"], 1)

            def mults(n):
                c, d = divmod(n, 2)
                b = n % 2
                v.wait_ge(S["exp_ready"], 4 * (n + 1))
                if n >= 2:
                    v.wait_ge(S["o_done"], 1)
                kn = k_fm[:, c, 0:P] if d == 0 else k_fm[:, c, P:2 * P]
                near = kv[b][:, 0:512].rearrange("p (b j) -> p b j", b=4)
                far = kv[b][:, 512:1536].rearrange("p (b j) -> p b j", b=4)
                step(TT(near, near, bc(kn.rearrange("p (a j) -> p a j", a=1), [P, 4, P]), ALU.mult))
                step(TT(far, far, bc(k_fm[:, c, 0:T].rearrange("p (a j) -> p a j", a=1), [P, 4, T]), ALU.mult))
                step(TT(qv[b], qv[b], q_fm[:, c, :], ALU.mult))
                step(TT(qd[:, d, :], qd[:, d, :], q_fm[:, c, :], ALU.mult))
                TT(kx[b], kx[b], k_fm[:, c, T:T + TX], ALU.mult).then_inc(S["kvmul_ready"], 1)

            def scores(n):
                c, d = divmod(n, 2)
                if n == 0:
                    v.wait_ge(S["kvarg_ready"], 1)
                if n >= 2:
                    v.wait_ge(S["o_done"], 1)
                for e in range(2):
                    v.wait_ge(S["score_done"], 2 * n + e + 1)
                    TT(pt[:, d, e, :], bank[e][:, 0:SPAN], mask[d], ALU.mult).then_inc(S["pt_ready"], 1)
                misc_read(V.tensor_copy(kxT, misc_wait(M_GLA + 2 * n)[:, 0:256]))
                misc_read(V.tensor_copy(gS[:, d, :], misc_wait(M_GLA + 2 * n + 1)[:, 0:DV]))

            args(0)
            args(1)
            v.wait_ge(S["negA_ready"], 1)
            v.wait_ge(S["dt_sp"], 1)
            step.settle()
            step(TT(dta, dta, dtt, ALU.add))
            step.settle()
            for d in range(2):
                step(TT(a_tm[:, :, d, :], dta[:, :, d, :], bc(negA3[:, d:d + 1, :], [P, 4, SH]), ALU.mult))
            step.settle()
            TS(a_tm, a_tm, -1.0, None, ALU.mult).then_inc(S["dt_exp"], 1)
            for g in range(SG):
                b = misc_wait(M_CB + g)
                step(TT(cbm[:, 0, g, 0:256], b[:, 0:256], mask[0][:, 0:256], ALU.mult))
                step(TT(cbm[:, 0, g, 256:384], b[:, 384:512], mask[0][:, 256:384], ALU.mult))
                step(TT(cbm[:, 1, g, 0:128], b[:, 0:128], mask[1][:, 0:128], ALU.mult))
                misc_read(TT(cbm[:, 1, g, 128:384], b[:, 256:512], mask[1][:, 128:384], ALU.mult))
            misc_read(V.tensor_copy(b_tm.rearrange("p t g s -> p (t g s)"), misc_wait(M_B)))
            mults(0)
            scores(0)
            args(2)
            mults(1)
            scores(1)
            args(3)
            mults(2)
            scores(2)
            mults(3)
            scores(3)

            v.wait_ge(S["tm_done"], len(TM))
            for t in range(4):
                misc_read(V.tensor_copy(xs_tm[:, t, :], misc_wait(M_X + t)))
            misc_read(V.tensor_copy(acol.rearrange("p t d h -> p (t d h)"), misc_wait(M_ACOL)[:, 0:64]))
            v.wait_ge(S["misc_read"], M_ACOL + 1)
            v.wait_ge(S["eac_ready"], 1)
            step(TT(dta[:, 2:4], dta[:, 2:4], eac[:, 2:4], ALU.mult))
            step.settle()
            hp = lambda ap: ap.rearrange("p (h q) -> p h q", h=SH)
            for d in range(2):
                for t in range(2):
                    last = TT(hp(xw[:, t, d, :]), hp(xs_tm[:, 2 + t, :]),
                              bc(dta[:, 2 + t, d, :].rearrange("p (h q) -> p h q", q=1), [P, SH, HP]), ALU.mult)
                    if t == 0:
                        step(last)
                last.then_inc(S["xw_ready"], 1)
            for d in range(2):
                for t in range(2):
                    step(TT(hp(xdt[:, t, d, :]), hp(xs_tm[:, t, :]),
                            bc(dta[:, t, d, :].rearrange("p (h q) -> p h q", q=1), [P, SH, HP]), ALU.mult))
            ya = y_acc.rearrange("p (t c) -> p t c", t=2)
            for t in range(2):
                step(TT(hp(ya[:, t, :]), hp(xs_tm[:, t, :]),
                        bc(d_row.rearrange("p (h q) -> p h q", q=1), [P, SH, HP]), ALU.mult))
            for d in range(2):
                misc_read(V.tensor_copy(sS[:, d, :], misc_wait(M_ST + d)))
            v.wait_ge(S["xw_ready"], 2)
            ytmp = hA[:, 0:512]
            for t in range(2):
                for d in range(2):
                    b = misc_wait(M_YOFF + 2 * t + d)
                    v.wait_ge(S["misc_read"], M_YOFF + 2 * t + d)
                    step.settle()
                    misc_read(TT(hp(ytmp), hp(b), bc(eac[:, t, d, :].rearrange("p (h q) -> p h q", q=1), [P, SH, HP]),
                                 ALU.mult))
                    v.wait_ge(S["misc_read"], M_YOFF + 2 * t + d + 1)
                    step(TT(ya[:, t, :], ya[:, t, :], ytmp, ALU.add))
            step.settle()

            def seg_arg(i):
                h, d = divmod(i, 2)
                s = seg[i % 4]
                b = bank[3 + i % 2]
                v.wait_ge(S["rb_done"], i + 1)
                if i >= 4:
                    v.wait_ge(S["ydiag_done"], (i - 4) // 2 + 1)
                spans = [(0, 0, 256, 0), (256, 128, 256, 1)] if d == 0 else [(0, 0, 128, 0), (128, 0, 256, 1)]
                for x, (to, c0, c1, jt) in enumerate(spans):
                    ins = TS(s[:, to:to + c1 - c0], b[:, c0:c1], acol[:, jt, d, h:h + 1], 0.0, ALU.subtract, ALU.min)
                    if x == 0:
                        step(ins)
                        step.settle()
                    else:
                        ins.then_inc(S["arg_ready"], 1)

            def seg_mult(i):
                h, d = divmod(i, 2)
                v.wait_ge(S["segexp_ready"], i + 1)
                TT(seg[i % 4], seg[i % 4], cbm[:, d, h // HPG, :], ALU.mult).then_inc(S["segm_ready"], 1)

            v.wait_ge(S["o_done"], 2)
            seg_arg(0)
            for i in range(2 * SH):
                if i + 1 < 2 * SH:
                    seg_arg(i + 1)
                seg_mult(i)
                if i == 9:
                    v.wait_ge(S["mr"], 64)
                    v.wait_ge(S["mod2_used"], KC)
                    TT(modrow[:, 0, :], bank[0], modrow[:, 0, :], ALU.add).then_inc(S["row2_ready"], 1)
            v.wait_ge(S["mod2_used"], 2 * KC)
            v.wait_ge(S["mr"], 64)
            TT(modrow[:, 1, :], bank[1], modrow[:, 1, :], ALU.add).then_inc(S["row2_ready"], 1)

            for i in range(8):
                b = misc_wait(M_ROWS + i)
                dst = gB[:, 512 * i:512 * (i + 1)]
                misc_read(TS(dst, b, 1.0 if i in (4, 5) else 0.0, None, ALU.add))

            v.wait_ge(S["o_copied"], 4)
            v.wait_ge(S["silu_ready"], 1)
            o4 = o_sb.rearrange("p (t h v) -> p t h v", t=2, h=GH)
            tmp = hA[:, 0:1024]
            step(TT(tmp, o_sb, o_sb, ALU.mult))
            step.settle()
            step(V.tensor_reduce(stat[:, 0:8], tmp.rearrange("p (a v) -> p a v", a=8), AX.X, ALU.add))
            step.settle()
            step(TS(stat[:, 0:8], stat[:, 0:8], 1.0 / DV, EPS, ALU.mult, ALU.add))
            step.settle()
            V.reciprocal(stat[:, 0:8], stat[:, 0:8]).then_inc(S["gst"], 1)
            v.wait_ge(S["ydiag_done"], SH)
            for t in range(2):
                step(TT(ya[:, t, :], ya[:, t, :], bank[5 + t], ALU.add))
            step.settle()
            step(TT(ya, ya, vgz[:, :, 1024:1536], ALU.mult))
            step.settle()
            step(TT(tmp, y_acc, y_acc, ALU.mult))
            step.settle()
            step(V.tensor_reduce(stat[:, 8:12], tmp.rearrange("p (a v) -> p a v", a=4), AX.X, ALU.add))
            step.settle()
            step(TS(stat[:, 8:12], stat[:, 8:12], SG / SI, EPS, ALU.mult, ALU.add))
            step.settle()
            V.reciprocal(stat[:, 8:12], stat[:, 8:12]).then_inc(S["sst"], 1)
            v.wait_ge(S["gsq"], 1)
            o3 = o_sb.rearrange("p (a v) -> p a v", a=8)
            step(TT(o3, o3, bc(stat[:, 0:8].rearrange("p (a v) -> p a v", v=1), [P, 8, DV]), ALU.mult))
            step.settle()
            step(TT(o3, o3, bc(gnrow.rearrange("p (a v) -> p a v", a=1), [P, 8, DV]), ALU.mult))
            step.settle()
            gv = vgz[:, :, 512:1024].rearrange("p t (h v) -> p t h v", h=GH)
            TT(gv, gv, o4, ALU.mult).then_inc(S["mix_ready"], 1)
            v.wait_ge(S["ssq"], 1)
            v.wait_ge(S["sn_in"], 16)
            y3 = y_acc.rearrange("p (a v) -> p a v", a=4)
            step(TT(y3, y3, bc(stat[:, 8:12].rearrange("p (a v) -> p a v", v=1), [P, 4, SI // SG]), ALU.mult))
            step.settle()
            TT(vgz[:, :, 1024:1536], ya, bc(snrow.rearrange("p (a v) -> p a v", a=1), [P, 2, SI]), ALU.mult
               ).then_inc(S["mix_ready"], 1)
            for r in range(4):
                t, half = divmod(r, 2)
                b = misc_wait(M_MIXT + r).rearrange("p (q c) -> p q c", q=4)
                misc_read(V.tensor_copy(mixT[:, 4 * half:4 * half + 4, t * P:(t + 1) * P], b))
            v.wait_ge(S["misc_read"], M_MIXT + 4)
            v.wait_ge(S["late_in"], 80)
            v.wait_ge(S["misc_read"], M_ROWS + 8)
            step(TT(w2b, w2b, n2row, ALU.mult))
            step(V.memset(zeros, 0.0))
            step(V.memset(RT, -1.0))
            step(V.memset(GT, 0.0))
            for r in range(4):
                t, half = divmod(r, 2)
                v.wait_ge(S["op_done"], r + 1)
                cols = slice(512 * half, 512 * half + 512)
                tm_ = fB[:, 0:512]
                step.settle()
                if r:
                    v.wait_ge(S["xnew_ready"], r)
                TT(tm_, bank[3 + r % 2], g1b[:, cols], ALU.mult).then_inc(S["op_read"], 1)
                v.wait_ge(S["op_read"], r + 1)
                TT(x_tm[:, t, cols], x_tm[:, t, cols], tm_, ALU.add).then_inc(S["xnew_ready"], 1)
            for t in range(NT):
                v.wait_ge(S["nsq"], 2 * t + 1)
                st = stat[:, 22 + t:23 + t]
                step(TS(st, stat[:, 20 + t:21 + t], 1.0 / D, EPS, ALU.mult, ALU.add))
                step.settle()
                V.reciprocal(st, st).then_inc(S["nst"], 1)
                v.wait_ge(S["nsq"], 2 * t + 2)
                step(STT(out=h2[:, t, :], in0=x_tm[:, t, :], scalar=st, in1=w2b, op0=ALU.mult, op1=ALU.mult))
                step.settle()
                TT(h2[:, t, :], h2[:, t, :], sh2b, ALU.add).then_inc(S["h2_ready"], 1)
            for r in range(4):
                t, half = divmod(r, 2)
                b = misc_wait(M_H2T + r).rearrange("p (q c) -> p q c", q=4)
                misc_read(V.tensor_copy(h2T[:, 4 * half:4 * half + 4, t * P:(t + 1) * P], b))
            b = misc_wait(M_LOG)[:, 0:2 * NE].rearrange("p (t e) -> p t e", t=2)
            misc_read(TT(lg, b, bc(brrow.rearrange("p (a e) -> p a e", a=1), [P, 2, NE]), ALU.add))
            v.wait_ge(S["misc_read"], M_LOG + 1)
            for t in range(2):
                step(V.max(top8[:, t, :], lg[:, t, :]))
            step.settle()
            sel, eq, ce, ex = rt
            for t in range(2):
                m4 = top8[:, t, 3:4]
                step(TS(sel[:, t, :], lg[:, t, :], m4, None, ALU.is_gt))
                step(TS(eq[:, t, :], lg[:, t, :], m4, None, ALU.is_equal))
            step.settle()
            for t in range(2):
                last = TS(ex[:, t, :], lg[:, t, :], top8[:, t, 0:1], None, ALU.subtract)
                if t == 0:
                    step(last)
            last.then_inc(S["ex_ready"], 1)
            for t in range(2):
                step(V.tensor_tensor_scan(ce[:, t, :], bc(ones[:, 0:1], [P, NE]), eq[:, t, :], 0.0, ALU.mult, ALU.add))
            step(V.tensor_reduce(stat[:, 28:30], sel, AX.X, ALU.add))
            step.settle()
            for t in range(2):
                step(TS(ce[:, t, :], ce[:, t, :], stat[:, 28 + t:29 + t], 4.5, ALU.add, ALU.is_lt))
            step.settle()
            step(TT(eq, eq, ce, ALU.mult))
            step.settle()
            TT(sel, sel, eq, ALU.add).then_inc(S["sel_made"], 1)
            v.wait_ge(S["sel_made"], 1)
            v.wait_ge(S["ex_done"], 1)
            step(TT(ex, ex, sel, ALU.mult))
            step.settle()
            step(V.tensor_reduce(stat[:, 28:30], ex, AX.X, ALU.add))
            step.settle()
            step(V.reciprocal(stat[:, 28:30], stat[:, 28:30]))
            step.settle()
            for t in range(2):
                step(TS(GT[:, t, 0:NE], ex[:, t, :], stat[:, 28 + t:29 + t], None, ALU.mult))
            b = misc_wait(M_RANK)[:, 0:3 * NE].rearrange("p (i e) -> p i e", i=3)
            misc_read(V.tensor_copy(cnt, b))
            v.wait_ge(S["misc_read"], M_RANK + 1)
            step(STT(out=eq, in0=cnt[:, 0:2, :], scalar=1.0, in1=sel, op0=ALU.add, op1=ALU.mult))
            step.settle()
            step(TS(RT[:, :, 0:NE], eq, -1.0, None, ALU.add))
            step.settle()


            def select_tokens(j):
                for t in range(2):
                    last = TS(S_j[:, t, :], slot_no[:, 0:SLOTS], RT[:, t, bass.ds(j, 1)], None, ALU.is_equal)
                last.then_inc(S["s_ready"], 1)

            def select_expert(j):
                TS(job_sel, part_no[0:NE, :], JE[0:NE, bass.ds(j, 1)], None, ALU.is_equal).then_inc(S["sel_ready"], 1)

            def job(j):
                v.wait_ge(S["sgt_done"], j + 1)
                for t in range(2):
                    last = TS(SG_j[:, t, :], slot_no, RT[:, t, bass.ds(j, 1)], GT[:, t, bass.ds(j, 1)],
                              ALU.is_equal, ALU.mult)
                last.then_inc(S["sg_ready"], 1)
                v.wait_ge(S["gather_done"], j + 1)
                select_tokens(j + 1)
                v.wait_ge(S["sgt_done"], j + 2)
                v.wait_ge(S["scat_done"], j + 2)
                V.tensor_copy(SGT, bank[3][:, 0:256].rearrange("p (t c) -> p t c", t=2)).then_inc(S["sgt_ready"], 1)
                v.wait_ge(S["gu_done"], j + 1)
                TS(gm, bank[0], LIMIT, None, ALU.min).then_inc(S["gm_ready"], 1)
                v.wait_ge(S["actT_done"], j + 1)
                TS(act, bank[1], LIMIT, -LIMIT, ALU.min, ALU.max).then_inc(S["up_read"], 1)
                v.wait_ge(S["up_read"], 2 * j + 1)
                v.wait_ge(S["gm_ready"], j + 1)
                STT(out=act, in0=act, scalar=1.0, in1=gm, op0=ALU.add, op1=ALU.mult).then_inc(S["up_read"], 1)
                v.wait_ge(S["up_read"], 2 * j + 2)
                v.wait_ge(S["sig_ready"], j + 1)
                TT(act, act, sig, ALU.mult).then_inc(S["act_ready"], 1)
                v.wait_ge(S["sel_used"], j + 1)
                select_expert(j + 1)

            v.wait_ge(S["misc_filled"], M_RANK + 1)
            select_tokens(0)
            select_expert(0)
            V.memset(SGT, 0.0).then_inc(S["sgt_ready"], 1)
            V.memset(ysb, 0.0).then_inc(S["y_ready"], 1)
            overflow_tables(nc, v, S, step, cnt, RT, GT, JE, ovi, ov, no32, ones)
            with v.Fori(0, NE) as j:
                job(j)
            v.wait_ge(S["ovtab"], 1)
            n = v.value_load(ovi[0:1, NOV:NOV + 1], min_val=0, max_val=NOV)
            with v.Fori(NE, NJ) as j:
                with v.If(n > j - NE):
                    job(j)
            v.wait_ge(S["moe_done"], 1)
            for t in range(NT):
                for half in range(2):
                    cols = slice(512 * half, 512 * half + 512)
                    b = bank[4 + 2 * t + half]
                    step(TT(fB[:, cols], b, g2b[:, cols], ALU.mult))
                step.settle()
                TT(x_tm[:, t, :], x_tm[:, t, :], fB[:, 0:1024], ALU.add).then_inc(S["fsq"], 1)
                v.wait_ge(S["fst"], 2 * t + 1)
                st = stat[:, 26 + t:27 + t]
                step(TS(st, stat[:, 24 + t:25 + t], 1.0 / D, EPS, ALU.mult, ALU.add))
                step.settle()
                V.reciprocal(st, st).then_inc(S["fsq"], 1)
                v.wait_ge(S["fst"], 2 * t + 2)
                STT(out=x_tm[:, t, :], in0=x_tm[:, t, :], scalar=st, in1=fnrow, op0=ALU.mult, op1=ALU.mult
                    ).then_inc(S["out_ready"], 1)


def kernel(**inputs):
    import numpy as np
    import concourse.bacc as bacc
    from concourse.bass_utils import run_bass_kernel_spmd

    g = {k: np.asarray(v) for k, v in inputs.items()}
    w_in = g["w_in"][0]
    off = np.cumsum([0, 256, 256, 512, 512, RANK, 512, 1024, SH])
    q, k, v, gg, gk, z, xbc, dt = (w_in[:, off[i]:off[i + 1]] for i in range(8))
    units = np.concatenate([xbc, k, q, v, gg, z], axis=1)
    arr = {
        "x": g["x"][0],
        "xT": g["x"][0].T.reshape(KC, P, T),
        "ctxT": g["ctx"][0].T.reshape(KC, P, TX),
        "c2": np.stack([g["c"][0], g["c_ctx"]], axis=1).reshape(KC, P, 2),
        "w_mod": g["w_mod"][0],
        "bmodT": g["b_mod"][0][:2048].reshape(16, P).T,
        "b_mod2": g["b_mod"][0][2048:].reshape(2, 4, 512),
        "n1T": g["norm1"][0].reshape(KC, P).T,
        "w_in": units.reshape(KC, P, N_IN, 256).transpose(2, 1, 0, 3).reshape(N_IN, P, UNIT),
        "wgk": gk.reshape(KC, P, RANK),
        "wdt": dt.reshape(KC, P, SH),
        "wup": g["gla_w_gk_up"][0].transpose(1, 0, 2),
        "bgk": g["gla_b_gk"][0].reshape(2, 2, P).transpose(2, 1, 0).reshape(P, 4),
        "convw": g["ssd_conv_w"][0].reshape(9, 8, P).transpose(2, 1, 0),
        "convb": g["ssd_conv_b"][0].reshape(8, P).T,
        "gla_norm": g["gla_norm"][0],
        "ssd_norm": g["ssd_norm"][0],
        "ssd_D": g["ssd_D"][0],
        "dtb": g["ssd_dt_bias"][0].reshape(16),
        "alog": g["ssd_A_log"][0].reshape(16),
        "w_out": g["w_out"][0],
        "norm2": g["norm2"][0],
        "final_norm": g["final_norm"],
        "w_router": g["w_router"][0],
        "b_router": g["b_router"][0],
        "w_gate_up": g["w_gate_up"][0],
        "w_down": g["w_down"][0],
        "b_moe": np.concatenate([g["b_gate_up"][0], g["b_down"][0]], axis=1),
    }
    nc = bacc.Bacc("TRN2", target_bir_lowering=False, num_devices=1)
    arrays, A = {}, {}
    for name, a in arr.items():
        a = np.ascontiguousarray(a)
        arrays[f"in_{name}"] = a
        A[name] = nc.dram_tensor(f"in_{name}", a.shape, mybir.dt.from_np(a.dtype), kind="ExternalInput").ap()
    out = nc.dram_tensor("out_0", (1, T, D), F32, kind="ExternalOutput").ap()
    layer_kernel(nc, A, out)
    return run_bass_kernel_spmd(nc, [arrays], core_ids=[0]).results[0]["out_0"]
```

```python
from contextlib import ExitStack

import concourse.bass as bass
from concourse import mybir

F32 = mybir.dt.float32
I32 = mybir.dt.int32
ALU = mybir.AluOpType
ACT = mybir.ActivationFunctionType
AX = mybir.AxisListType

P = 128
D = 1024
KC = D // P
T = 256
TX = 256
NT = T // P
EPS = 1e-6
GH, DK, DV = 4, 64, 128
RANK = 16
GATE_NORM = 16.0
BLK = 64
NB = T // BLK
NPT = P // BLK
KNEAR, KV = NPT * P, NPT * (P + T)
CLAMP = 40.0
SH, HP, SG, NS = 8, 64, 2, 128
HPG = SH // SG
SI = SH * HP
GRID = 64
ROWS = T // GRID
NE = 32
FF = 1024
SLOTS = 64
NJ = NE + 15
FEW = 4
LIMIT, ALPHA = 7.0, 1.702
UNIT = 2048
N_SMALL = 11
NSLOT = 12
FSLOT = 10
N_MOD1, N_IN, N_MOD2, N_OUT = 8, 12, 16, 4
N_FRONT = N_MOD1 + N_IN + N_MOD2 + N_OUT
SPAN = 384


def bc(ap, shape):
    return ap.to_broadcast(shape)


def job_tables(nc, v, S, step, total, nblk, incl, job_no, w, JE, JQ, ints, ones):
    V = nc.vector
    TT, TS, STT = V.tensor_tensor, V.tensor_scalar, V.scalar_tensor_tensor
    n = NJ + 1
    step(TS(nblk, total, SLOTS + 0.5, 1.0, ALU.is_gt, ALU.add))
    for b in range(2, T // SLOTS):
        step.settle()
        step(STT(out=nblk, in0=total, scalar=b * SLOTS + 0.5, in1=nblk, op0=ALU.is_gt, op1=ALU.add))
    step.settle()
    step(V.tensor_tensor_scan(incl, bc(ones[:, 0:1], [P, NE]), nblk, 0.0, ALU.mult, ALU.add))
    step.settle()
    step(TS(ints[:, 2 * n:2 * n + NE], incl, -1.0, None, ALU.add))
    row = lambda ap: bc(ap.rearrange("p (a e) -> p a e", a=1), [P, n, NE])
    step(TT(w, row(incl), bc(job_no[:, 0:n].rearrange("p (i a) -> p i a", a=1), [P, n, NE]), ALU.is_le))
    step.settle()
    step(V.tensor_reduce(JE, w, AX.X, ALU.add))
    step.settle()
    step(TT(w, w, row(nblk), ALU.mult))
    step.settle()
    step(V.tensor_reduce(JQ, w, AX.X, ALU.add))
    step.settle()
    step(TT(JQ, job_no[:, 0:n], JQ, ALU.subtract))
    step.settle()
    step(TS(JQ, JQ, float(T // SLOTS - 1), None, ALU.min))
    step.settle()
    step(V.tensor_copy(ints[:, 0:n], JE))
    step.settle()
    V.tensor_copy(ints[:, n:2 * n], JQ).then_inc(S["job_tables"], 1)


def layer_kernel(nc, A, out):
    with ExitStack() as ctx:
        def sb(name, cols, parts=P, dt=F32):
            return ctx.enter_context(nc.sbuf_tensor(name, [parts, cols], dt))[:]

        def sem(name):
            return ctx.enter_context(nc.semaphore(name))

        ring = sb("ring", NSLOT * UNIT)
        bank = [ctx.enter_context(nc.psum_tensor(f"bank{i}", [P, 512], F32))[:] for i in range(8)]

        def slot(i):
            return ring[:, i * UNIT:(i + 1) * UNIT]

        conv = ring[:, FSLOT * UNIT:].rearrange("p (m t) -> p m t", m=8)
        o_sb = ring[:, FSLOT * UNIT:FSLOT * UNIT + 1024]
        y_acc = ring[:, FSLOT * UNIT + 1024:FSLOT * UNIT + 2048]

        hA = sb("hA", 4096)
        hT = hA.rearrange("p (k t) -> p k t", k=KC)
        xs_tm = hA[:, 0:2048].rearrange("p (t c) -> p t c", t=4)
        xdt = hA[:, 2048:4096].rearrange("p (t d c) -> p t d c", t=2, d=2)
        brows = hA[0:NE, 0:3072]

        cB = sb("cB", 4096)
        xbc = cB.rearrange("p (m t) -> p m t", m=8)
        xw = cB[:, 0:2048].rearrange("p (t d c) -> p t d c", t=2, d=2)
        cbm = cB[:, 2048:2048 + 4 * SPAN].rearrange("p (d g c) -> p d g c", d=2, g=2)
        b_tm = cB[:, 3584:4096].rearrange("p (t g s) -> p t g s", t=2, g=2)
        mixT = cB[:, 0:2048].rearrange("p (k t) -> p k t", k=KC)
        h2 = cB[:, 2048:4096].rearrange("p (t c) -> p t c", t=NT)

        dB = sb("dB", 2048)
        k_fm = dB[:, 0:1024].rearrange("p (c t) -> p c t", c=2)
        q_fm = dB[:, 1024:1536].rearrange("p (c t) -> p c t", c=2)
        gk_fm = dB[0:RANK, 1536:2048]
        dt_fm = dB[64:64 + SH, 1536:2048]
        n2row = dB[:, 0:1024]
        fnrow = dB[:, 1024:2048]

        fB = sb("fB", 4096)
        vgz = fB[:, 0:3072].rearrange("p (t c) -> p t c", t=2)
        vx = fB[:, 3072:4096].rearrange("p (t c) -> p t c", t=2)
        h2T = fB[:, 0:2048].rearrange("p (k t) -> p k t", k=KC)

        gB = sb("gB", 4 * 2 * 257 + 2 * 1536)
        pre = gB[:, 0:2056].rearrange("p (n s t) -> p n s t", n=4, s=2)
        kv = [gB[:, 2056 + KV * i:2056 + KV * (i + 1)] for i in range(4)]
        soft = gB[:, 2056:2056 + 2048].rearrange("p (n t) -> p n t", n=4)
        sq = [gB[:, 512 * i:512 * (i + 1)] for i in range(KC)]
        rstd1 = gB[:, 4096:4608]
        sqout = gB[:, 4096:5120]
        g1b, sh2b, w2b, g2b = (gB[:, 1024 * i:1024 * (i + 1)] for i in range(4))

        pB = sb("pB", 2560)
        ld = pB[:, 0:2048].rearrange("p (n t) -> p n t", n=4)
        pt = pB[:, 0:4 * SPAN].rearrange("p (d e c) -> p d e c", d=2, e=2)
        seg = [pB[:, SPAN * i:SPAN * (i + 1)] for i in range(4)]
        x_tm = pB[:, 0:2048].rearrange("p (t c) -> p t c", t=2)

        qv = [sb(f"qv{i}", 256) for i in range(2)]
        kx = [sb(f"kx{i}", 256) for i in range(2)]
        qd_ = sb("qd", 512)
        qd = [qd_[:, 0:T], qd_[:, T:2 * T], dB[:, 1536:1536 + T], dB[:, 1536 + T:2048]]
        kxT = sb("kxT", 256)
        gS = sb("gS", 256).rearrange("p (d v) -> p d v", d=2)
        sS = sb("sS", 1024).rearrange("p (d c) -> p d c", d=2)
        mask = [sb(f"mask{d}", SPAN) for d in range(2)]
        upper, ones, lower = mask[0][:, 0:P], mask[0][:, P:2 * P], mask[1][:, 0:P]
        s_upper, s_lower, ident = sb("s_upper", P), sb("s_lower", P), sb("ident", P)
        slot_no = sb("slot_no", 2 * SLOTS)
        part_no = sb("part_no", SLOTS)
        cs = sb("cs", KC * 32).rearrange("p (k c) -> p k c", k=KC)
        c_in = sb("c_in", KC * 2).rearrange("p (k c) -> p k c", k=KC)
        modrow = sb("modrow", 1024).rearrange("p (r c) -> p r c", r=2)
        modrow1 = pB[:, 2048:2560]
        modc = sb("modc", 32).rearrange("p (g c) -> p g c", g=16)
        bmodT, n1T = sb("bmodT", 16), sb("n1T", KC)
        bgk = sb("bgk", 4)
        wup = dB[0:RANK, 1024:1536].rearrange("r (d c) -> r d c", d=2)
        wgk = pB[:, 0:KC * RANK].rearrange("p (k c) -> p k c", k=KC)
        wdt = cB[:, 4096 - KC * SH:].rearrange("p (k c) -> p k c", k=KC)
        convw = sb("convw", 72).rearrange("p (m j) -> p m j", m=8)
        convb = sb("convb", 8)
        gnrow, snrow = sb("gnrow", DV), pB[:, 2048:2560]
        d_row, dtb, negA = sb("d_row", SH), sb("dtb", 16), sb("negA", 16)
        dtb3, negA3 = (v.rearrange("p (d h) -> p d h", d=2) for v in (dtb, negA))
        dtr = sb("dtr", 4 * SH).rearrange("p (t h) -> p t h", t=4)
        dta = sb("dta", 64).rearrange("p (t d h) -> p t d h", t=4, d=2)
        dtt = sb("dtt", 64).rearrange("p (t d h) -> p t d h", t=4, d=2)
        a_tm = sb("a_tm", 64).rearrange("p (t d h) -> p t d h", t=4, d=2)
        acol = sb("acol", 64).rearrange("p (t d h) -> p t d h", t=4, d=2)
        eac = sb("eac", 64).rearrange("p (t d h) -> p t d h", t=4, d=2)
        stat = sb("stat", 32)
        wr = gS.rearrange("p d v -> p (d v)").rearrange("p (k e) -> p k e", k=KC)
        brrow = sb("brrow", NE)
        lg = fB[:, 3776:3840].rearrange("p (t e) -> p t e", t=2)
        top8 = fB[:, 3840:3856].rearrange("p (t e) -> p t e", t=2)
        rt = [kxT[:, 64 * i:64 * i + 64].rearrange("p (t e) -> p t e", t=2) for i in range(4)]
        RT, GT = (qv[1][:, i * 2 * (NE + 1):(i + 1) * 2 * (NE + 1)].rearrange("p (t j) -> p t j", t=2) for i in range(2))
        JE, JQ = kx[0][:, 0:NJ + 1], kx[0][:, P:P + NJ + 1]
        ints = sb("ints", 2 * (NJ + 1) + NE, dt=I32)
        int_e = lambda j: ints[0:1, bass.ds(j, 1)]
        int_q = lambda j: ints[0:1, bass.ds(j + NJ + 1, 1)]
        int_last = lambda e: ints[0:1, bass.ds(e + 2 * (NJ + 1), 1)]
        cnt = fB[:, 3856:3952].rearrange("p (i e) -> p i e", i=3)
        S_j = fB[:, 2048:2176].rearrange("p (t s) -> p t s", t=2)
        SG_j = fB[:, 2176:2432].rearrange("p (t s) -> p t s", t=2)
        SGT = fB[:, 2432:2688].rearrange("p (t c) -> p t c", t=2)
        xg = fB[:, 2688:3200].rearrange("p (k s) -> p k s", k=KC)
        gm = fB[:, 3200:3712]
        sig = sS.rearrange("p d c -> p (d c)")[:, 0:512]
        act = sS.rearrange("p d c -> p (d c)")[:, 512:1024]
        actT = modrow.rearrange("p r c -> p (r c)")[:, 0:512].rearrange("p (q c) -> p q c", q=4)
        ysb = modrow.rearrange("p r c -> p (r c)")[:, 512:1024]
        job_sel = fB[0:NE, 3712:3776]
        jobs_w = fB[:, 0:(NJ + 1) * NE].rearrange("p (i e) -> p i e", e=NE)
        slot_q = cB[:, 0:2 * T]
        job_no = cB[:, 2 * T:2 * T + NJ + 1]

        loaded = [sem(f"slot{i}_loaded") for i in range(NSLOT)]
        names = """norm_in ones_ready modc_ready hl_ready hx_ready dtT_ready dtt_done gla_sq ssd_sq log_done rank_done mod1_used mod2_used cT_in xT_in small_in late_in consts zeroed cs_ready row1_ready
        sq_ready sq_summed sum_done rinv_ready rstd_ready xh_ready h_ready
        fm_done fm_evac gate_done gate_read soft_arg soft_ready
        tm_done tm_evac misc_filled misc_read conv_ready conv_act
        dt_ready dt_exp dt_sp kvarg_ready exp_ready kvmul_ready
        score_done pt_ready o_done o_copied
        sn_in eac_ready negA_ready rb_done arg_ready segexp_ready segm_ready segm_used ydiag_done
        row2_ready rows_ready silu_ready gst sst gsq ssq mix_ready ex_ready ex_done h2_ready yz_ready sel_made xw_ready seg0
        op_done op_read xnew_ready nsq nst
        s_ready sg_ready sgt_ready sel_ready gather_done xg_ready gu_done gm_ready sig_ready
        act_ready actT_done actT_ready sel_used y_ready sgt_done scat_done moe_used moe_done up_read
        job_tables slots_ready fsq fst out_ready stored dve act pool mr""".split()
        S = {n: sem(n) for n in names}

        class Steps:

            def __init__(self, eng, sm):
                self.eng, self.sm, self.n = eng, sm, 0

            def __call__(self, ins):
                self.n += 1
                ins.then_inc(self.sm, 1)

            def settle(self):
                self.eng.wait_ge(self.sm, self.n)

        MISC = (bank[2], bank[7])
        M_MODT, M_CB, M_B = 0, 1, 3
        M_ACOL = 4
        M_GLA = 5
        M_X = 13
        X_ORDER = (2, 3, 0, 1)
        M_ST = 17
        M_YOFF = 19
        M_ROWS = (23, 24, 25, 26, 29, 30, 31, 32)
        M_MIXT = (27, 28, 33, 34)
        M_H2T = 35

        def in_item_bank(i):
            return bank[3 + i % 2]

        def op_bank(r):
            return bank[(3, 4, 1, 0)[r]]

        def rb_bank(i):
            return bank[(3, 4, 1)[i % 3]]

        FM = [("gk", 0, True)] + [("xbc", m, m < 6) for m in range(8)] + [("k", 0, True), ("k", 1, True),
                                                                       ("q", 0, False), ("q", 1, False)]
        TM = [("dt", 0, 0), ("v", 0, 0), ("v", 0, 1), ("v", 1, 0), ("v", 1, 1),
              ("g", 0, 0), ("g", 1, 0), ("z", 0, 0), ("z", 1, 0)]
        U_IN = N_MOD1
        U_MOD2 = U_IN + N_IN
        U_OUT = U_MOD2 + N_MOD2

        def consumed(u):
            if u < U_IN:
                return S["mod1_used"], u + 1
            if u < U_IN + 6:
                return S["fm_done"], 2 * (u - U_IN) + 3
            if u < U_MOD2:
                return S["tm_done"], (3, 5, 6, 7, 8, 9)[u - U_IN - 6]
            if u < U_OUT:
                return S["mod2_used"], u - U_MOD2 + 1
            return S["op_done"], 4 if u < U_OUT + 2 else 8

        def front_slot(u):
            return slot(u % FSLOT)

        def await_unit(eng, u):
            eng.wait_ge(loaded[u % FSLOT], 16 * (u // FSLOT + 1))

        GU = A["w_gate_up"].rearrange("e (k p) f -> e k p f", p=P)
        DN = A["w_down"].rearrange("e (i k p) f -> e i p k f", p=P, k=2)

        block = ctx.enter_context(nc.Block())

        @block.sync
        def _(sp):
            sp.dma_start(c_in, A["c2"].rearrange("k p c -> p k c")).then_inc(S["cT_in"], 16)

            def front_unit(u):
                if u >= FSLOT:
                    sp.wait_ge(*consumed(u - FSLOT))
                dst = front_slot(u)
                if u < U_IN:
                    src = A["w_mod"][u * P:(u + 1) * P, 0:UNIT]
                elif u < U_MOD2:
                    src = A["w_in"][u - U_IN]
                elif u < U_OUT:
                    r, k = divmod(u - U_MOD2, KC)
                    src = A["w_mod"][k * P:(k + 1) * P, (r + 1) * UNIT:(r + 2) * UNIT]
                else:
                    i = u - U_OUT
                    src = A["w_out"][2 * i * P:2 * (i + 1) * P, :].rearrange("(k p) n -> p k n", p=P)
                    dst = dst.rearrange("p (k n) -> p k n", k=2)
                sp.dma_start(dst, src).then_inc(loaded[u % FSLOT], 16)

            sp.dma_start(hT[:, :, 0:T], A["xT"].rearrange("k p t -> p k t")).then_inc(S["xT_in"], 16)
            sp.dma_start(hT[:, :, T:T + TX], A["ctxT"].rearrange("k p t -> p k t")).then_inc(S["xT_in"], 16)
            for u in range(N_FRONT):
                front_unit(u)

            def expert_unit(i, gate_up, down):
                dst = slot(i)
                if i < KC:
                    sp.dma_start(dst, gate_up[i]).then_inc(loaded[i], 16)
                else:
                    sp.dma_start(dst.rearrange("p (k n) -> p k n", k=2), down[i - KC]).then_inc(loaded[i], 16)

            for i in range(NSLOT):
                if i < FSLOT:
                    sp.wait_ge(*consumed(N_FRONT - FSLOT + i))
                else:
                    sp.wait_ge(S["mix_ready"], 2)
                expert_unit(i, GU[0], DN[0])

            def dyn(e):
                return (GU[bass.ds(e, 1)].rearrange("e k p f -> (e k) p f"),
                        DN[bass.ds(e, 1)].rearrange("e i p k f -> (e i) p k f"))

            sp.wait_ge(S["job_tables"], 1)
            with sp.Fori(1, NE) as e:
                g, d = dyn(e)
                last = sp.value_load(int_last(e - 1), min_val=0, max_val=NJ - 1)
                for i in range(NSLOT):
                    sp.wait_ge(S["moe_used"], NSLOT * last + (i + 1))
                    expert_unit(i, g, d)
            for t in range(NT):
                sp.wait_ge(S["out_ready"], t + 1)
                sp.dma_start(out[0, t * P:(t + 1) * P, :], x_tm[:, t, :]).then_inc(S["stored"], 16)
            sp.wait_ge(S["stored"], 16 * NT)

        @block.gpsimd
        def _(pool):
            step = Steps(pool, S["pool"])
            small = [(bgk, A["bgk"]), (wup, A["wup"]),
                     (wgk, A["wgk"].rearrange("k p c -> p k c")), (wdt, A["wdt"].rearrange("k p c -> p k c")),
                     (convw, A["convw"]), (convb, A["convb"]),
                     (gnrow, A["gla_norm"].partition_broadcast(P)),
                     (d_row, A["ssd_D"].partition_broadcast(P)), (dtb, A["dtb"].partition_broadcast(P)),
                     (negA, A["alog"].partition_broadcast(P)),
                     (brrow, A["b_router"].partition_broadcast(P))]
            assert len(small) == N_SMALL
            nc.gpsimd.memset(cs, 0.0).then_inc(S["zeroed"], 1)
            nc.gpsimd.memset(mask[0], 1.0).then_inc(S["ones_ready"], 1)
            pool.dma_start(bmodT, A["bmodT"]).then_inc(S["norm_in"], 16)
            pool.dma_start(n1T, A["n1T"]).then_inc(S["norm_in"], 16)
            pool.wait_ge(S["ones_ready"], 1)
            step(nc.gpsimd.memset(mask[1], 1.0))
            step(nc.gpsimd.memset(ident, 0.0))
            step(nc.gpsimd.memset(modrow, 0.0))
            step(nc.gpsimd.iota(
                slot_no.rearrange("p (a s) -> p a s", a=2), [[0, 2], [1, SLOTS]], base=0, channel_multiplier=0,
                allow_small_or_imprecise_dtypes=True))
            step(nc.gpsimd.iota(part_no, [[0, SLOTS]], base=0, channel_multiplier=1,
                                allow_small_or_imprecise_dtypes=True))
            step.settle()
            for d, sgn in ((0, 1), (1, -1)):
                for b in (0, 2):
                    v = mask[d][:, b * P:(b + 1) * P]
                    step(nc.gpsimd.affine_select(out=v, in_=v, compare_op=ALU.is_ge, fill=0.0, base=0,
                                                 pattern=[[sgn, P]], channel_multiplier=-sgn))
            step(nc.gpsimd.affine_select(out=ident, in_=ident, compare_op=ALU.not_equal, fill=1.0, base=0,
                                         pattern=[[-1, P]], channel_multiplier=1))
            step(nc.gpsimd.affine_select(out=s_upper, in_=ones, compare_op=ALU.is_gt, fill=0.0, base=0,
                                         pattern=[[1, P]], channel_multiplier=-1))
            step(nc.gpsimd.affine_select(out=s_lower, in_=ones, compare_op=ALU.is_gt, fill=0.0, base=0,
                                         pattern=[[-1, P]], channel_multiplier=1))
            step.settle()
            nc.gpsimd.memset(stat, 0.0).then_inc(S["consts"], 1)
            for dst, src in small:
                pool.dma_start(dst, src).then_inc(S["small_in"], 16)
            for g in range(4):
                pool.dma_start(modrow[32 * g:32 * g + 1], A["b_mod2"][:, g:g + 1, :].rearrange("r g c -> g r c")
                               ).then_inc(S["mr"], 16)
            pool.wait_ge(S["misc_filled"], M_MODT + 1)
            pool.dma_start(snrow, A["ssd_norm"].partition_broadcast(P)).then_inc(S["sn_in"], 16)
            pool.wait_ge(S["kvmul_ready"], 4)
            pool.wait_ge(S["o_done"], 2)
            pool.dma_start(wr, A["w_router"].rearrange("(k p) e -> p k e", p=P)).then_inc(S["late_in"], 16)
            pool.dma_start(n2row, A["norm2"].partition_broadcast(P)).then_inc(S["late_in"], 16)
            pool.dma_start(fnrow, A["final_norm"].partition_broadcast(P)).then_inc(S["late_in"], 16)
            pool.wait_ge(S["ydiag_done"], SH)
            pool.wait_ge(S["segm_ready"], 2 * SH)
            pool.dma_start(x_tm, A["x"].rearrange("(t p) c -> p t c", p=P)).then_inc(S["late_in"], 16)
            pool.dma_start(brows, A["b_moe"]).then_inc(S["late_in"], 16)
            pool.wait_ge(S["op_done"], 8)
            nc.gpsimd.iota(job_no, [[1, NJ + 1]], base=0, channel_multiplier=0,
                           allow_small_or_imprecise_dtypes=True).then_inc(S["slots_ready"], 1)
            nc.gpsimd.iota(slot_q.rearrange("p (q a s) -> p q a s", a=2, s=SLOTS), [[SLOTS, T // SLOTS], [0, 2], [1, SLOTS]],
                           base=0, channel_multiplier=0, allow_small_or_imprecise_dtypes=True).then_inc(S["slots_ready"], 1)

        @block.scalar
        def _(sc):
            step = Steps(sc, S["act"])
            A_ = nc.scalar.activation
            sc.wait_ge(S["cT_in"], 16)
            sc.wait_ge(S["zeroed"], 1)
            A_(cs[:, :, 0:2], c_in, ACT.Silu).then_inc(S["cs_ready"], 1)
            sc.wait_ge(S["xT_in"], 32)
            for k in range(KC):
                A_(sq[k], hT[:, k, :], ACT.Square).then_inc(S["sq_ready"], 1)
            sc.wait_ge(S["rinv_ready"], 1)
            A_(rstd1, rstd1, ACT.Sqrt).then_inc(S["rstd_ready"], 1)
            sc.wait_ge(S["modc_ready"], 1)
            for k in range(KC):
                v = hT[:, k, T:T + TX]
                A_(v, v, ACT.Identity, bias=modc[:, k, 1:2], scale=modc[:, 8 + k, 1:2]).then_inc(S["hx_ready"], 1)

            def fm_evac(i):
                kind, m, with_ctx = FM[i]
                n = T + TX if with_ctx else T
                src = in_item_bank(i)
                sc.wait_ge(S["fm_done"], i + 1)
                if kind == "gk":
                    A_(dt_fm, src[64:64 + SH, 0:n], ACT.Copy).then_inc(S["dtT_ready"], 1)
                    A_(gk_fm, src[0:RANK, 0:n], ACT.Copy).then_inc(S["fm_evac"], 1)
                elif kind == "xbc":
                    A_(xbc[:, m, 0:n], src[:, 0:n], ACT.Copy).then_inc(S["fm_evac"], 1)
                elif kind == "k":
                    A_(k_fm[:, m, :], src, ACT.Copy).then_inc(S["fm_evac"], 1)
                else:
                    A_(q_fm[:, m, :], src[:, 0:n], ACT.Copy, scale=DK ** -0.5).then_inc(S["fm_evac"], 1)

            def conv_silu(m):
                n = T + TX if m < 6 else T
                sc.wait_ge(S["conv_ready"], m + 1)
                A_(conv[:, m, 0:n], conv[:, m, 0:n], ACT.Silu).then_inc(S["conv_act"], 1)

            for i in range(3):
                fm_evac(i)
            sc.wait_ge(S["soft_arg"], 1)
            step(A_(soft, soft, ACT.Exp))
            step.settle()
            A_(soft, soft, ACT.Ln, bias=1.0).then_inc(S["soft_ready"], 1)
            for i in range(3, len(FM)):
                fm_evac(i)
                if i >= 5:
                    conv_silu(i - 5)

            def tm_evac(i):
                kind, half, c = TM[i]
                b = in_item_bank(len(FM) + i)
                sc.wait_ge(S["tm_done"], i + 1)
                if kind == "dt":
                    A_(dtr, b[:, 0:4 * SH].rearrange("p (t h) -> p t h", t=4), ACT.Copy).then_inc(S["tm_evac"], 1)
                    return
                col = {"v": 0, "g": 512, "z": 1024}[kind] + 256 * half
                dst = (vx if c else vgz)[:, :, col:col + 256]
                A_(dst, b.rearrange("p (t c) -> p t c", t=2), ACT.Copy).then_inc(S["tm_evac"], 1)

            tm_evac(0)
            sc.wait_ge(S["small_in"], 16 * N_SMALL)
            A_(negA, negA, ACT.Exp).then_inc(S["negA_ready"], 1)
            sc.wait_ge(S["dt_ready"], 1)
            step(A_(dtt, dtt, ACT.Exp))
            step.settle()
            A_(dtt, dtt, ACT.Ln, bias=1.0).then_inc(S["dt_sp"], 1)

            def decay_exps(n):
                d = n % 2
                b = n % 2
                up = 1.0 / GATE_NORM
                sc.wait_ge(S["kvarg_ready"], n + 1)
                sgn = -1.0 if d == 0 else 1.0
                A_(kv[n], kv[n], ACT.Exp, scale=sgn * up).then_inc(S["exp_ready"], 1)
                A_(qv[b], qv[b], ACT.Exp, scale=-sgn * up).then_inc(S["exp_ready"], 1)
                if d == 0:
                    A_(qd[n], pre[:, n, 0, 1:T + 1], ACT.Exp, scale=up).then_inc(S["exp_ready"], 1)
                    A_(kx[b], pre[:, n, 1, 1:TX + 1], ACT.Exp, scale=-up,
                       bias=stat[:, 16 + n:17 + n]).then_inc(S["exp_ready"], 1)
                else:
                    A_(qd[n], pre[:, n, 0, 0:T], ACT.Exp, scale=-up,
                       bias=stat[:, 16 + n:17 + n]).then_inc(S["exp_ready"], 1)
                    A_(kx[b], pre[:, n, 1, 0:TX], ACT.Exp, scale=up).then_inc(S["exp_ready"], 1)

            def o_copy(c):
                sc.wait_ge(S["o_done"], c + 1)
                ov_ = o_sb.rearrange("p (t h v) -> p t h v", t=2, h=GH)
                for e in range(2):
                    src = bank[5 + e].rearrange("p (t c v) -> p t c v", t=2, c=2)[:, :, c, :]
                    A_(ov_[:, :, 2 * c + e, :], src, ACT.Copy).then_inc(S["o_copied"], 1)

            tm_evac(1)
            tm_evac(2)
            decay_exps(0)
            tm_evac(3)
            tm_evac(4)
            decay_exps(1)
            sc.wait_ge(S["misc_read"], M_ACOL + 1)
            A_(eac, acol, ACT.Exp).then_inc(S["eac_ready"], 1)
            tm_evac(5)
            decay_exps(2)
            tm_evac(6)
            decay_exps(3)
            tm_evac(7)
            tm_evac(8)
            sc.wait_ge(S["misc_filled"], M_X + 4)
            o_copy(0)
            o_copy(1)
            sc.wait_ge(S["tm_evac"], len(TM))
            gz = vgz[:, :, 512:1536]
            A_(gz, gz, ACT.Silu).then_inc(S["silu_ready"], 1)
            sc.wait_ge(S["o_copied"], 4)
            for a in range(8):
                last = A_(sqout[:, a * DV:(a + 1) * DV], o_sb[:, a * DV:(a + 1) * DV], ACT.Square,
                          accum_out=stat[:, a:a + 1])
            last.then_inc(S["gla_sq"], 1)
            sc.wait_ge(S["gst"], 1)
            A_(stat[:, 0:8], stat[:, 0:8], ACT.Sqrt).then_inc(S["gsq"], 1)

            def mod_row(i):
                sc.wait_ge(S["misc_filled"], M_ROWS[i] + 1)
                sc.wait_ge(S["misc_read"], M_ROWS[i])
                A_(gB[:, 512 * i:512 * (i + 1)], MISC[M_ROWS[i] % 2], ACT.Identity,
                   bias=1.0 if i in (4, 5) else 0.0).then_inc(S["misc_read"], 1)

            def mix_t(half, t):
                m = M_MIXT[2 * half + t]
                sc.wait_ge(S["misc_filled"], m + 1)
                sc.wait_ge(S["misc_read"], m)
                A_(mixT[:, 4 * half:4 * half + 4, t * P:(t + 1) * P],
                   MISC[m % 2].rearrange("p (q c) -> p q c", q=4), ACT.Copy).then_inc(S["misc_read"], 1)

            for i in range(2 * SH):
                sc.wait_ge(S["arg_ready"], i + 1)
                A_(seg[i % 4], seg[i % 4], ACT.Exp).then_inc(S["segexp_ready"], 1)
                if i in (12, 14):
                    mod_row(i - 12)
                    mod_row(i - 11)
            mix_t(0, 0)
            mix_t(0, 1)
            for t in range(2):
                sc.wait_ge(S["yz_ready"], t + 1)
                for g in range(SG):
                    last = A_(sqout[:, 512 * t + 256 * g:512 * t + 256 * (g + 1)], y_acc[:, 512 * t + 256 * g:512 * t + 256 * (g + 1)],
                              ACT.Square, accum_out=stat[:, 8 + 2 * t + g:9 + 2 * t + g])
            last.then_inc(S["ssd_sq"], 1)
            sc.wait_ge(S["sst"], 1)
            A_(stat[:, 8:12], stat[:, 8:12], ACT.Sqrt).then_inc(S["ssq"], 1)
            for i in range(4, 8):
                mod_row(i)
            mix_t(1, 0)
            mix_t(1, 1)

            def h2_t(t):
                for half in range(2):
                    m = M_H2T + 2 * t + half
                    sc.wait_ge(S["misc_filled"], m + 1)
                    sc.wait_ge(S["misc_read"], m)
                    A_(h2T[:, 4 * half:4 * half + 4, t * P:(t + 1) * P],
                       MISC[m % 2].rearrange("p (q c) -> p q c", q=4), ACT.Copy).then_inc(S["misc_read"], 1)

            for t in range(NT):
                sc.wait_ge(S["xnew_ready"], 2 * (t + 1))
                A_(fB[:, 2048:3072], x_tm[:, t, :], ACT.Square,
                   accum_out=stat[:, 20 + t:21 + t]).then_inc(S["nsq"], 1)
                sc.wait_ge(S["nst"], t + 1)
                A_(stat[:, 22 + t:23 + t], stat[:, 22 + t:23 + t], ACT.Sqrt).then_inc(S["nsq"], 1)
                if t == 0:
                    h2_t(0)
            h2_t(1)

            sc.wait_ge(S["ex_ready"], 1)
            A_(rt[3], rt[3], ACT.Exp).then_inc(S["ex_done"], 1)

            def job(j):
                sc.wait_ge(S["gm_ready"], j + 1)
                A_(sig, gm, ACT.Sigmoid, scale=ALPHA).then_inc(S["sig_ready"], 1)

            with sc.Fori(0, NE) as j:
                job(j)
            sc.wait_ge(S["job_tables"], 1)
            last = sc.value_load(int_last(NE - 1), min_val=NE - 1, max_val=NJ - 1)
            with sc.Fori(NE, NE + FEW) as j:
                with sc.If(last > j - 1):
                    job(j)
            with sc.If(last > NE + FEW - 1):
                with sc.Fori(NE + FEW, NJ) as j:
                    with sc.If(last > j - 1):
                        job(j)
            A_(stat[:, 30:31], stat[:, 30:31], ACT.Sqrt)
            for t in range(NT):
                sc.wait_ge(S["fsq"], t + 1)
                A_(h2[:, t, :], x_tm[:, t, :], ACT.Square, accum_out=stat[:, 24 + t:25 + t]).then_inc(S["fst"], 1)
            for t in range(NT):
                sc.wait_ge(S["fsq"], NT + t + 1)
                A_(stat[:, 26 + t:27 + t], stat[:, 26 + t:27 + t], ACT.Sqrt).then_inc(S["fst"], 1)

        @block.tensor
        def _(pe):
            mm = nc.tensor.matmul

            def misc_begin(i):
                if i >= 2:
                    pe.wait_ge(S["misc_read"], i - 1)
                return MISC[i % 2]

            def mod_unit(u, dst, k, used):
                await_unit(pe, u)
                w = front_slot(u)
                for g in range(4):
                    last = mm(dst[32 * g:32 * g + 32, :], cs[:, k, :], w[:, 512 * g:512 * (g + 1)],
                              start=(k == 0), stop=(k == KC - 1))
                last.then_inc(used, 1)

            pe.wait_ge(S["ones_ready"], 1)
            for k in range(KC):
                pe.wait_ge(S["sq_ready"], k + 1)
                mm(bank[1], ones, sq[k], start=(k == 0), stop=(k == KC - 1)).then_inc(S["sq_summed"], 1)
            pe.wait_ge(S["cs_ready"], 1)
            for k in range(KC):
                mod_unit(k, bank[0], k, S["mod1_used"])
            pe.wait_ge(S["consts"], 1)
            b = misc_begin(M_MODT)
            pe.wait_ge(S["row1_ready"], 1)
            for q in range(4):
                last = nc.tensor.transpose(b[:, q * P:(q + 1) * P], modrow1[:, q * P:(q + 1) * P], ident)
            last.then_inc(S["misc_filled"], 1)

            def fm_chunk(i):
                kind, m, with_ctx = FM[i]
                n = T + TX if with_ctx else T
                b = in_item_bank(i)
                u = U_IN + (i - 1) // 2
                if kind != "gk":
                    await_unit(pe, u)
                    w = front_slot(u).rearrange("p (k c) -> p k c", k=KC)[:, :, P * ((i - 1) % 2):P * ((i - 1) % 2) + P]
                else:
                    w = wgk
                    pe.wait_ge(S["small_in"], 16 * N_SMALL)
                if i >= 2:
                    pe.wait_ge(S["fm_evac"], i - 1)
                for k in range(KC):
                    if i == 0:
                        pe.wait_ge(S["hl_ready"], k + 1)
                        pe.wait_ge(S["hx_ready"], k + 1)
                    last = mm(b[0:w.shape[2], 0:n], w[:, k, :], hT[:, k, 0:n], start=(k == 0), stop=(k == KC - 1))
                    if i == 0:
                        last = mm(b[64:64 + SH, 0:n], wdt[:, k, :], hT[:, k, 0:n], start=(k == 0), stop=(k == KC - 1))
                last.then_inc(S["fm_done"], 1)

            def fm_unit(a):
                fm_chunk(a)
                fm_chunk(a + 1)

            fm_chunk(0)
            fm_unit(1)
            pe.wait_ge(S["fm_evac"], 1)
            for n in range(4):
                c, d = divmod(n, 2)
                if n >= 2:
                    pe.wait_ge(S["gate_read"], n - 1)
                mm(bank[5 + n % 2], wup[:, d, c * P:(c + 1) * P], gk_fm, start=True, stop=True
                   ).then_inc(S["gate_done"], 1)
            for a in range(3, len(FM), 2):
                fm_unit(a)

            def tm_item(i):
                kind, half, c = TM[i]
                n = len(FM) + i
                b = in_item_bank(n)
                if i == 0:
                    pe.wait_ge(S["fm_evac"], n - 1)
                elif i == 1:
                    pe.wait_ge(S["fm_evac"], n - 1)
                else:
                    pe.wait_ge(S["tm_evac"], i - 1)
                if kind == "dt":
                    pe.wait_ge(S["dtT_ready"], 1)
                    for t in range(4):
                        last = nc.tensor.transpose(b[:, SH * t:SH * (t + 1)], dt_fm[:, t * P:(t + 1) * P],
                                                   ident[64:64 + SH, 64:64 + SH])
                    last.then_inc(S["tm_done"], 1)
                    return
                u = U_IN + 6 + {"v": 0, "g": 2, "z": 4}[kind] + half
                await_unit(pe, u)
                w = front_slot(u).rearrange("p (k c) -> p k c", k=KC)
                for t in range(2):
                    for k in range(KC):
                        last = mm(b[:, 256 * t:256 * (t + 1)], hT[:, k, (2 * c + t) * P:(2 * c + t + 1) * P], w[:, k, :],
                                  start=(k == 0), stop=(k == KC - 1))
                last.then_inc(S["tm_done"], 1)

            def acol_sums():
                b = misc_begin(M_ACOL)
                pe.wait_ge(S["dt_exp"], 1)
                for d in range(2):
                    near, far = (upper, 0) if d == 0 else (lower, 1)
                    for t in range(2):
                        dst = b[:, (t * 2 + d) * SH:(t * 2 + d + 1) * SH]
                        both = t != far
                        mm(dst, near, a_tm[:, t, d, :], start=True, stop=not both)
                        if both:
                            mm(dst, ones, a_tm[:, 1 - t, d, :], start=False, stop=True)
                    near, far = (s_lower, 1) if d == 0 else (s_upper, 0)
                    for t in range(2):
                        dst = b[:, ((2 + t) * 2 + d) * SH:((2 + t) * 2 + d + 1) * SH]
                        both = t != far
                        last = mm(dst, near, a_tm[:, 2 + t, d, :], start=True, stop=not both)
                        if both:
                            last = mm(dst, ones, a_tm[:, 3 - t, d, :], start=False, stop=True)
                last.then_inc(S["misc_filled"], 1)

            for i in range(3):
                tm_item(i)
            pe.wait_ge(S["conv_act"], 8)
            for g in range(SG):
                b = misc_begin(M_CB + g)
                for jt in range(2):
                    last = mm(b[:, 256 * jt:256 * (jt + 1)], conv[:, 4 + g, jt * P:(jt + 1) * P], conv[:, 6 + g, 0:T],
                              start=True, stop=True)
                last.then_inc(S["misc_filled"], 1)
            b = misc_begin(M_B)
            for t in range(2):
                for g in range(SG):
                    last = nc.tensor.transpose(b[:, (2 * t + g) * P:(2 * t + g + 1) * P],
                                               conv[:, 4 + g, (2 + t) * P:(3 + t) * P], ident)
            last.then_inc(S["misc_filled"], 1)

            def gla_scores(n):
                c, d = divmod(n, 2)
                kb, qb = kv[n], qv[n % 2]
                pe.wait_ge(S["kvmul_ready"], n + 1)
                for e in range(2):
                    rows = slice(64 * e, 64 * e + 64)
                    b = bank[e]
                    if n >= 1:
                        pe.wait_ge(S["pt_ready"], 2 * (n - 1) + e + 1)
                    elif e == 0:
                        pe.wait_ge(S["row1_ready"], 1)
                    else:
                        pe.wait_ge(S["rinv_ready"], 1)
                    for blk in range(NB):
                        near = (blk < NPT) == (d == 0)
                        i4 = blk % NPT
                        q = qb[rows, blk * BLK:(blk + 1) * BLK]
                        if near:
                            col = (0 if d == 0 else 2 * P) + i4 * BLK
                            last = mm(b[:, col:col + BLK], kb[rows, i4 * P:(i4 + 1) * P], q, start=True, stop=True)
                        else:
                            for jt in range(2):
                                col = (1 + jt if d == 0 else jt) * P + i4 * BLK
                                last = mm(b[:, col:col + BLK],
                                          kb[rows, KNEAR + T * i4 + P * jt:KNEAR + T * i4 + P * (jt + 1)], q,
                                          start=True, stop=True)
                    last.then_inc(S["score_done"], 1)
                b = misc_begin(M_GLA + 2 * n)
                for t in range(2):
                    last = nc.tensor.transpose(b[:, t * P:(t + 1) * P], kx[n % 2][:, t * P:(t + 1) * P], ident)
                last.then_inc(S["misc_filled"], 1)
                b = misc_begin(M_GLA + 2 * n + 1)
                pe.wait_ge(S["misc_read"], M_GLA + 2 * n + 1)
                pe.wait_ge(S["tm_evac"], 5)
                for e in range(2):
                    h = 2 * c + e
                    for t in range(2):
                        last = mm(b[64 * e:64 * e + 64, 0:DV], kxT[:, t * P + 64 * e:t * P + 64 * e + 64],
                                  vx[:, t, h * DV:(h + 1) * DV], start=(t == 0), stop=(t == 1))
                last.then_inc(S["misc_filled"], 1)

            def gla_out(c):
                pe.wait_ge(S["pt_ready"], 4 * (c + 1))
                pe.wait_ge(S["misc_read"], M_GLA + 4 * (c + 1))
                if c == 0:
                    pe.wait_ge(S["gate_read"], 4)
                for e in range(2):
                    h = 2 * c + e
                    rows = slice(64 * e, 64 * e + 64)
                    for t in range(2):
                        dst = bank[5 + e][:, (2 * t + c) * DV:(2 * t + c + 1) * DV]
                        terms = [(0, 0, 0), (1, 0, 0), (1, 1, 1)] if t == 0 else [(0, 0, 1), (0, 1, 2), (1, 1, 2)]
                        for x, (d, jt, s) in enumerate(terms):
                            mm(dst, pt[:, d, e, s * P:(s + 1) * P], vgz[:, jt, h * DV:(h + 1) * DV],
                               start=(x == 0), stop=False)
                        for d in range(2):
                            last = mm(dst, qd[2 * c + d][rows, t * P:(t + 1) * P], gS[rows, d, :], start=False, stop=(d == 1))
                last.then_inc(S["o_done"], 1)

            def x_t(i):
                b = misc_begin(M_X + i)
                t = X_ORDER[i]
                for m in range(4):
                    last = nc.tensor.transpose(b[:, m * P:(m + 1) * P], conv[:, m, t * P:(t + 1) * P], ident)
                last.then_inc(S["misc_filled"], 1)

            acol_sums()
            tm_item(3)
            tm_item(4)
            gla_scores(0)
            tm_item(5)
            gla_scores(1)
            tm_item(6)
            gla_out(0)
            tm_item(7)
            gla_scores(2)
            tm_item(8)
            gla_scores(3)
            x_t(0)
            x_t(1)
            gla_out(1)
            x_t(2)
            x_t(3)
            for d in range(2):
                b = misc_begin(M_ST + d)
                pe.wait_ge(S["xw_ready"], d + 1)
                for g in range(SG):
                    for t in range(2):
                        last = mm(b[:, 256 * g:256 * (g + 1)], b_tm[:, t, g, :], xw[:, t, d, 256 * g:256 * (g + 1)],
                                  start=(t == 0), stop=(t == 1))
                last.then_inc(S["misc_filled"], 1)
            for t in range(2):
                for d in range(2):
                    b = misc_begin(M_YOFF + 2 * t + d)
                    pe.wait_ge(S["misc_read"], M_ST + d + 1)
                    for g in range(SG):
                        last = mm(b[:, 256 * g:256 * (g + 1)], conv[:, 6 + g, t * P:(t + 1) * P],
                                  sS[:, d, 256 * g:256 * (g + 1)], start=True, stop=True)
                    last.then_inc(S["misc_filled"], 1)

            def row_sums(i):
                h, d = divmod(i, 2)
                b = rb_bank(i)
                if i >= 3:
                    pe.wait_ge(S["arg_ready"], i - 2)
                elif i == 0:
                    pe.wait_ge(S["tm_evac"], len(TM))
                tri = (upper, lower)[d]
                a = [bc(a_tm[:, t, d, h:h + 1], [P, P]) for t in range(2)]
                for t in range(2):
                    dst = b[:, t * P:(t + 1) * P]
                    both = t == 1 - d
                    last = mm(dst, a[t], tri, start=True, stop=not both)
                    if both:
                        last = mm(dst, a[1 - t], ones, start=False, stop=True)
                last.then_inc(S["rb_done"], 1)

            def ssd_out(h):
                pe.wait_ge(S["segm_ready"], 2 * h + 2)
                if h == 0:
                    pe.wait_ge(S["o_copied"], 4)
                for t in range(2):
                    dst = bank[5 + t][:, h * HP:(h + 1) * HP]
                    terms = [(0, 0, 0), (1, 0, 0), (1, 1, 1)] if t == 0 else [(0, 0, 1), (0, 1, 2), (1, 1, 2)]
                    for x, (d, jt, s) in enumerate(terms):
                        last = mm(dst, seg[(2 * h + d) % 4][:, s * P:(s + 1) * P], xdt[:, jt, d, h * HP:(h + 1) * HP],
                                  start=(x == 0), stop=(x == 2))
                last.then_inc(S["ydiag_done"], 1)

            pe.wait_ge(S["pt_ready"], 8)
            for i in range(3):
                row_sums(i)

            def mod_row(i):
                b = misc_begin(M_ROWS[i])
                pe.wait_ge(S["row2_ready"], i // 4 + 1)
                g = 32 * (i % 4)
                mm(b, ones[g:g + 1, :], modrow[g:g + 1, i // 4, :], start=True, stop=True
                   ).then_inc(S["misc_filled"], 1)

            def mix_t(half, t):
                b = misc_begin(M_MIXT[2 * half + t])
                pe.wait_ge(S["mix_ready"], half + 1)
                for q in range(4):
                    col = 512 + (4 * half + q) * P
                    last = nc.tensor.transpose(b[:, q * P:(q + 1) * P], vgz[:, t, col:col + P], ident)
                last.then_inc(S["misc_filled"], 1)

            for h in range(SH):
                for d in range(2):
                    m = 2 * h + d
                    if m == KC:
                        pe.wait_ge(S["row2_ready"], 1)
                    mod_unit(U_MOD2 + m, bank[0], m % KC, S["mod2_used"])
                for i in (2 * h + 3, 2 * h + 4):
                    if i < 2 * SH:
                        row_sums(i)
                if h in (5, 6):
                    mod_row(2 * (h - 5))
                    mod_row(2 * (h - 5) + 1)
                if h == 7:
                    mix_t(0, 0)
                    mix_t(0, 1)
                ssd_out(h)

            def out_proj(r, half):
                t, c = divmod(r, 2)
                for k in range(4 * half, 4 * half + 4):
                    await_unit(pe, U_OUT + k // 2)
                    w = front_slot(U_OUT + k // 2)[:, (k % 2) * 1024 + c * 512:(k % 2) * 1024 + c * 512 + 512]
                    last = mm(op_bank(r), mixT[:, k, t * P:(t + 1) * P], w, start=(k == 0), stop=(k == KC - 1),
                              skip_group_check=True)
                last.then_inc(S["op_done"], 1)

            pe.wait_ge(S["misc_read"], M_MIXT[1] + 1)
            pe.wait_ge(S["arg_ready"], 2 * SH)
            for r in range(4):
                if r == 3:
                    pe.wait_ge(S["row2_ready"], 2)
                out_proj(r, 0)
            for i in range(4, 8):
                mod_row(i)
            mix_t(1, 0)
            mix_t(1, 1)
            pe.wait_ge(S["misc_read"], M_MIXT[3] + 1)
            for r in range(4):
                out_proj(r, 1)

            for t in range(2):
                for half in range(2):
                    b = misc_begin(M_H2T + 2 * t + half)
                    pe.wait_ge(S["h2_ready"], t + 1)
                    for q in range(4):
                        k = 4 * half + q
                        last = nc.tensor.transpose(b[:, q * P:(q + 1) * P], h2[:, t, k * P:(k + 1) * P], ident)
                    last.then_inc(S["misc_filled"], 1)
                pe.wait_ge(S["misc_read"], M_H2T + 2 * t + 2)
                for k in range(KC):
                    last = mm(bank[5][:, t * NE:(t + 1) * NE], h2T[:, k, t * P:(t + 1) * P], wr[:, k, :],
                              start=(k == 0), stop=(k == KC - 1))
                last.then_inc(S["log_done"], 1)
            b = bank[6]
            pe.wait_ge(S["sel_made"], 1)
            sel = rt[0]
            mm(b[:, 0:NE], s_upper, sel[:, 0, :], start=True, stop=True)
            mm(b[:, NE:2 * NE], s_upper, sel[:, 1, :], start=True, stop=False)
            mm(b[:, NE:2 * NE], ones, sel[:, 0, :], start=False, stop=True)
            mm(b[:, 2 * NE:3 * NE], ones, sel[:, 0, :], start=True, stop=False)
            mm(b[:, 2 * NE:3 * NE], ones, sel[:, 1, :], start=False, stop=True).then_inc(S["rank_done"], 1)

            def acc(t, half):
                return bank[4 + 2 * t + half]

            def gather(j):
                pe.wait_ge(S["s_ready"], j + 1)
                for k in range(KC):
                    for t in range(2):
                        last = mm(bank[3][:, k * SLOTS:(k + 1) * SLOTS], h2[:, t, k * P:(k + 1) * P], S_j[:, t, :],
                                  start=(t == 0), stop=(t == 1))
                last.then_inc(S["gather_done"], 1)

            gather(0)
            pe.wait_ge(S["late_in"], 80)

            def scatter(jobs, first=False, final=False):
                pe.wait_ge(S["y_ready"], jobs + 1)
                pe.wait_ge(S["sgt_ready"], jobs + 1)
                for t in range(2):
                    for half in range(2):
                        rows = slice(64 * half, 64 * half + 64)
                        last = mm(acc(t, half), SGT[rows, t, :], ysb[rows, :], start=first, stop=final,
                                  skip_group_check=True)
                return last

            def job(j, first=False):
                pe.wait_ge(S["sel_ready"], j + 1)
                for b, col in ((bank[0], 0), (bank[1], FF)):
                    for half in range(2):
                        mm(b[64 * half:64 * half + 64, :], job_sel, brows[:, col + 512 * half:col + 512 * half + 512],
                           start=True, stop=False)
                pe.wait_ge(S["xg_ready"], j + 1)
                e = 0 if first else pe.value_load(int_e(j), min_val=0, max_val=NE - 1)
                for k in range(KC):
                    pe.wait_ge(loaded[k], 16 * (e + 1 + N_FRONT // FSLOT))
                    w = slot(k)
                    for b, col in ((bank[0], 0), (bank[1], FF)):
                        for half in range(2):
                            last = mm(b[64 * half:64 * half + 64, :], xg[:, k, :],
                                      w[:, col + 512 * half:col + 512 * half + 512], start=False, stop=(k == KC - 1))
                    last.then_inc(S["moe_used"], 1)
                scatter(j, first).then_inc(S["scat_done"], 1)
                pe.wait_ge(S["sg_ready"], j + 1)
                for t in range(2):
                    last = nc.tensor.transpose(bank[2][:, t * P:(t + 1) * P], SG_j[:, t, :], ident)
                last.then_inc(S["sgt_done"], 1)
                pe.wait_ge(S["act_ready"], j + 1)
                for q in range(4):
                    last = nc.tensor.transpose(bank[0][:, q * P:(q + 1) * P], act[:, q * P:(q + 1) * P], ident)
                last.then_inc(S["actT_done"], 1)
                gather(j + 1)
                pe.wait_ge(S["sgt_ready"], j + 2)
                for half in range(2):
                    last = mm(bank[2][64 * half:64 * half + 64, :], job_sel,
                              brows[:, 2 * FF + 512 * half:2 * FF + 512 * half + 512], start=True, stop=False)
                last.then_inc(S["sel_used"], 1)
                pe.wait_ge(S["actT_ready"], j + 1)
                for c in range(KC):
                    s = KC + c // 2
                    if c % 2 == 0:
                        front = N_FRONT // FSLOT if s < FSLOT else 0
                        pe.wait_ge(loaded[s], 16 * (e + 1 + front))
                    hh, q = divmod(c, 4)
                    for half in range(2):
                        last = mm(bank[2][64 * half:64 * half + 64, :], actT[:, q, 64 * hh:64 * hh + 64],
                                  slot(s)[:, (c % 2) * 1024 + 512 * half:(c % 2) * 1024 + 512 * half + 512],
                                  start=False, stop=(c == KC - 1))
                    if c % 2 == 1:
                        last.then_inc(S["moe_used"], 1)

            job(0, first=True)
            pe.wait_ge(S["job_tables"], 1)
            with pe.Fori(1, NE) as j:
                job(j)
            last = pe.value_load(int_last(NE - 1), min_val=NE - 1, max_val=NJ - 1)
            with pe.Fori(NE, NE + FEW) as j:
                with pe.If(last > j - 1):
                    job(j)
            with pe.If(last > NE + FEW - 1):
                with pe.Fori(NE + FEW, NJ) as j:
                    with pe.If(last > j - 1):
                        job(j)
            scatter(last + 1, final=True).then_inc(S["moe_done"], 1)

        @block.vector
        def _(v):
            V = nc.vector
            step = Steps(v, S["dve"])
            TT, TS, STT = V.tensor_tensor, V.tensor_scalar, V.scalar_tensor_tensor

            def misc_wait(i):
                v.wait_ge(S["misc_filled"], i + 1)
                return MISC[i % 2]

            def misc_read(ins):
                ins.then_inc(S["misc_read"], 1)

            v.wait_ge(S["sq_summed"], KC)
            step(TS(rstd1, bank[1], 1.0 / D, EPS, ALU.mult, ALU.add))
            step.settle()
            V.reciprocal(rstd1, rstd1).then_inc(S["rinv_ready"], 1)
            v.wait_ge(S["rstd_ready"], 1)
            TT(hT, hT, bc(rstd1.rearrange("p (a t) -> p a t", a=1), [P, KC, T + TX]), ALU.mult).then_inc(S["xh_ready"], 1)
            v.wait_ge(S["mod1_used"], KC)
            V.tensor_copy(modrow1, bank[0]).then_inc(S["row1_ready"], 1)
            b = misc_wait(M_MODT).rearrange("p (q g c) -> p g q c", q=4, g=4)
            v.wait_ge(S["norm_in"], 32)
            bm = bmodT.rearrange("p (g q) -> p g q", g=4)
            mc = modc.rearrange("p (g q) c -> p g q c", g=4)
            step(TT(mc[:, :, :, 0], b[:, :, :, 0], bm, ALU.add))
            misc_read(TT(mc[:, :, :, 1], b[:, :, :, 1], bm, ALU.add))
            v.wait_ge(S["misc_read"], 1)
            step.settle()
            step(TS(modc[:, 8:16, :], modc[:, 8:16, :], 1.0, None, ALU.add))
            step.settle()
            v.wait_ge(S["xh_ready"], 1)
            TT(modc[:, 8:16, :], modc[:, 8:16, :], bc(n1T.rearrange("p (k c) -> p k c", c=1), [P, KC, 2]), ALU.mult
               ).then_inc(S["modc_ready"], 1)
            v.wait_ge(S["modc_ready"], 1)
            for k in range(KC):
                x = hT[:, k, 0:T]
                TS(x, x, modc[:, 8 + k, 0:1], modc[:, k, 0:1], ALU.mult, ALU.add).then_inc(S["hl_ready"], 1)
            step(V.memset(pre[:, :, :, 0:1], 0.0))

            def conv_chunk(m):
                v.wait_ge(S["fm_evac"], m + 2)
                if m == 0:
                    v.wait_ge(S["small_in"], 16 * N_SMALL)
                x, y = xbc[:, m, :], conv[:, m, :]
                n = T + TX if m < 6 else T
                step(TS(y[:, 0:n], x[:, 0:n], convw[:, m, 4:5], convb[:, m:m + 1], ALU.mult, ALU.add))
                x3 = x[:, 0:T].rearrange("p (r c) -> p r c", r=ROWS)
                y3 = y[:, 0:T].rearrange("p (r c) -> p r c", r=ROWS)
                for tap in (0, 1, 2, 3, 5, 6, 7, 8):
                    dy, dx = tap // 3 - 1, tap % 3 - 1
                    r0, r1 = max(0, -dy), ROWS - max(0, dy)
                    c0, c1 = max(0, -dx), GRID - max(0, dx)
                    yo = y3[:, r0:r1, c0:c1]
                    xi = x3[:, r0 + dy:r1 + dy, c0 + dx:c1 + dx]
                    step.settle()
                    ins = STT(out=yo, in0=xi, scalar=convw[:, m, tap:tap + 1], in1=yo, op0=ALU.mult, op1=ALU.add)
                    if tap == 8:
                        ins.then_inc(S["conv_ready"], 1)
                    else:
                        step(ins)
                    if dy == 0 and m < 6:
                        yo = y[:, T + c0:T + TX - max(0, dx)]
                        xi = x[:, T + c0 + dx:T + TX - max(0, dx) + dx]
                        step(STT(out=yo, in0=xi, scalar=convw[:, m, tap:tap + 1], in1=yo, op0=ALU.mult, op1=ALU.add))

            conv_chunk(0)
            for n in range(4):
                v.wait_ge(S["gate_done"], n + 1)
                step(TS(ld[:, n, :], bank[5 + n % 2], bgk[:, n:n + 1], 0.0, ALU.add, ALU.min))
                TS(soft[:, n, :], bank[5 + n % 2], bgk[:, n:n + 1], 0.0, ALU.add, ALU.max).then_inc(S["gate_read"], 1)
            v.wait_ge(S["gate_read"], 4)
            step.settle()
            TT(soft, ld, soft, ALU.subtract).then_inc(S["soft_arg"], 1)
            conv_chunk(1)
            v.wait_ge(S["soft_ready"], 1)
            step.settle()
            step(TT(ld, ld, soft, ALU.subtract))
            step.settle()
            for n in range(4):
                for s in range(2):
                    step(V.tensor_tensor_scan(pre[:, n, s, 1:T + 1], bc(ones[:, 0:1], [P, T]),
                                              ld[:, n, s * T:(s + 1) * T], 0.0, ALU.mult, ALU.add))
            step.settle()
            for n in range(4):
                s = 1 if n % 2 == 0 else 0
                step(TS(stat[:, 16 + n:17 + n], pre[:, n, s, T:T + 1], 1.0 / GATE_NORM, None, ALU.mult))
            for m in range(2, 8):
                conv_chunk(m)

            v.wait_ge(S["tm_evac"], 1)
            for d in range(2):
                step(TT(dta[:, :, d, :], dtr, bc(dtb3[:, d:d + 1, :], [P, 4, SH]), ALU.add))
            step.settle()
            step(TS(dtt, dta, 0.0, None, ALU.min))
            step.settle()
            step(TS(dta, dta, 0.0, None, ALU.max))
            step.settle()
            TT(dtt, dtt, dta, ALU.subtract).then_inc(S["dt_ready"], 1)

            def args(n):
                d, b = n % 2, n % 2
                off = 1 if d == 0 else 0
                src = pre[:, n, 0, off:off + T]
                lim = CLAMP * GATE_NORM
                clip = (-lim, ALU.max) if d == 0 else (lim, ALU.min)
                if n >= 2:
                    v.wait_ge(S["score_done"], 2 * (n - 1))
                for blk in range(NB):
                    near = (blk < NPT) == (d == 0)
                    i4 = blk % NPT
                    ref = pre[:, n, 0, blk * BLK + BLK // 2:blk * BLK + BLK // 2 + 1]
                    if near:
                        dst = kv[n][:, i4 * P:(i4 + 1) * P]
                        s = src[:, 0:P] if d == 0 else src[:, P:2 * P]
                    else:
                        dst = kv[n][:, KNEAR + i4 * T:KNEAR + (i4 + 1) * T]
                        s = src
                    step(TS(dst, s, ref, clip[0], ALU.subtract, clip[1]))
                    last = TS(qv[b][:, blk * BLK:(blk + 1) * BLK], src[:, blk * BLK:(blk + 1) * BLK], ref,
                              -clip[0], ALU.subtract, ALU.min if d == 0 else ALU.max)
                    if blk < NB - 1:
                        step(last)
                last.then_inc(S["kvarg_ready"], 1)

            def mults(n):
                c, d = divmod(n, 2)
                b = n % 2
                v.wait_ge(S["exp_ready"], 4 * (n + 1))
                kn = k_fm[:, c, 0:P] if d == 0 else k_fm[:, c, P:2 * P]
                near = kv[n][:, 0:KNEAR].rearrange("p (b j) -> p b j", b=NPT)
                far = kv[n][:, KNEAR:KV].rearrange("p (b j) -> p b j", b=NPT)
                step(TT(near, near, bc(kn.rearrange("p (a j) -> p a j", a=1), [P, NPT, P]), ALU.mult))
                step(TT(far, far, bc(k_fm[:, c, 0:T].rearrange("p (a j) -> p a j", a=1), [P, NPT, T]), ALU.mult))
                step(TT(qv[b], qv[b], q_fm[:, c, :], ALU.mult))
                step(TT(qd[n], qd[n], q_fm[:, c, :], ALU.mult))
                TT(kx[b], kx[b], k_fm[:, c, T:T + TX], ALU.mult).then_inc(S["kvmul_ready"], 1)

            def scores(n):
                c, d = divmod(n, 2)
                if n == 0:
                    v.wait_ge(S["kvarg_ready"], 1)
                if n >= 2:
                    v.wait_ge(S["o_done"], 1)
                for e in range(2):
                    v.wait_ge(S["score_done"], 2 * n + e + 1)
                    TT(pt[:, d, e, :], bank[e][:, 0:SPAN], mask[d], ALU.mult).then_inc(S["pt_ready"], 1)
                misc_read(V.tensor_copy(kxT, misc_wait(M_GLA + 2 * n)[:, 0:256]))
                misc_read(V.tensor_copy(gS[:, d, :], misc_wait(M_GLA + 2 * n + 1)[:, 0:DV]))

            args(0)
            v.wait_ge(S["negA_ready"], 1)
            v.wait_ge(S["dt_sp"], 1)
            step.settle()
            step(TT(dta, dta, dtt, ALU.add))
            step.settle()
            for d in range(2):
                step(TT(a_tm[:, :, d, :], dta[:, :, d, :], bc(negA3[:, d:d + 1, :], [P, 4, SH]), ALU.mult))
            step.settle()
            TS(a_tm, a_tm, -1.0, None, ALU.mult).then_inc(S["dt_exp"], 1)
            args(1)
            for g in range(SG):
                b = misc_wait(M_CB + g)
                step(TT(cbm[:, 0, g, 0:256], b[:, 0:256], mask[0][:, 0:256], ALU.mult))
                step(TT(cbm[:, 0, g, 256:384], b[:, 384:512], mask[0][:, 256:384], ALU.mult))
                step(TT(cbm[:, 1, g, 0:128], b[:, 0:128], mask[1][:, 0:128], ALU.mult))
                misc_read(TT(cbm[:, 1, g, 128:384], b[:, 256:512], mask[1][:, 128:384], ALU.mult))
            misc_read(V.tensor_copy(b_tm.rearrange("p t g s -> p (t g s)"), misc_wait(M_B)))
            misc_read(V.tensor_copy(acol.rearrange("p t d h -> p (t d h)"), misc_wait(M_ACOL)[:, 0:64]))
            mults(0)
            scores(0)
            args(2)
            mults(1)
            scores(1)
            args(3)
            mults(2)
            scores(2)
            mults(3)
            scores(3)

            v.wait_ge(S["tm_done"], len(TM))
            for i in range(2):
                misc_read(V.tensor_copy(xs_tm[:, X_ORDER[i], :], misc_wait(M_X + i)))
            v.wait_ge(S["misc_read"], M_X + 2)
            v.wait_ge(S["eac_ready"], 1)
            step(TT(dta[:, 2:4], dta[:, 2:4], eac[:, 2:4], ALU.mult))
            step.settle()
            hp = lambda ap: ap.rearrange("p (h q) -> p h q", h=SH)
            for d in range(2):
                for t in range(2):
                    last = TT(hp(xw[:, t, d, :]), hp(xs_tm[:, 2 + t, :]),
                              bc(dta[:, 2 + t, d, :].rearrange("p (h q) -> p h q", q=1), [P, SH, HP]), ALU.mult)
                    if t == 0:
                        step(last)
                last.then_inc(S["xw_ready"], 1)
            for i in range(2, 4):
                misc_read(V.tensor_copy(xs_tm[:, X_ORDER[i], :], misc_wait(M_X + i)))
            v.wait_ge(S["misc_read"], M_X + 4)
            v.wait_ge(S["gla_sq"], 1)
            step(TS(stat[:, 0:8], stat[:, 0:8], 1.0 / DV, EPS, ALU.mult, ALU.add))
            step.settle()
            V.reciprocal(stat[:, 0:8], stat[:, 0:8]).then_inc(S["gst"], 1)
            for d in range(2):
                for t in range(2):
                    step(TT(hp(xdt[:, t, d, :]), hp(xs_tm[:, t, :]),
                            bc(dta[:, t, d, :].rearrange("p (h q) -> p h q", q=1), [P, SH, HP]), ALU.mult))
            ya = y_acc.rearrange("p (t c) -> p t c", t=2)
            for t in range(2):
                step(TT(hp(ya[:, t, :]), hp(xs_tm[:, t, :]),
                        bc(d_row.rearrange("p (h q) -> p h q", q=1), [P, SH, HP]), ALU.mult))
            for d in range(2):
                misc_read(V.tensor_copy(sS[:, d, :], misc_wait(M_ST + d)))
            v.wait_ge(S["xw_ready"], 2)
            ytmp = hA[:, 0:512]
            for t in range(2):
                for d in range(2):
                    b = misc_wait(M_YOFF + 2 * t + d)
                    v.wait_ge(S["misc_read"], M_YOFF + 2 * t + d)
                    step.settle()
                    misc_read(TT(hp(ytmp), hp(b), bc(eac[:, t, d, :].rearrange("p (h q) -> p h q", q=1), [P, SH, HP]),
                                 ALU.mult))
                    v.wait_ge(S["misc_read"], M_YOFF + 2 * t + d + 1)
                    step(TT(ya[:, t, :], ya[:, t, :], ytmp, ALU.add))
            step.settle()

            def seg_arg(i):
                h, d = divmod(i, 2)
                s = seg[i % 4]
                b = rb_bank(i)
                v.wait_ge(S["rb_done"], i + 1)
                if i >= 4:
                    v.wait_ge(S["ydiag_done"], (i - 4) // 2 + 1)
                spans = [(0, 0, 256, 0), (256, 128, 256, 1)] if d == 0 else [(0, 0, 128, 0), (128, 0, 256, 1)]
                for x, (to, c0, c1, jt) in enumerate(spans):
                    ins = TS(s[:, to:to + c1 - c0], b[:, c0:c1], acol[:, jt, d, h:h + 1], 0.0, ALU.subtract, ALU.min)
                    if x == 0:
                        step(ins)
                        step.settle()
                    else:
                        ins.then_inc(S["arg_ready"], 1)

            def seg_mult(i):
                h, d = divmod(i, 2)
                v.wait_ge(S["segexp_ready"], i + 1)
                TT(seg[i % 4], seg[i % 4], cbm[:, d, h // HPG, :], ALU.mult).then_inc(S["segm_ready"], 1)

            v.wait_ge(S["o_done"], 2)
            seg_arg(0)
            for i in range(2 * SH):
                if i + 1 < 2 * SH:
                    seg_arg(i + 1)
                seg_mult(i)
                if i == 4:
                    v.wait_ge(S["gsq"], 1)
                    v.wait_ge(S["silu_ready"], 1)
                    for a in range(8):
                        o = o_sb[:, a * DV:(a + 1) * DV]
                        step(STT(out=o, in0=o, scalar=stat[:, a:a + 1], in1=gnrow, op0=ALU.mult, op1=ALU.mult))
                if i == 6:
                    step.settle()
                    gv = vgz[:, :, 512:1024]
                    TT(gv, gv, o_sb.rearrange("p (t c) -> p t c", t=2), ALU.mult).then_inc(S["mix_ready"], 1)
                if i == 7:
                    v.wait_ge(S["mr"], 64)
                    v.wait_ge(S["mod2_used"], KC)
                    TT(modrow[:, 0, :], bank[0], modrow[:, 0, :], ALU.add).then_inc(S["row2_ready"], 1)
            v.wait_ge(S["segm_ready"], 2 * SH)
            v.wait_ge(S["mod2_used"], 2 * KC)
            TT(modrow[:, 1, :], bank[0], modrow[:, 1, :], ALU.add).then_inc(S["row2_ready"], 1)

            v.wait_ge(S["ydiag_done"], SH)
            for t in range(2):
                step(TT(ya[:, t, :], ya[:, t, :], bank[5 + t], ALU.add))
            step.settle()
            for t in range(2):
                TT(ya[:, t, :], ya[:, t, :], vgz[:, t, 1024:1536], ALU.mult).then_inc(S["yz_ready"], 1)
            v.wait_ge(S["ssd_sq"], 1)
            step(TS(stat[:, 8:12], stat[:, 8:12], SG / SI, EPS, ALU.mult, ALU.add))
            step.settle()
            V.reciprocal(stat[:, 8:12], stat[:, 8:12]).then_inc(S["sst"], 1)
            v.wait_ge(S["ssq"], 1)
            v.wait_ge(S["sn_in"], 16)
            for t in range(2):
                for g in range(SG):
                    c = slice(256 * g, 256 * (g + 1))
                    last = STT(out=vgz[:, t, 1024 + 256 * g:1024 + 256 * (g + 1)], in0=ya[:, t, c],
                               scalar=stat[:, 8 + 2 * t + g:9 + 2 * t + g], in1=snrow[:, c], op0=ALU.mult, op1=ALU.mult)
            last.then_inc(S["mix_ready"], 1)
            v.wait_ge(S["late_in"], 80)
            v.wait_ge(S["misc_read"], M_ROWS[5] + 1)
            step(TT(w2b, w2b, n2row, ALU.mult))
            step(V.memset(RT, -1.0))
            step(V.memset(GT, 0.0))
            for t in range(2):
                for half in range(2):
                    r = 2 * t + half
                    v.wait_ge(S["op_done"], 5 + r)
                    cols = slice(512 * half, 512 * half + 512)
                    tm_ = fB[:, 3072 + 512 * half:3584 + 512 * half] if t else fB[:, cols]
                    TT(tm_, op_bank(r), g1b[:, cols], ALU.mult).then_inc(S["op_read"], 1)
                    v.wait_ge(S["op_read"], r + 1)
                    TT(x_tm[:, t, cols], x_tm[:, t, cols], tm_, ALU.add).then_inc(S["xnew_ready"], 1)
                v.wait_ge(S["nsq"], 2 * t + 1)
                st = stat[:, 22 + t:23 + t]
                step(TS(st, stat[:, 20 + t:21 + t], 1.0 / D, EPS, ALU.mult, ALU.add))
                step.settle()
                V.reciprocal(st, st).then_inc(S["nst"], 1)
                v.wait_ge(S["nsq"], 2 * t + 2)
                step(STT(out=h2[:, t, :], in0=x_tm[:, t, :], scalar=st, in1=w2b, op0=ALU.mult, op1=ALU.mult))
                step.settle()
                TT(h2[:, t, :], h2[:, t, :], sh2b, ALU.add).then_inc(S["h2_ready"], 1)
                if t == 0:
                    v.wait_ge(S["misc_read"], M_ROWS[7] + 1)
                    V.memset(ysb, 0.0).then_inc(S["y_ready"], 1)
            v.wait_ge(S["log_done"], 2)
            b = bank[5][:, 0:2 * NE].rearrange("p (t e) -> p t e", t=2)
            step(TT(lg, b, bc(brrow.rearrange("p (a e) -> p a e", a=1), [P, 2, NE]), ALU.add))
            step.settle()
            for t in range(2):
                step(V.max(top8[:, t, :], lg[:, t, :]))
            step.settle()
            sel, eq, ce, ex = rt
            for t in range(2):
                m4 = top8[:, t, 3:4]
                step(TS(sel[:, t, :], lg[:, t, :], m4, None, ALU.is_gt))
                step(TS(eq[:, t, :], lg[:, t, :], m4, None, ALU.is_equal))
            step.settle()
            for t in range(2):
                last = TS(ex[:, t, :], lg[:, t, :], top8[:, t, 0:1], None, ALU.subtract)
                if t == 0:
                    step(last)
            last.then_inc(S["ex_ready"], 1)
            for t in range(2):
                step(V.tensor_tensor_scan(ce[:, t, :], bc(ones[:, 0:1], [P, NE]), eq[:, t, :], 0.0, ALU.mult, ALU.add))
            step(V.tensor_reduce(stat[:, 28:30], sel, AX.X, ALU.add))
            step.settle()
            for t in range(2):
                step(TS(ce[:, t, :], ce[:, t, :], stat[:, 28 + t:29 + t], 4.5, ALU.add, ALU.is_lt))
            step.settle()
            step(TT(eq, eq, ce, ALU.mult))
            step.settle()
            TT(sel, sel, eq, ALU.add).then_inc(S["sel_made"], 1)
            v.wait_ge(S["sel_made"], 1)
            v.wait_ge(S["ex_done"], 1)
            step(TT(ex, ex, sel, ALU.mult))
            step.settle()
            step(V.tensor_reduce(stat[:, 28:30], ex, AX.X, ALU.add))
            step.settle()
            step(V.reciprocal(stat[:, 28:30], stat[:, 28:30]))
            step.settle()
            for t in range(2):
                step(TS(GT[:, t, 0:NE], ex[:, t, :], stat[:, 28 + t:29 + t], None, ALU.mult))
            v.wait_ge(S["rank_done"], 1)
            b = bank[6][:, 0:3 * NE].rearrange("p (i e) -> p i e", i=3)
            step(V.tensor_copy(cnt, b))
            step.settle()
            step(STT(out=eq, in0=cnt[:, 0:2, :], scalar=1.0, in1=sel, op0=ALU.add, op1=ALU.mult))
            step.settle()
            step(TS(RT[:, :, 0:NE], eq, -1.0, None, ALU.add))
            step.settle()


            def select_tokens(slots, own):
                for t in range(2):
                    last = TS(S_j[:, t, :], slots, own[:, t, :], None, ALU.is_equal)
                last.then_inc(S["s_ready"], 1)

            def select_gates(slots2, own, gate):
                for t in range(2):
                    last = TS(SG_j[:, t, :], slots2, own[:, t, :], gate[:, t, :], ALU.is_equal, ALU.mult)
                last.then_inc(S["sg_ready"], 1)

            def select_expert(j):
                TS(job_sel, part_no[0:NE, :], JE[0:NE, bass.ds(j, 1)], None, ALU.is_equal).then_inc(S["sel_ready"], 1)

            def xg_copy(j):
                v.wait_ge(S["gather_done"], j + 1)
                V.tensor_copy(xg.rearrange("p k s -> p (k s)"), bank[3]).then_inc(S["xg_ready"], 1)

            def job(j):
                v.wait_ge(S["gather_done"], j + 1)
                e = v.value_load(int_e(j + 1), min_val=0, max_val=NE)
                q = v.value_load(int_q(j + 1), min_val=0, max_val=T // SLOTS - 1)
                select_tokens(slot_q[:, bass.ds(q * (2 * SLOTS), SLOTS)], RT[:, :, bass.ds(e, 1)])
                v.wait_ge(S["moe_used"], NSLOT * j + KC)
                TS(gm, bank[0], LIMIT, None, ALU.min).then_inc(S["gm_ready"], 1)
                TS(act, bank[1], LIMIT, -LIMIT, ALU.min, ALU.max).then_inc(S["up_read"], 1)
                v.wait_ge(S["up_read"], 2 * j + 1)
                v.wait_ge(S["gm_ready"], j + 1)
                STT(out=act, in0=act, scalar=1.0, in1=gm, op0=ALU.add, op1=ALU.mult).then_inc(S["up_read"], 1)
                v.wait_ge(S["up_read"], 2 * j + 2)
                v.wait_ge(S["sig_ready"], j + 1)
                TT(act, act, sig, ALU.mult).then_inc(S["act_ready"], 1)
                v.wait_ge(S["sgt_done"], j + 1)
                v.wait_ge(S["scat_done"], j + 1)
                V.tensor_copy(SGT, bank[2][:, 0:256].rearrange("p (t c) -> p t c", t=2)).then_inc(S["sgt_ready"], 1)
                v.wait_ge(S["actT_done"], j + 1)
                V.tensor_copy(actT, bank[0].rearrange("p (q c) -> p q c", q=4)).then_inc(S["actT_ready"], 1)
                xg_copy(j + 1)
                select_gates(slot_q[:, bass.ds(q * (2 * SLOTS), 2 * SLOTS)], RT[:, :, bass.ds(e, 1)], GT[:, :, bass.ds(e, 1)])
                v.wait_ge(S["sel_used"], j + 1)
                select_expert(j + 1)
                v.wait_ge(S["moe_used"], NSLOT * (j + 1))
                V.tensor_copy(ysb, bank[2]).then_inc(S["y_ready"], 1)

            select_tokens(slot_no[:, 0:SLOTS], RT[:, :, 0:1])
            TS(job_sel, part_no[0:NE, :], 0.0, None, ALU.is_equal).then_inc(S["sel_ready"], 1)
            select_gates(slot_no, RT[:, :, 0:1], GT[:, :, 0:1])
            V.memset(SGT, 0.0).then_inc(S["sgt_ready"], 1)
            xg_copy(0)
            v.wait_ge(S["slots_ready"], 2)
            job_tables(nc, v, S, step, cnt[:, 2, :], cnt[:, 0, :], cnt[:, 1, :], job_no, jobs_w, JE, JQ, ints, ones)
            v.wait_ge(S["job_tables"], 1)
            job(0)
            with v.Fori(1, NE) as j:
                job(j)
            last = v.value_load(int_last(NE - 1), min_val=NE - 1, max_val=NJ - 1)
            with v.Fori(NE, NE + FEW) as j:
                with v.If(last > j - 1):
                    job(j)
            with v.If(last > NE + FEW - 1):
                with v.Fori(NE + FEW, NJ) as j:
                    with v.If(last > j - 1):
                        job(j)
            v.wait_ge(S["moe_done"], 1)
            for t in range(NT):
                for half in range(2):
                    cols = slice(512 * half, 512 * half + 512)
                    b = bank[4 + 2 * t + half]
                    step(TT(fB[:, 1024 * t + 512 * half:1024 * t + 512 * half + 512], b, g2b[:, cols], ALU.mult))
                step.settle()
                TT(x_tm[:, t, :], x_tm[:, t, :], fB[:, 1024 * t:1024 * (t + 1)], ALU.add).then_inc(S["fsq"], 1)
            for t in range(NT):
                v.wait_ge(S["fst"], t + 1)
                st = stat[:, 26 + t:27 + t]
                step(TS(st, stat[:, 24 + t:25 + t], 1.0 / D, EPS, ALU.mult, ALU.add))
                step.settle()
                V.reciprocal(st, st).then_inc(S["fsq"], 1)
            for t in range(NT):
                v.wait_ge(S["fst"], NT + t + 1)
                STT(out=x_tm[:, t, :], in0=x_tm[:, t, :], scalar=stat[:, 26 + t:27 + t], in1=fnrow, op0=ALU.mult,
                    op1=ALU.mult).then_inc(S["out_ready"], 1)


def kernel(**inputs):
    import numpy as np
    import concourse.bacc as bacc
    from concourse.bass_utils import run_bass_kernel_spmd

    g = {k: np.asarray(v) for k, v in inputs.items()}
    w_in = g["w_in"][0]
    off = np.cumsum([0, 256, 256, 512, 512, RANK, 512, 1024, SH])
    q, k, v, gg, gk, z, xbc, dt = (w_in[:, off[i]:off[i + 1]] for i in range(8))
    units = np.concatenate([xbc, k, q, v, gg, z], axis=1)
    arr = {
        "x": g["x"][0],
        "xT": g["x"][0].T.reshape(KC, P, T),
        "ctxT": g["ctx"][0].T.reshape(KC, P, TX),
        "c2": np.stack([g["c"][0], g["c_ctx"]], axis=1).reshape(KC, P, 2),
        "w_mod": g["w_mod"][0],
        "bmodT": g["b_mod"][0][:2048].reshape(16, P).T,
        "b_mod2": g["b_mod"][0][2048:].reshape(2, 4, 512),
        "n1T": g["norm1"][0].reshape(KC, P).T,
        "w_in": units.reshape(KC, P, N_IN, 256).transpose(2, 1, 0, 3).reshape(N_IN, P, UNIT),
        "wgk": gk.reshape(KC, P, RANK),
        "wdt": dt.reshape(KC, P, SH),
        "wup": g["gla_w_gk_up"][0].transpose(1, 0, 2),
        "bgk": g["gla_b_gk"][0].reshape(2, 2, P).transpose(2, 1, 0).reshape(P, 4),
        "convw": g["ssd_conv_w"][0].reshape(9, 8, P).transpose(2, 1, 0),
        "convb": g["ssd_conv_b"][0].reshape(8, P).T,
        "gla_norm": g["gla_norm"][0],
        "ssd_norm": g["ssd_norm"][0],
        "ssd_D": g["ssd_D"][0],
        "dtb": g["ssd_dt_bias"][0].reshape(16),
        "alog": g["ssd_A_log"][0].reshape(16),
        "w_out": g["w_out"][0],
        "norm2": g["norm2"][0],
        "final_norm": g["final_norm"],
        "w_router": g["w_router"][0],
        "b_router": g["b_router"][0],
        "w_gate_up": g["w_gate_up"][0],
        "w_down": g["w_down"][0],
        "b_moe": np.concatenate([g["b_gate_up"][0], g["b_down"][0]], axis=1),
    }
    nc = bacc.Bacc("TRN2", target_bir_lowering=False, num_devices=1)
    arrays, A = {}, {}
    for name, a in arr.items():
        a = np.ascontiguousarray(a)
        arrays[f"in_{name}"] = a
        A[name] = nc.dram_tensor(f"in_{name}", a.shape, mybir.dt.from_np(a.dtype), kind="ExternalInput").ap()
    out = nc.dram_tensor("out_0", (1, T, D), F32, kind="ExternalOutput").ap()
    layer_kernel(nc, A, out)
    return run_bass_kernel_spmd(nc, [arrays], core_ids=[0]).results[0]["out_0"]
```

```python
from contextlib import ExitStack

import concourse.bass as bass
from concourse import mybir

F32 = mybir.dt.float32
I32 = mybir.dt.int32
BF16 = mybir.dt.bfloat16
ALU = mybir.AluOpType
ACT = mybir.ActivationFunctionType
AX = mybir.AxisListType

P = 128
D = 1024
KC = D // P
T = 256
TX = 256
NT = T // P
EPS = 1e-6
GH, DK, DV = 4, 64, 128
RANK = 16
GATE_NORM = 16.0
BLK = 64
NB = T // BLK
NPT = P // BLK
KNEAR, KV = NPT * P, NPT * (P + T)
CLAMP = 40.0
SH, HP, SG, NS = 8, 64, 2, 128
HPG = SH // SG
SI = SH * HP
GRID = 64
ROWS = T // GRID
NE = 32
FF = 1024
SLOTS = 64
NJ = NE + 15
FEW = 4
LIMIT, ALPHA = 7.0, 1.702
PARTS = 3
UNIT = 2048
N_SMALL = 9
NSLOT = 12
FSLOT = 10
N_MOD1, N_IN, N_MOD2, N_OUT = 8, 12, 16, 4
N_FRONT = N_MOD1 + N_IN + N_MOD2 + N_OUT
SPAN = 384


def bc(ap, shape):
    return ap.to_broadcast(shape)


def last_jobs(nc, S, step, total, nblk, incl, last, ones):
    V = nc.vector
    TS, STT = V.tensor_scalar, V.scalar_tensor_tensor
    step(TS(nblk, total, SLOTS + 0.5, 1.0, ALU.is_gt, ALU.add))
    for b in range(2, T // SLOTS):
        step.settle()
        step(STT(out=nblk, in0=total, scalar=b * SLOTS + 0.5, in1=nblk, op0=ALU.is_gt, op1=ALU.add))
    step.settle()
    step(V.tensor_tensor_scan(incl, bc(ones[:, 0:1], [P, NE]), nblk, 0.0, ALU.mult, ALU.add))
    step.settle()
    TS(last, incl, -1.0, None, ALU.add).then_inc(S["last_jobs"], 1)


def job_tables(nc, S, step, nblk, incl, job_no, w, JE, JQ, ints):
    V = nc.vector
    TT, TS = V.tensor_tensor, V.tensor_scalar
    n = NJ + 1
    row = lambda ap: bc(ap.rearrange("p (a e) -> p a e", a=1), [P, n, NE])
    step(TT(w, row(incl), bc(job_no[:, 0:n].rearrange("p (i a) -> p i a", a=1), [P, n, NE]), ALU.is_le))
    step.settle()
    step(V.tensor_reduce(JE, w, AX.X, ALU.add))
    step.settle()
    step(TT(w, w, row(nblk), ALU.mult))
    step.settle()
    step(V.tensor_reduce(JQ, w, AX.X, ALU.add))
    step.settle()
    step(TT(JQ, job_no[:, 0:n], JQ, ALU.subtract))
    step.settle()
    step(TS(JQ, JQ, float(T // SLOTS - 1), None, ALU.min))
    step.settle()
    step(V.tensor_copy(ints[:, 0:n], JE))
    step.settle()
    V.tensor_copy(ints[:, n:2 * n], JQ).then_inc(S["job_tables"], 1)


def layer_kernel(nc, A, out):
    with ExitStack() as ctx:
        def sb(name, cols, parts=P, dt=F32):
            return ctx.enter_context(nc.sbuf_tensor(name, [parts, cols], dt))[:]

        def sem(name):
            return ctx.enter_context(nc.semaphore(name))

        ring = sb("ring", NSLOT * UNIT)
        bank = [ctx.enter_context(nc.psum_tensor(f"bank{i}", [P, 512], F32))[:] for i in range(8)]

        def slot(i):
            return ring[:, i * UNIT:(i + 1) * UNIT]

        conv = ring[:, FSLOT * UNIT:].rearrange("p (m t) -> p m t", m=8)
        o_sb = ring[:, FSLOT * UNIT:FSLOT * UNIT + 1024]
        y_acc = ring[:, FSLOT * UNIT + 1024:FSLOT * UNIT + 2048]

        hA = sb("hA", 4096)
        hT = hA.rearrange("p (k t) -> p k t", k=KC)
        xs_tm = hA[:, 0:2048].rearrange("p (t c) -> p t c", t=4)
        xdt = hA[:, 2048:4096].rearrange("p (t d c) -> p t d c", t=2, d=2)
        brows = hA[0:PARTS * NE, 0:2 * FF + D]
        gu_bias = hA[0:PARTS * NE, 3072:4096].bitcast(BF16)

        cB = sb("cB", 4096)
        xbc = cB.rearrange("p (m t) -> p m t", m=8)
        xw = cB[:, 0:2048].rearrange("p (t d c) -> p t d c", t=2, d=2)
        cbm = cB[:, 2048:2048 + 4 * SPAN].rearrange("p (d g c) -> p d g c", d=2, g=2)
        b_tm = cB[:, 3584:4096].rearrange("p (t g s) -> p t g s", t=2, g=2)
        mixT = cB[:, 0:2048].rearrange("p (k t) -> p k t", k=KC)
        h2 = cB[:, 2048:4096].rearrange("p (t c) -> p t c", t=NT)

        dB = sb("dB", 2048)
        k_fm = dB[:, 0:1024].rearrange("p (c t) -> p c t", c=2)
        q_fm = dB[:, 1024:1536].rearrange("p (c t) -> p c t", c=2)
        gk_fm = dB[0:RANK, 1536:2048]
        dt_fm = dB[64:64 + SH, 1536:2048]
        n2row = dB[:, 0:1024]
        fnrow = dB[:, 1024:2048]

        fB = sb("fB", 4096)
        vgz = fB[:, 0:3072].rearrange("p (t c) -> p t c", t=2)
        vx = fB[:, 3072:4096].rearrange("p (t c) -> p t c", t=2)
        h2T = fB[:, 0:2048].rearrange("p (k t) -> p k t", k=KC)

        gB = sb("gB", 4 * 2 * 257 + 2 * 1536)
        pre = gB[:, 0:2056].rearrange("p (n s t) -> p n s t", n=4, s=2)
        kv = [gB[:, 2056 + KV * i:2056 + KV * (i + 1)] for i in range(4)]
        soft = gB[:, 2056:2056 + 2048].rearrange("p (n t) -> p n t", n=4)
        sq = [gB[:, 512 * i:512 * (i + 1)] for i in range(KC)]
        rstd1 = gB[:, 4096:4608]
        sqout = gB[:, 4096:5120]
        g1b, sh2b, w2b, g2b = (gB[:, 1024 * i:1024 * (i + 1)] for i in range(4))

        pB = sb("pB", 2560)
        ld = pB[:, 0:2048].rearrange("p (n t) -> p n t", n=4)
        pt = pB[:, 0:4 * SPAN].rearrange("p (d e c) -> p d e c", d=2, e=2)
        seg = [pB[:, SPAN * i:SPAN * (i + 1)] for i in range(4)]
        x_tm = pB[:, 0:2048].rearrange("p (t c) -> p t c", t=2)
        down_bias = pB[0:PARTS * NE, 2048:2560].bitcast(BF16)

        qv = [sb(f"qv{i}", 256) for i in range(2)]
        kx = [sb(f"kx{i}", 256) for i in range(2)]
        qd_ = sb("qd", 512)
        qd = [qd_[:, 0:T], qd_[:, T:2 * T], dB[:, 1536:1536 + T], dB[:, 1536 + T:2048]]
        kxT = sb("kxT", 256)
        gS = sb("gS", 256).rearrange("p (d v) -> p d v", d=2)
        sS = sb("sS", 1024).rearrange("p (d c) -> p d c", d=2)
        mask = [sb(f"mask{d}", SPAN) for d in range(2)]
        upper, ones, lower = mask[0][:, 0:P], mask[0][:, P:2 * P], mask[1][:, 0:P]
        s_upper, s_lower, ident = sb("s_upper", P), sb("s_lower", P), sb("ident", P)
        slot_no = sb("slot_no", 2 * SLOTS)
        part_no = sb("part_no", SLOTS)
        cs = sb("cs", KC * 32).rearrange("p (k c) -> p k c", k=KC)
        c_in = sb("c_in", KC * 2).rearrange("p (k c) -> p k c", k=KC)
        modrow = sb("modrow", 1024).rearrange("p (r c) -> p r c", r=2)
        modrow1 = pB[:, 2048:2560]
        modc = sb("modc", 32).rearrange("p (g c) -> p g c", g=16)
        bmodT, n1T = sb("bmodT", 16), sb("n1T", KC)
        bgk = sb("bgk", 4)
        wup = dB[0:RANK, 1024:1536].rearrange("r (d c) -> r d c", d=2)
        wgk = pB[:, 0:KC * RANK].rearrange("p (k c) -> p k c", k=KC)
        wdt = cB[:, 4096 - KC * SH:].rearrange("p (k c) -> p k c", k=KC)
        convw = sb("convw", 72).rearrange("p (m j) -> p m j", m=8)
        convb = sb("convb", 8)
        gnrow, snrow = sb("gnrow", DV), pB[:, 2048:2560]
        d_row, dtb, negA = sb("d_row", SH), sb("dtb", 16), sb("negA", 16)
        dtb3, negA3 = (v.rearrange("p (d h) -> p d h", d=2) for v in (dtb, negA))
        dtr = sb("dtr", 4 * SH).rearrange("p (t h) -> p t h", t=4)
        dta = sb("dta", 64).rearrange("p (t d h) -> p t d h", t=4, d=2)
        dtt = sb("dtt", 64).rearrange("p (t d h) -> p t d h", t=4, d=2)
        a_tm = sb("a_tm", 64).rearrange("p (t d h) -> p t d h", t=4, d=2)
        acol = sb("acol", 64).rearrange("p (t d h) -> p t d h", t=4, d=2)
        eac = sb("eac", 64).rearrange("p (t d h) -> p t d h", t=4, d=2)
        stat = sb("stat", 32)
        wr = gS.rearrange("p d v -> p (d v)").rearrange("p (k e) -> p k e", k=KC)
        brrow = sb("brrow", NE)
        lg = fB[:, 3776:3840].rearrange("p (t e) -> p t e", t=2)
        top8 = fB[:, 3840:3856].rearrange("p (t e) -> p t e", t=2)
        rt = [kxT[:, 64 * i:64 * i + 64].rearrange("p (t e) -> p t e", t=2) for i in range(4)]
        RT, GT = (qv[1][:, P * i:P * i + 2 * (NE + 1)].rearrange("p (t j) -> p t j", t=2) for i in range(2))
        JE, JQ = kx[0][:, 0:NJ + 1], kx[0][:, P:P + NJ + 1]
        ints = sb("ints", 2 * (NJ + 1) + NE, dt=I32)
        int_e = lambda j: ints[0:1, bass.ds(j, 1)]
        int_q = lambda j: ints[0:1, bass.ds(j + NJ + 1, 1)]
        int_last = lambda e: ints[0:1, bass.ds(e + 2 * (NJ + 1), 1)]
        cnt = fB[:, 3856:3952].rearrange("p (i e) -> p i e", i=3)
        S_j = fB[:, 2048:2176].rearrange("p (t s) -> p t s", t=2)
        SG_j = fB[:, 2176:2432].rearrange("p (t s) -> p t s", t=2)
        SGT = fB[:, 2432:2688].rearrange("p (t c) -> p t c", t=2)
        xg = fB[:, 2688:3200].rearrange("p (k s) -> p k s", k=KC)
        gm = fB[:, 3200:3712]
        sig = sS.rearrange("p d c -> p (d c)")[:, 0:512]
        act = sS.rearrange("p d c -> p (d c)")[:, 512:1024]
        actT = modrow.rearrange("p r c -> p (r c)")[:, 0:512].rearrange("p (q c) -> p q c", q=4)
        ysb = modrow.rearrange("p r c -> p (r c)")[:, 512:1024]
        job_sel = fB[0:PARTS * NE, 3712:3744].bitcast(BF16)
        jobs_w = fB[:, 0:(NJ + 1) * NE].rearrange("p (i e) -> p i e", e=NE)
        slot_q = cB[:, 0:2 * T]
        job_no = cB[:, 2 * T:2 * T + NJ + 1]

        loaded = [sem(f"slot{i}_loaded") for i in range(NSLOT)]
        names = """ones_ready zeroed consts cT_in xT_in norm_in small_in sn_in mr late_in bias_in bias_split
        cs_ready sq_ready sq_summed rinv_ready rstd_ready xh_ready mod1_used row1_ready modc_ready hl_ready hx_ready
        fm_done fm_evac gate_done gate_read soft_arg soft_ready conv_ready conv_act
        dtT_ready tm_done tm_evac dt_ready dt_exp dt_sp negA_ready misc_filled misc_read
        kvarg_ready exp_ready kvmul_ready score_done pt_ready o_done o_copied
        mod2_scaled mod2_used modsum_ready
        eac_ready xw_ready rb_done arg_ready segexp_ready segm_ready ydiag_done
        silu_ready gla_sq gst gsq yz_ready ssd_sq sst ssq mix_ready
        op_done op_read xnew_ready nsq nst h2_ready log_done ex_ready ex_done sel_made rank_done
        last_jobs job_tables slots_ready s_ready gather_done xg_ready sel_ready sel_used gm_ready up_read sig_ready
        act_ready actT_done actT_ready sg_ready sgt_done sgt_ready y_ready scat_done moe_used moe_done
        fsq fst out_ready stored dve act pool""".split()
        S = {n: sem(n) for n in names}

        class Steps:

            def __init__(self, eng, sm):
                self.eng, self.sm, self.n = eng, sm, 0

            def __call__(self, ins):
                self.n += 1
                ins.then_inc(self.sm, 1)

            def settle(self):
                self.eng.wait_ge(self.sm, self.n)

        MISC = (bank[2], bank[7])
        M_MODT, M_CB, M_B = 0, 1, 3
        M_ACOL = 4
        M_ROWS = (11, 12, 13, 14, 29, 30, 31, 32)
        M_GLA = (5, 7, 9, 15)
        M_X = 17
        X_ORDER = (2, 3, 0, 1)
        M_ST = 21
        M_YOFF = 23
        M_MIXT = (27, 28, 33, 34)
        M_H2T = 35

        def in_item_bank(i):
            return bank[3 + i % 2]

        def op_bank(r):
            return bank[(3, 4, 1, 0)[r]]

        def rb_bank(i):
            return bank[(3, 4, 1, 0)[i % 4]]

        FM = [("gk", 0, True)] + [("xbc", m, m < 6) for m in range(8)] + [("k", 0, True), ("k", 1, True),
                                                                       ("q", 0, False), ("q", 1, False)]
        TM = [("dt", 0, 0), ("v", 0, 0), ("v", 0, 1), ("v", 1, 0), ("v", 1, 1),
              ("g", 0, 0), ("g", 1, 0), ("z", 0, 0), ("z", 1, 0)]
        U_IN = N_MOD1
        U_MOD2 = U_IN + N_IN
        U_OUT = U_MOD2 + N_MOD2

        def consumed(u):
            if u < U_IN:
                return S["mod1_used"], u + 1
            if u < U_IN + 6:
                return S["fm_done"], 2 * (u - U_IN) + 3
            if u < U_MOD2:
                return S["tm_done"], (3, 5, 6, 7, 8, 9)[u - U_IN - 6]
            if u < U_OUT:
                r, k = divmod(u - U_MOD2, KC)
                return (S["mod2_used"], (KC - 1) * r + k) if k else (S["misc_filled"], M_ROWS[4 * r + 3] + 1)
            return S["op_done"], 4 if u < U_OUT + 2 else 8

        def front_slot(u):
            return slot(u % FSLOT)

        def await_unit(eng, u):
            eng.wait_ge(loaded[u % FSLOT], 16 * (u // FSLOT + 1))

        GU = A["w_gate_up"].rearrange("e (k p) f -> e k p f", p=P)
        DN = A["w_down"].rearrange("e (i k p) f -> e i p k f", p=P, k=2)

        block = ctx.enter_context(nc.Block())

        @block.sync
        def _(sp):
            sp.dma_start(c_in, A["c2"].rearrange("k p c -> p k c")).then_inc(S["cT_in"], 16)

            def front_unit(u):
                if u >= FSLOT:
                    sp.wait_ge(*consumed(u - FSLOT))
                dst = front_slot(u)
                if u < U_IN:
                    src = A["w_mod"][u * P:(u + 1) * P, 0:UNIT]
                elif u < U_MOD2:
                    src = A["w_in"][u - U_IN]
                elif u < U_OUT:
                    r, k = divmod(u - U_MOD2, KC)
                    src = A["w_mod"][k * P:(k + 1) * P, (r + 1) * UNIT:(r + 2) * UNIT]
                else:
                    i = u - U_OUT
                    src = A["w_out"][2 * i * P:2 * (i + 1) * P, :].rearrange("(k p) n -> p k n", p=P)
                    dst = dst.rearrange("p (k n) -> p k n", k=2)
                sp.dma_start(dst, src).then_inc(loaded[u % FSLOT], 16)

            sp.dma_start(hT[:, :, 0:T], A["xT"].rearrange("k p t -> p k t")).then_inc(S["xT_in"], 16)
            sp.dma_start(hT[:, :, T:T + TX], A["ctxT"].rearrange("k p t -> p k t")).then_inc(S["xT_in"], 16)
            for u in range(N_FRONT):
                front_unit(u)

            def expert_unit(i, gate_up, down):
                dst = slot(i)
                if i < KC:
                    sp.dma_start(dst, gate_up[i]).then_inc(loaded[i], 16)
                else:
                    sp.dma_start(dst.rearrange("p (k n) -> p k n", k=2), down[i - KC]).then_inc(loaded[i], 16)

            for i in range(NSLOT):
                if i < FSLOT:
                    sp.wait_ge(*consumed(N_FRONT - FSLOT + i))
                else:
                    sp.wait_ge(S["mix_ready"], 2)
                expert_unit(i, GU[0], DN[0])

            def dyn(e):
                return (GU[bass.ds(e, 1)].rearrange("e k p f -> (e k) p f"),
                        DN[bass.ds(e, 1)].rearrange("e i p k f -> (e i) p k f"))

            sp.wait_ge(S["last_jobs"], 1)
            with sp.Fori(1, NE) as e:
                g, d = dyn(e)
                last = sp.value_load(int_last(e - 1), min_val=0, max_val=NJ - 1)
                for i in range(NSLOT):
                    sp.wait_ge(S["moe_used"], NSLOT * last + (i + 1))
                    expert_unit(i, g, d)
            for t in range(NT):
                sp.wait_ge(S["out_ready"], t + 1)
                sp.dma_start(out[0, t * P:(t + 1) * P, :], x_tm[:, t, :]).then_inc(S["stored"], 16)
            sp.wait_ge(S["stored"], 16 * NT)

        @block.gpsimd
        def _(pool):
            step = Steps(pool, S["pool"])
            small = [(bgk, A["bgk"]), (wup, A["wup"]),
                     (convw, A["convw"]), (convb, A["convb"]),
                     (gnrow, A["gla_norm"].partition_broadcast(P)),
                     (d_row, A["ssd_D"].partition_broadcast(P)), (dtb, A["dtb"].partition_broadcast(P)),
                     (negA, A["alog"].partition_broadcast(P)),
                     (brrow, A["b_router"].partition_broadcast(P))]
            assert len(small) == N_SMALL
            nc.gpsimd.memset(cs, 0.0).then_inc(S["zeroed"], 1)
            nc.gpsimd.memset(mask[0], 1.0).then_inc(S["ones_ready"], 1)
            pool.dma_start(bmodT, A["bmodT"]).then_inc(S["norm_in"], 16)
            pool.dma_start(n1T, A["n1T"]).then_inc(S["norm_in"], 16)
            pool.dma_start(wgk, A["wgk"].rearrange("k p c -> p k c")).then_inc(S["norm_in"], 16)
            pool.dma_start(wdt, A["wdt"].rearrange("k p c -> p k c")).then_inc(S["norm_in"], 16)
            pool.wait_ge(S["ones_ready"], 1)
            step(nc.gpsimd.memset(mask[1], 1.0))
            step(nc.gpsimd.memset(ident, 0.0))
            step(nc.gpsimd.iota(
                slot_no.rearrange("p (a s) -> p a s", a=2), [[0, 2], [1, SLOTS]], base=0, channel_multiplier=0,
                allow_small_or_imprecise_dtypes=True))
            for g in range(PARTS):
                step.settle()
                step(nc.gpsimd.iota(part_no[NE * g:NE * (g + 1)], [[0, SLOTS]], base=0, channel_multiplier=1,
                                    allow_small_or_imprecise_dtypes=True))
            step.settle()
            for d, sgn in ((0, 1), (1, -1)):
                for b in (0, 2):
                    v = mask[d][:, b * P:(b + 1) * P]
                    step(nc.gpsimd.affine_select(out=v, in_=v, compare_op=ALU.is_ge, fill=0.0, base=0,
                                                 pattern=[[sgn, P]], channel_multiplier=-sgn))
            step(nc.gpsimd.affine_select(out=ident, in_=ident, compare_op=ALU.not_equal, fill=1.0, base=0,
                                         pattern=[[-1, P]], channel_multiplier=1))
            step(nc.gpsimd.affine_select(out=s_upper, in_=ones, compare_op=ALU.is_gt, fill=0.0, base=0,
                                         pattern=[[1, P]], channel_multiplier=-1))
            step(nc.gpsimd.affine_select(out=s_lower, in_=ones, compare_op=ALU.is_gt, fill=0.0, base=0,
                                         pattern=[[-1, P]], channel_multiplier=1))
            step.settle()
            nc.gpsimd.memset(stat, 0.0).then_inc(S["consts"], 1)
            for dst, src in small:
                pool.dma_start(dst, src).then_inc(S["small_in"], 16)
            for g in range(4):
                pool.dma_start(modrow[32 * g:32 * g + 1], A["b_mod2"][:, g:g + 1, :].rearrange("r g c -> g r c")
                               ).then_inc(S["mr"], 16)
            pool.wait_ge(S["misc_filled"], M_MODT + 1)
            pool.dma_start(snrow, A["ssd_norm"].partition_broadcast(P)).then_inc(S["sn_in"], 16)
            for r in range(2):
                acc = front_slot(U_MOD2 + KC * r)
                for k in range(KC):
                    u = U_MOD2 + KC * r + k
                    pool.wait_ge(S["mod2_scaled"], KC * r + k + 1)
                    if k == 0:
                        continue
                    if k > 1:
                        pool.wait_ge(S["mod2_used"], (KC - 1) * r + k - 1)
                    nc.gpsimd.tensor_tensor(acc, acc, front_slot(u), ALU.add).then_inc(S["mod2_used"], 1)
                pool.wait_ge(S["mod2_used"], (KC - 1) * (r + 1))
                pool.wait_ge(S["mr"], 64)
                for g in range(4):
                    row = acc[32 * g:32 * g + 1, 512 * g:512 * (g + 1)]
                    nc.gpsimd.tensor_tensor(row, row, modrow[32 * g:32 * g + 1, r, :], ALU.add
                                            ).then_inc(S["modsum_ready"], 1)
                    pool.wait_ge(S["modsum_ready"], 4 * r + g + 1)
            pool.wait_ge(S["kvmul_ready"], 4)
            pool.wait_ge(S["o_done"], 2)
            pool.dma_start(wr, A["w_router"].rearrange("(k p) e -> p k e", p=P)).then_inc(S["late_in"], 16)
            pool.dma_start(n2row, A["norm2"].partition_broadcast(P)).then_inc(S["late_in"], 16)
            pool.dma_start(fnrow, A["final_norm"].partition_broadcast(P)).then_inc(S["late_in"], 16)
            pool.wait_ge(S["ydiag_done"], SH)
            pool.wait_ge(S["segm_ready"], 2 * SH)
            pool.dma_start(x_tm, A["x"].rearrange("(t p) c -> p t c", p=P)).then_inc(S["late_in"], 16)
            for g in range(PARTS):
                pool.dma_start(brows[NE * g:NE * (g + 1)], A["b_moe"]).then_inc(S["bias_in"], 16)
            pool.wait_ge(S["bias_in"], 16 * PARTS)
            for src, dst in ((brows[:, 0:2 * FF], gu_bias), (brows[:, 2 * FF:2 * FF + D], down_bias)):
                if dst is down_bias:
                    pool.wait_ge(S["mix_ready"], 2)
                for g in range(PARTS):
                    rows = slice(0, NE * (PARTS - g))
                    if g:
                        step(nc.gpsimd.tensor_tensor(src[rows], src[rows], dst[rows], ALU.subtract))
                        step.settle()
                    step(nc.gpsimd.tensor_copy(dst[rows], src[rows]))
                    step.settle()
            nc.gpsimd.memset(stat[:, 31:32], 0.0).then_inc(S["bias_split"], 1)
            pool.wait_ge(S["op_done"], 8)
            nc.gpsimd.iota(job_no, [[1, NJ + 1]], base=0, channel_multiplier=0,
                           allow_small_or_imprecise_dtypes=True).then_inc(S["slots_ready"], 1)
            nc.gpsimd.iota(slot_q.rearrange("p (q a s) -> p q a s", a=2, s=SLOTS),
                           [[SLOTS, T // SLOTS], [0, 2], [1, SLOTS]], base=0, channel_multiplier=0,
                           allow_small_or_imprecise_dtypes=True).then_inc(S["slots_ready"], 1)

        @block.scalar
        def _(sc):
            step = Steps(sc, S["act"])
            A_ = nc.scalar.activation
            sc.wait_ge(S["cT_in"], 16)
            sc.wait_ge(S["zeroed"], 1)
            A_(cs[:, :, 0:2], c_in, ACT.Silu).then_inc(S["cs_ready"], 1)
            sc.wait_ge(S["xT_in"], 32)
            for k in range(KC):
                A_(sq[k], hT[:, k, :], ACT.Square).then_inc(S["sq_ready"], 1)
            sc.wait_ge(S["rinv_ready"], 1)
            A_(rstd1, rstd1, ACT.Sqrt).then_inc(S["rstd_ready"], 1)
            sc.wait_ge(S["modc_ready"], 1)
            for k in range(KC):
                v = hT[:, k, T:T + TX]
                A_(v, v, ACT.Identity, bias=modc[:, k, 1:2], scale=modc[:, 8 + k, 1:2]).then_inc(S["hx_ready"], 1)

            def fm_evac(i):
                kind, m, with_ctx = FM[i]
                n = T + TX if with_ctx else T
                src = in_item_bank(i)
                sc.wait_ge(S["fm_done"], i + 1)
                if kind == "gk":
                    A_(dt_fm, src[64:64 + SH, 0:n], ACT.Copy).then_inc(S["dtT_ready"], 1)
                    A_(gk_fm, src[0:RANK, 0:n], ACT.Copy).then_inc(S["fm_evac"], 1)
                elif kind == "xbc":
                    A_(xbc[:, m, 0:n], src[:, 0:n], ACT.Copy).then_inc(S["fm_evac"], 1)
                elif kind == "k":
                    A_(k_fm[:, m, :], src, ACT.Copy).then_inc(S["fm_evac"], 1)
                else:
                    A_(q_fm[:, m, :], src[:, 0:n], ACT.Copy, scale=DK ** -0.5).then_inc(S["fm_evac"], 1)

            def conv_silu(m):
                n = T + TX if m < 6 else T
                sc.wait_ge(S["conv_ready"], m + 1)
                A_(conv[:, m, 0:n], conv[:, m, 0:n], ACT.Silu).then_inc(S["conv_act"], 1)

            def mod2_scale(m):
                await_unit(sc, U_MOD2 + m)
                w = front_slot(U_MOD2 + m)
                A_(w, w, ACT.Copy, scale=cs[:, m % KC, 0:1]).then_inc(S["mod2_scaled"], 1)

            for i in range(3):
                fm_evac(i)
            sc.wait_ge(S["soft_arg"], 1)
            step(A_(soft, soft, ACT.Exp))
            step.settle()
            A_(soft, soft, ACT.Ln, bias=1.0).then_inc(S["soft_ready"], 1)
            for i in range(3, len(FM)):
                fm_evac(i)
                if i >= 5:
                    conv_silu(i - 5)
                if i in (9, 10, 12):
                    mod2_scale((9, 10, 12).index(i))

            def tm_evac(i):
                kind, half, c = TM[i]
                b = in_item_bank(len(FM) + i)
                sc.wait_ge(S["tm_done"], i + 1)
                if kind == "dt":
                    A_(dtr, b[:, 0:4 * SH].rearrange("p (t h) -> p t h", t=4), ACT.Copy).then_inc(S["tm_evac"], 1)
                    return
                col = {"v": 0, "g": 512, "z": 1024}[kind] + 256 * half
                dst = (vx if c else vgz)[:, :, col:col + 256]
                A_(dst, b.rearrange("p (t c) -> p t c", t=2), ACT.Copy).then_inc(S["tm_evac"], 1)

            tm_evac(0)
            sc.wait_ge(S["small_in"], 16 * N_SMALL)
            A_(negA, negA, ACT.Exp).then_inc(S["negA_ready"], 1)
            sc.wait_ge(S["dt_ready"], 1)
            step(A_(dtt, dtt, ACT.Exp))
            step.settle()
            A_(dtt, dtt, ACT.Ln, bias=1.0).then_inc(S["dt_sp"], 1)

            def decay_exps(n):
                d = n % 2
                b = n % 2
                up = 1.0 / GATE_NORM
                sc.wait_ge(S["kvarg_ready"], n + 1)
                sgn = -1.0 if d == 0 else 1.0
                A_(kv[n], kv[n], ACT.Exp, scale=sgn * up).then_inc(S["exp_ready"], 1)
                A_(qv[b], qv[b], ACT.Exp, scale=-sgn * up).then_inc(S["exp_ready"], 1)
                if d == 0:
                    A_(qd[n], pre[:, n, 0, 1:T + 1], ACT.Exp, scale=up).then_inc(S["exp_ready"], 1)
                    A_(kx[b], pre[:, n, 1, 1:TX + 1], ACT.Exp, scale=-up,
                       bias=stat[:, 16 + n:17 + n]).then_inc(S["exp_ready"], 1)
                else:
                    A_(qd[n], pre[:, n, 0, 0:T], ACT.Exp, scale=-up,
                       bias=stat[:, 16 + n:17 + n]).then_inc(S["exp_ready"], 1)
                    A_(kx[b], pre[:, n, 1, 0:TX], ACT.Exp, scale=up).then_inc(S["exp_ready"], 1)

            def mod_row(i):
                sc.wait_ge(S["misc_filled"], M_ROWS[i] + 1)
                sc.wait_ge(S["misc_read"], M_ROWS[i])
                A_(gB[:, 512 * i:512 * (i + 1)], MISC[M_ROWS[i] % 2], ACT.Identity,
                   bias=1.0 if i in (4, 5) else 0.0).then_inc(S["misc_read"], 1)

            def o_copy(c):
                sc.wait_ge(S["o_done"], c + 1)
                ov_ = o_sb.rearrange("p (t h v) -> p t h v", t=2, h=GH)
                for e in range(2):
                    src = bank[5 + e].rearrange("p (t c v) -> p t c v", t=2, c=2)[:, :, c, :]
                    A_(ov_[:, :, 2 * c + e, :], src, ACT.Copy).then_inc(S["o_copied"], 1)

            mod2_scale(3)
            tm_evac(1)
            tm_evac(2)
            decay_exps(0)
            mod2_scale(4)
            tm_evac(3)
            tm_evac(4)
            decay_exps(1)
            mod2_scale(5)
            sc.wait_ge(S["misc_read"], M_ACOL + 1)
            A_(eac, acol, ACT.Exp).then_inc(S["eac_ready"], 1)
            tm_evac(5)
            decay_exps(2)
            tm_evac(6)
            decay_exps(3)
            mod2_scale(6)
            mod2_scale(7)
            tm_evac(7)
            mod2_scale(8)
            tm_evac(8)
            for i in range(4):
                mod_row(i)
            mod2_scale(9)
            sc.wait_ge(S["misc_filled"], M_X + 4)
            o_copy(0)
            o_copy(1)
            sc.wait_ge(S["tm_evac"], len(TM))
            gz = vgz[:, :, 512:1536]
            A_(gz, gz, ACT.Silu).then_inc(S["silu_ready"], 1)
            sc.wait_ge(S["o_copied"], 4)
            for a in range(8):
                last = A_(sqout[:, a * DV:(a + 1) * DV], o_sb[:, a * DV:(a + 1) * DV], ACT.Square,
                          accum_out=stat[:, a:a + 1])
            last.then_inc(S["gla_sq"], 1)
            mod2_scale(10)
            mod2_scale(11)
            sc.wait_ge(S["gst"], 1)
            A_(stat[:, 0:8], stat[:, 0:8], ACT.Sqrt).then_inc(S["gsq"], 1)

            def mix_t(half, t):
                m = M_MIXT[2 * half + t]
                sc.wait_ge(S["misc_filled"], m + 1)
                sc.wait_ge(S["misc_read"], m)
                A_(mixT[:, 4 * half:4 * half + 4, t * P:(t + 1) * P],
                   MISC[m % 2].rearrange("p (q c) -> p q c", q=4), ACT.Copy).then_inc(S["misc_read"], 1)

            for i in range(2 * SH):
                sc.wait_ge(S["arg_ready"], i + 1)
                A_(seg[i % 4], seg[i % 4], ACT.Exp).then_inc(S["segexp_ready"], 1)
                if i in (1, 3, 5, 7):
                    mod2_scale(12 + i // 2)
            mix_t(0, 0)
            mix_t(0, 1)
            for i in range(4, 8):
                mod_row(i)
            for t in range(2):
                sc.wait_ge(S["yz_ready"], t + 1)
                for g in range(SG):
                    c = slice(SI * t + 256 * g, SI * t + 256 * (g + 1))
                    last = A_(sqout[:, c], y_acc[:, c], ACT.Square, accum_out=stat[:, 8 + 2 * t + g:9 + 2 * t + g])
            last.then_inc(S["ssd_sq"], 1)
            sc.wait_ge(S["sst"], 1)
            A_(stat[:, 8:12], stat[:, 8:12], ACT.Sqrt).then_inc(S["ssq"], 1)
            mix_t(1, 0)
            mix_t(1, 1)

            def h2_t(t):
                for half in range(2):
                    m = M_H2T + 2 * t + half
                    sc.wait_ge(S["misc_filled"], m + 1)
                    sc.wait_ge(S["misc_read"], m)
                    A_(h2T[:, 4 * half:4 * half + 4, t * P:(t + 1) * P],
                       MISC[m % 2].rearrange("p (q c) -> p q c", q=4), ACT.Copy).then_inc(S["misc_read"], 1)

            for t in range(NT):
                for half in range(2):
                    sc.wait_ge(S["xnew_ready"], 2 * t + half + 1)
                    c = slice(512 * half, 512 * half + 512)
                    A_(fB[:, 2048 + 512 * half:2560 + 512 * half], x_tm[:, t, c], ACT.Square,
                       accum_out=stat[:, 20 + t + 4 * half:21 + t + 4 * half]).then_inc(S["nsq"], 1)
                sc.wait_ge(S["nst"], t + 1)
                A_(stat[:, 22 + t:23 + t], stat[:, 22 + t:23 + t], ACT.Sqrt).then_inc(S["nsq"], 1)
                if t == 0:
                    h2_t(0)
            h2_t(1)

            sc.wait_ge(S["ex_ready"], 1)
            A_(rt[3], rt[3], ACT.Exp).then_inc(S["ex_done"], 1)

            def job(j):
                sc.wait_ge(S["gm_ready"], j + 1)
                A_(sig, gm, ACT.Sigmoid, scale=ALPHA).then_inc(S["sig_ready"], 1)

            with sc.Fori(0, NE) as j:
                job(j)
            sc.wait_ge(S["job_tables"], 1)
            last = sc.value_load(int_last(NE - 1), min_val=NE - 1, max_val=NJ - 1)
            with sc.Fori(NE, NE + FEW) as j:
                with sc.If(last > j - 1):
                    job(j)
            with sc.If(last > NE + FEW - 1):
                with sc.Fori(NE + FEW, NJ) as j:
                    with sc.If(last > j - 1):
                        job(j)
            A_(stat[:, 30:31], stat[:, 30:31], ACT.Sqrt)
            for r in range(4):
                t, half = divmod(r, 2)
                sc.wait_ge(S["fsq"], r + 1)
                cols = slice(512 * half, 512 * half + 512)
                A_(h2[:, t, cols], x_tm[:, t, cols], ACT.Square, accum_out=stat[:, 24 + t + 4 * half:25 + t + 4 * half]
                   ).then_inc(S["fst"], 1)
            for t in range(NT):
                sc.wait_ge(S["fsq"], 2 * NT + t + 1)
                A_(stat[:, 26 + t:27 + t], stat[:, 26 + t:27 + t], ACT.Sqrt).then_inc(S["fst"], 1)

        @block.tensor
        def _(pe):
            mm = nc.tensor.matmul

            def misc_begin(i):
                if i >= 2:
                    pe.wait_ge(S["misc_read"], i - 1)
                return MISC[i % 2]

            def mod_unit(u, dst, k, used):
                await_unit(pe, u)
                w = front_slot(u)
                for g in range(4):
                    last = mm(dst[32 * g:32 * g + 32, :], cs[:, k, :], w[:, 512 * g:512 * (g + 1)],
                              start=(k == 0), stop=(k == KC - 1))
                last.then_inc(used, 1)

            pe.wait_ge(S["ones_ready"], 1)
            for k in range(KC):
                pe.wait_ge(S["sq_ready"], k + 1)
                mm(bank[1], ones, sq[k], start=(k == 0), stop=(k == KC - 1)).then_inc(S["sq_summed"], 1)
            pe.wait_ge(S["cs_ready"], 1)
            for k in range(KC):
                mod_unit(k, bank[0], k, S["mod1_used"])
            pe.wait_ge(S["consts"], 1)
            b = misc_begin(M_MODT)
            pe.wait_ge(S["row1_ready"], 1)
            for q in range(4):
                last = nc.tensor.transpose(b[:, q * P:(q + 1) * P], modrow1[:, q * P:(q + 1) * P], ident)
            last.then_inc(S["misc_filled"], 1)

            def fm_chunk(i):
                kind, m, with_ctx = FM[i]
                n = T + TX if with_ctx else T
                b = in_item_bank(i)
                u = U_IN + (i - 1) // 2
                if kind != "gk":
                    await_unit(pe, u)
                    w = front_slot(u).rearrange("p (k c) -> p k c", k=KC)[:, :, P * ((i - 1) % 2):P * ((i - 1) % 2) + P]
                else:
                    w = wgk
                    pe.wait_ge(S["norm_in"], 64)
                if i >= 2:
                    pe.wait_ge(S["fm_evac"], i - 1)
                for k in range(KC):
                    if i == 0:
                        pe.wait_ge(S["hl_ready"], k + 1)
                        pe.wait_ge(S["hx_ready"], k + 1)
                    last = mm(b[0:w.shape[2], 0:n], w[:, k, :], hT[:, k, 0:n], start=(k == 0), stop=(k == KC - 1))
                    if i == 0:
                        last = mm(b[64:64 + SH, 0:n], wdt[:, k, :], hT[:, k, 0:n], start=(k == 0), stop=(k == KC - 1))
                last.then_inc(S["fm_done"], 1)

            def fm_unit(a):
                fm_chunk(a)
                fm_chunk(a + 1)

            fm_chunk(0)
            fm_unit(1)
            pe.wait_ge(S["small_in"], 16 * N_SMALL)
            pe.wait_ge(S["fm_evac"], 1)
            for n in range(4):
                c, d = divmod(n, 2)
                if n >= 2:
                    pe.wait_ge(S["gate_read"], n - 1)
                mm(bank[5 + n % 2], wup[:, d, c * P:(c + 1) * P], gk_fm, start=True, stop=True
                   ).then_inc(S["gate_done"], 1)
            for a in range(3, len(FM), 2):
                fm_unit(a)

            def tm_item(i):
                kind, half, c = TM[i]
                n = len(FM) + i
                b = in_item_bank(n)
                if i == 0:
                    pe.wait_ge(S["fm_evac"], n - 1)
                elif i == 1:
                    pe.wait_ge(S["fm_evac"], n - 1)
                else:
                    pe.wait_ge(S["tm_evac"], i - 1)
                if kind == "dt":
                    pe.wait_ge(S["dtT_ready"], 1)
                    for t in range(4):
                        last = nc.tensor.transpose(b[:, SH * t:SH * (t + 1)], dt_fm[:, t * P:(t + 1) * P],
                                                   ident[64:64 + SH, 64:64 + SH])
                    last.then_inc(S["tm_done"], 1)
                    return
                u = U_IN + 6 + {"v": 0, "g": 2, "z": 4}[kind] + half
                await_unit(pe, u)
                w = front_slot(u).rearrange("p (k c) -> p k c", k=KC)
                for t in range(2):
                    for k in range(KC):
                        tokens = slice((2 * c + t) * P, (2 * c + t + 1) * P)
                        last = mm(b[:, 256 * t:256 * (t + 1)], hT[:, k, tokens], w[:, k, :],
                                  start=(k == 0), stop=(k == KC - 1))
                last.then_inc(S["tm_done"], 1)

            def acol_sums():
                b = misc_begin(M_ACOL)
                pe.wait_ge(S["dt_exp"], 1)
                for d in range(2):
                    near, far = (upper, 0) if d == 0 else (lower, 1)
                    for t in range(2):
                        dst = b[:, (t * 2 + d) * SH:(t * 2 + d + 1) * SH]
                        both = t != far
                        mm(dst, near, a_tm[:, t, d, :], start=True, stop=not both)
                        if both:
                            mm(dst, ones, a_tm[:, 1 - t, d, :], start=False, stop=True)
                    near, far = (s_lower, 1) if d == 0 else (s_upper, 0)
                    for t in range(2):
                        dst = b[:, ((2 + t) * 2 + d) * SH:((2 + t) * 2 + d + 1) * SH]
                        both = t != far
                        last = mm(dst, near, a_tm[:, 2 + t, d, :], start=True, stop=not both)
                        if both:
                            last = mm(dst, ones, a_tm[:, 3 - t, d, :], start=False, stop=True)
                last.then_inc(S["misc_filled"], 1)

            for i in range(3):
                tm_item(i)
            pe.wait_ge(S["conv_act"], 8)
            for g in range(SG):
                b = misc_begin(M_CB + g)
                for jt in range(2):
                    last = mm(b[:, 256 * jt:256 * (jt + 1)], conv[:, 4 + g, jt * P:(jt + 1) * P], conv[:, 6 + g, 0:T],
                              start=True, stop=True)
                last.then_inc(S["misc_filled"], 1)
            b = misc_begin(M_B)
            for t in range(2):
                for g in range(SG):
                    last = nc.tensor.transpose(b[:, (2 * t + g) * P:(2 * t + g + 1) * P],
                                               conv[:, 4 + g, (2 + t) * P:(3 + t) * P], ident)
            last.then_inc(S["misc_filled"], 1)

            def mod_row(i):
                b = misc_begin(M_ROWS[i])
                pe.wait_ge(S["modsum_ready"], 4 * (i // 4 + 1))
                g = i % 4
                mm(b, ones, front_slot(U_MOD2 + KC * (i // 4))[:, 512 * g:512 * (g + 1)], start=True, stop=True
                   ).then_inc(S["misc_filled"], 1)

            def gla_scores(n):
                c, d = divmod(n, 2)
                kb, qb = kv[n], qv[n % 2]
                pe.wait_ge(S["kvmul_ready"], n + 1)
                for e in range(2):
                    rows = slice(64 * e, 64 * e + 64)
                    b = bank[e]
                    if n >= 1:
                        pe.wait_ge(S["pt_ready"], 2 * (n - 1) + e + 1)
                    elif e == 0:
                        pe.wait_ge(S["row1_ready"], 1)
                    else:
                        pe.wait_ge(S["rinv_ready"], 1)
                    for blk in range(NB):
                        near = (blk < NPT) == (d == 0)
                        i4 = blk % NPT
                        q = qb[rows, blk * BLK:(blk + 1) * BLK]
                        if near:
                            col = (0 if d == 0 else 2 * P) + i4 * BLK
                            last = mm(b[:, col:col + BLK], kb[rows, i4 * P:(i4 + 1) * P], q, start=True, stop=True)
                        else:
                            for jt in range(2):
                                col = (1 + jt if d == 0 else jt) * P + i4 * BLK
                                last = mm(b[:, col:col + BLK],
                                          kb[rows, KNEAR + T * i4 + P * jt:KNEAR + T * i4 + P * (jt + 1)], q,
                                          start=True, stop=True)
                    last.then_inc(S["score_done"], 1)
                b = misc_begin(M_GLA[n])
                for t in range(2):
                    last = nc.tensor.transpose(b[:, t * P:(t + 1) * P], kx[n % 2][:, t * P:(t + 1) * P], ident)
                last.then_inc(S["misc_filled"], 1)
                b = misc_begin(M_GLA[n] + 1)
                pe.wait_ge(S["misc_read"], M_GLA[n] + 1)
                pe.wait_ge(S["tm_evac"], 5)
                for e in range(2):
                    h = 2 * c + e
                    for t in range(2):
                        last = mm(b[64 * e:64 * e + 64, 0:DV], kxT[:, t * P + 64 * e:t * P + 64 * e + 64],
                                  vx[:, t, h * DV:(h + 1) * DV], start=(t == 0), stop=(t == 1))
                last.then_inc(S["misc_filled"], 1)

            def gla_out(c):
                pe.wait_ge(S["pt_ready"], 4 * (c + 1))
                pe.wait_ge(S["misc_read"], M_GLA[2 * c + 1] + 2)
                if c == 0:
                    pe.wait_ge(S["gate_read"], 4)
                for e in range(2):
                    h = 2 * c + e
                    rows = slice(64 * e, 64 * e + 64)
                    for t in range(2):
                        dst = bank[5 + e][:, (2 * t + c) * DV:(2 * t + c + 1) * DV]
                        terms = [(0, 0, 0), (1, 0, 0), (1, 1, 1)] if t == 0 else [(0, 0, 1), (0, 1, 2), (1, 1, 2)]
                        for x, (d, jt, s) in enumerate(terms):
                            mm(dst, pt[:, d, e, s * P:(s + 1) * P], vgz[:, jt, h * DV:(h + 1) * DV],
                               start=(x == 0), stop=False)
                        for d in range(2):
                            last = mm(dst, qd[2 * c + d][rows, t * P:(t + 1) * P], gS[rows, d, :],
                                      start=False, stop=(d == 1))
                last.then_inc(S["o_done"], 1)

            def x_t(i):
                b = misc_begin(M_X + i)
                t = X_ORDER[i]
                for m in range(4):
                    last = nc.tensor.transpose(b[:, m * P:(m + 1) * P], conv[:, m, t * P:(t + 1) * P], ident)
                last.then_inc(S["misc_filled"], 1)

            acol_sums()
            tm_item(3)
            tm_item(4)
            gla_scores(0)
            tm_item(5)
            gla_scores(1)
            tm_item(6)
            gla_out(0)
            tm_item(7)
            gla_scores(2)
            tm_item(8)
            for i in range(4):
                mod_row(i)
            gla_scores(3)
            x_t(0)
            x_t(1)
            gla_out(1)
            x_t(2)
            x_t(3)
            for d in range(2):
                b = misc_begin(M_ST + d)
                pe.wait_ge(S["xw_ready"], d + 1)
                for g in range(SG):
                    for t in range(2):
                        last = mm(b[:, 256 * g:256 * (g + 1)], b_tm[:, t, g, :], xw[:, t, d, 256 * g:256 * (g + 1)],
                                  start=(t == 0), stop=(t == 1))
                last.then_inc(S["misc_filled"], 1)
            for t in range(2):
                for d in range(2):
                    b = misc_begin(M_YOFF + 2 * t + d)
                    pe.wait_ge(S["misc_read"], M_ST + d + 1)
                    for g in range(SG):
                        last = mm(b[:, 256 * g:256 * (g + 1)], conv[:, 6 + g, t * P:(t + 1) * P],
                                  sS[:, d, 256 * g:256 * (g + 1)], start=True, stop=True)
                    last.then_inc(S["misc_filled"], 1)

            def row_sums(i):
                h, d = divmod(i, 2)
                b = rb_bank(i)
                if i >= 4:
                    pe.wait_ge(S["arg_ready"], i - 3)
                elif i == 0:
                    pe.wait_ge(S["tm_evac"], len(TM))
                tri = (upper, lower)[d]
                a = [bc(a_tm[:, t, d, h:h + 1], [P, P]) for t in range(2)]
                for t in range(2):
                    dst = b[:, t * P:(t + 1) * P]
                    both = t == 1 - d
                    last = mm(dst, a[t], tri, start=True, stop=not both)
                    if both:
                        last = mm(dst, a[1 - t], ones, start=False, stop=True)
                last.then_inc(S["rb_done"], 1)

            def ssd_out(h):
                pe.wait_ge(S["segm_ready"], 2 * h + 2)
                if h == 0:
                    pe.wait_ge(S["o_copied"], 4)
                for t in range(2):
                    dst = bank[5 + t][:, h * HP:(h + 1) * HP]
                    terms = [(0, 0, 0), (1, 0, 0), (1, 1, 1)] if t == 0 else [(0, 0, 1), (0, 1, 2), (1, 1, 2)]
                    for x, (d, jt, s) in enumerate(terms):
                        last = mm(dst, seg[(2 * h + d) % 4][:, s * P:(s + 1) * P], xdt[:, jt, d, h * HP:(h + 1) * HP],
                                  start=(x == 0), stop=(x == 2))
                last.then_inc(S["ydiag_done"], 1)

            pe.wait_ge(S["pt_ready"], 8)
            for i in range(4):
                row_sums(i)

            def mix_t(half, t):
                b = misc_begin(M_MIXT[2 * half + t])
                pe.wait_ge(S["mix_ready"], half + 1)
                for q in range(4):
                    col = 512 + (4 * half + q) * P
                    last = nc.tensor.transpose(b[:, q * P:(q + 1) * P], vgz[:, t, col:col + P], ident)
                last.then_inc(S["misc_filled"], 1)

            for h in range(SH):
                for i in (2 * h + 4, 2 * h + 5):
                    if i < 2 * SH:
                        row_sums(i)
                if h == 7:
                    mix_t(0, 0)
                    mix_t(0, 1)
                ssd_out(h)

            def out_proj(r, half):
                t, c = divmod(r, 2)
                for k in range(4 * half, 4 * half + 4):
                    await_unit(pe, U_OUT + k // 2)
                    w = front_slot(U_OUT + k // 2)[:, (k % 2) * 1024 + c * 512:(k % 2) * 1024 + c * 512 + 512]
                    last = mm(op_bank(r), mixT[:, k, t * P:(t + 1) * P], w, start=(k == 0), stop=(k == KC - 1),
                              skip_group_check=True)
                last.then_inc(S["op_done"], 1)

            for i in range(4, 8):
                mod_row(i)
            pe.wait_ge(S["misc_read"], M_MIXT[1] + 1)
            pe.wait_ge(S["arg_ready"], 2 * SH)
            for r in range(4):
                out_proj(r, 0)
            mix_t(1, 0)
            mix_t(1, 1)
            pe.wait_ge(S["misc_read"], M_MIXT[3] + 1)
            for r in range(4):
                out_proj(r, 1)

            def keep_warm(n):
                for _ in range(n):
                    mm(bank[3], ones, h2[:, 0, 0:512], start=True, stop=True)

            def gate_up_bias(j, start=True):
                pe.wait_ge(S["sel_ready"], j + 1)
                for b, col in ((bank[0], 0), (bank[1], FF)):
                    for half in range(2):
                        mm(b[64 * half:64 * half + 64, :], job_sel, gu_bias[:, col + 512 * half:col + 512 * half + 512],
                           start=start, stop=False)

            for t in range(2):
                for half in range(2):
                    b = misc_begin(M_H2T + 2 * t + half)
                    pe.wait_ge(S["h2_ready"], 2 * t + half + 1)
                    for q in range(4):
                        k = 4 * half + q
                        last = nc.tensor.transpose(b[:, q * P:(q + 1) * P], h2[:, t, k * P:(k + 1) * P], ident)
                    last.then_inc(S["misc_filled"], 1)
                if t == 1:
                    keep_warm(1)
                pe.wait_ge(S["misc_read"], M_H2T + 2 * t + 2)
                for k in range(KC):
                    last = mm(bank[5][:, t * NE:(t + 1) * NE], h2T[:, k, t * P:(t + 1) * P], wr[:, k, :],
                              start=(k == 0), stop=(k == KC - 1))
                last.then_inc(S["log_done"], 1)
                if t == 0:
                    keep_warm(2)
            keep_warm(4)
            b = bank[6]
            pe.wait_ge(S["sel_made"], 1)
            sel = rt[0]
            mm(b[:, 0:NE], s_upper, sel[:, 0, :], start=True, stop=True)
            mm(b[:, NE:2 * NE], s_upper, sel[:, 1, :], start=True, stop=False)
            mm(b[:, NE:2 * NE], ones, sel[:, 0, :], start=False, stop=True)
            mm(b[:, 2 * NE:3 * NE], ones, sel[:, 0, :], start=True, stop=False)
            mm(b[:, 2 * NE:3 * NE], ones, sel[:, 1, :], start=False, stop=True).then_inc(S["rank_done"], 1)

            def acc(t, half):
                return bank[4 + 2 * t + half]

            def gather(j):
                pe.wait_ge(S["s_ready"], j + 1)
                for k in range(KC):
                    for t in range(2):
                        last = mm(bank[3][:, k * SLOTS:(k + 1) * SLOTS], h2[:, t, k * P:(k + 1) * P], S_j[:, t, :],
                                  start=(t == 0), stop=(t == 1))
                last.then_inc(S["gather_done"], 1)

            gather(0)

            def scatter(jobs, first=False, final=False):
                pe.wait_ge(S["y_ready"], jobs + 1)
                pe.wait_ge(S["sgt_ready"], jobs + 1)
                for t in range(2):
                    for half in range(2):
                        rows = slice(64 * half, 64 * half + 64)
                        last = mm(acc(t, half), SGT[rows, t, :], ysb[rows, :], start=first, stop=final,
                                  skip_group_check=True)
                        if final:
                            last.then_inc(S["moe_done"], 1)
                return last

            def job(j, first=False):
                if not first:
                    gate_up_bias(j)
                pe.wait_ge(S["xg_ready"], j + 1)
                e = 0 if first else pe.value_load(int_e(j), min_val=0, max_val=NE - 1)
                for k in range(KC):
                    if first and k == KC - 1:
                        pe.wait_ge(S["bias_split"], 1)
                        gate_up_bias(j, start=False)
                    pe.wait_ge(loaded[k], 16 * (e + 1 + N_FRONT // FSLOT))
                    w = slot(k)
                    for b, col in ((bank[0], 0), (bank[1], FF)):
                        for half in range(2):
                            last = mm(b[64 * half:64 * half + 64, :], xg[:, k, :],
                                      w[:, col + 512 * half:col + 512 * half + 512], start=(first and k == 0),
                                      stop=(k == KC - 1))
                    last.then_inc(S["moe_used"], 1)
                scatter(j, first).then_inc(S["scat_done"], 1)
                pe.wait_ge(S["sg_ready"], j + 1)
                for t in range(2):
                    last = nc.tensor.transpose(bank[2][:, t * P:(t + 1) * P], SG_j[:, t, :], ident)
                last.then_inc(S["sgt_done"], 1)
                pe.wait_ge(S["act_ready"], j + 1)
                for q in range(4):
                    last = nc.tensor.transpose(bank[0][:, q * P:(q + 1) * P], act[:, q * P:(q + 1) * P], ident)
                last.then_inc(S["actT_done"], 1)
                gather(j + 1)
                pe.wait_ge(S["sgt_ready"], j + 2)
                for half in range(2):
                    last = mm(bank[2][64 * half:64 * half + 64, :], job_sel,
                              down_bias[:, 512 * half:512 * half + 512], start=True, stop=False)
                last.then_inc(S["sel_used"], 1)
                pe.wait_ge(S["actT_ready"], j + 1)
                for c in range(KC):
                    s = KC + c // 2
                    if c % 2 == 0:
                        front = N_FRONT // FSLOT if s < FSLOT else 0
                        pe.wait_ge(loaded[s], 16 * (e + 1 + front))
                    hh, q = divmod(c, 4)
                    for half in range(2):
                        last = mm(bank[2][64 * half:64 * half + 64, :], actT[:, q, 64 * hh:64 * hh + 64],
                                  slot(s)[:, (c % 2) * 1024 + 512 * half:(c % 2) * 1024 + 512 * half + 512],
                                  start=False, stop=(c == KC - 1))
                    if c % 2 == 1:
                        last.then_inc(S["moe_used"], 1)

            job(0, first=True)
            pe.wait_ge(S["job_tables"], 1)
            with pe.Fori(1, NE) as j:
                job(j)
            last = pe.value_load(int_last(NE - 1), min_val=NE - 1, max_val=NJ - 1)
            with pe.Fori(NE, NE + FEW) as j:
                with pe.If(last > j - 1):
                    job(j)
            with pe.If(last > NE + FEW - 1):
                with pe.Fori(NE + FEW, NJ) as j:
                    with pe.If(last > j - 1):
                        job(j)
            scatter(last + 1, final=True)

        @block.vector
        def _(v):
            V = nc.vector
            step = Steps(v, S["dve"])
            TT, TS, STT = V.tensor_tensor, V.tensor_scalar, V.scalar_tensor_tensor

            def misc_wait(i):
                v.wait_ge(S["misc_filled"], i + 1)
                return MISC[i % 2]

            def misc_read(ins):
                ins.then_inc(S["misc_read"], 1)

            v.wait_ge(S["sq_summed"], KC)
            step(TS(rstd1, bank[1], 1.0 / D, EPS, ALU.mult, ALU.add))
            step.settle()
            V.reciprocal(rstd1, rstd1).then_inc(S["rinv_ready"], 1)
            v.wait_ge(S["rstd_ready"], 1)
            TT(hT, hT, bc(rstd1.rearrange("p (a t) -> p a t", a=1), [P, KC, T + TX]), ALU.mult
               ).then_inc(S["xh_ready"], 1)
            v.wait_ge(S["mod1_used"], KC)
            V.tensor_copy(modrow1, bank[0]).then_inc(S["row1_ready"], 1)
            b = misc_wait(M_MODT).rearrange("p (q g c) -> p g q c", q=4, g=4)
            v.wait_ge(S["norm_in"], 64)
            bm = bmodT.rearrange("p (g q) -> p g q", g=4)
            mc = modc.rearrange("p (g q) c -> p g q c", g=4)
            step(TT(mc[:, :, :, 0], b[:, :, :, 0], bm, ALU.add))
            misc_read(TT(mc[:, :, :, 1], b[:, :, :, 1], bm, ALU.add))
            v.wait_ge(S["misc_read"], 1)
            step.settle()
            step(TS(modc[:, 8:16, :], modc[:, 8:16, :], 1.0, None, ALU.add))
            step.settle()
            v.wait_ge(S["xh_ready"], 1)
            TT(modc[:, 8:16, :], modc[:, 8:16, :], bc(n1T.rearrange("p (k c) -> p k c", c=1), [P, KC, 2]), ALU.mult
               ).then_inc(S["modc_ready"], 1)
            v.wait_ge(S["modc_ready"], 1)
            for k in range(KC):
                x = hT[:, k, 0:T]
                TS(x, x, modc[:, 8 + k, 0:1], modc[:, k, 0:1], ALU.mult, ALU.add).then_inc(S["hl_ready"], 1)
            step(V.memset(pre[:, :, :, 0:1], 0.0))

            def conv_chunk(m):
                v.wait_ge(S["fm_evac"], m + 2)
                if m == 0:
                    v.wait_ge(S["small_in"], 16 * N_SMALL)
                x, y = xbc[:, m, :], conv[:, m, :]
                n = T + TX if m < 6 else T
                step(TS(y[:, 0:n], x[:, 0:n], convw[:, m, 4:5], convb[:, m:m + 1], ALU.mult, ALU.add))
                x3 = x[:, 0:T].rearrange("p (r c) -> p r c", r=ROWS)
                y3 = y[:, 0:T].rearrange("p (r c) -> p r c", r=ROWS)
                for tap in (0, 1, 2, 3, 5, 6, 7, 8):
                    dy, dx = tap // 3 - 1, tap % 3 - 1
                    r0, r1 = max(0, -dy), ROWS - max(0, dy)
                    c0, c1 = max(0, -dx), GRID - max(0, dx)
                    yo = y3[:, r0:r1, c0:c1]
                    xi = x3[:, r0 + dy:r1 + dy, c0 + dx:c1 + dx]
                    step.settle()
                    ins = STT(out=yo, in0=xi, scalar=convw[:, m, tap:tap + 1], in1=yo, op0=ALU.mult, op1=ALU.add)
                    if tap == 8:
                        ins.then_inc(S["conv_ready"], 1)
                    else:
                        step(ins)
                    if dy == 0 and m < 6:
                        yo = y[:, T + c0:T + TX - max(0, dx)]
                        xi = x[:, T + c0 + dx:T + TX - max(0, dx) + dx]
                        step(STT(out=yo, in0=xi, scalar=convw[:, m, tap:tap + 1], in1=yo, op0=ALU.mult, op1=ALU.add))

            conv_chunk(0)
            for n in range(4):
                v.wait_ge(S["gate_done"], n + 1)
                step(TS(ld[:, n, :], bank[5 + n % 2], bgk[:, n:n + 1], 0.0, ALU.add, ALU.min))
                TS(soft[:, n, :], bank[5 + n % 2], bgk[:, n:n + 1], 0.0, ALU.add, ALU.max).then_inc(S["gate_read"], 1)
            v.wait_ge(S["gate_read"], 4)
            step.settle()
            TT(soft, ld, soft, ALU.subtract).then_inc(S["soft_arg"], 1)
            conv_chunk(1)
            v.wait_ge(S["soft_ready"], 1)
            step.settle()
            step(TT(ld, ld, soft, ALU.subtract))
            step.settle()
            for n in range(4):
                for s in range(2):
                    step(V.tensor_tensor_scan(pre[:, n, s, 1:T + 1], bc(ones[:, 0:1], [P, T]),
                                              ld[:, n, s * T:(s + 1) * T], 0.0, ALU.mult, ALU.add))
            step.settle()
            for n in range(4):
                s = 1 if n % 2 == 0 else 0
                step(TS(stat[:, 16 + n:17 + n], pre[:, n, s, T:T + 1], 1.0 / GATE_NORM, None, ALU.mult))
            for m in range(2, 8):
                conv_chunk(m)

            v.wait_ge(S["tm_evac"], 1)
            for d in range(2):
                step(TT(dta[:, :, d, :], dtr, bc(dtb3[:, d:d + 1, :], [P, 4, SH]), ALU.add))
            step.settle()
            step(TS(dtt, dta, 0.0, None, ALU.min))
            step.settle()
            step(TS(dta, dta, 0.0, None, ALU.max))
            step.settle()
            TT(dtt, dtt, dta, ALU.subtract).then_inc(S["dt_ready"], 1)

            def args(n):
                d, b = n % 2, n % 2
                off = 1 if d == 0 else 0
                src = pre[:, n, 0, off:off + T]
                lim = CLAMP * GATE_NORM
                clip = (-lim, ALU.max) if d == 0 else (lim, ALU.min)
                if n >= 2:
                    v.wait_ge(S["score_done"], 2 * (n - 1))
                for blk in range(NB):
                    near = (blk < NPT) == (d == 0)
                    i4 = blk % NPT
                    ref = pre[:, n, 0, blk * BLK + BLK // 2:blk * BLK + BLK // 2 + 1]
                    if near:
                        dst = kv[n][:, i4 * P:(i4 + 1) * P]
                        s = src[:, 0:P] if d == 0 else src[:, P:2 * P]
                    else:
                        dst = kv[n][:, KNEAR + i4 * T:KNEAR + (i4 + 1) * T]
                        s = src
                    step(TS(dst, s, ref, clip[0], ALU.subtract, clip[1]))
                    last = TS(qv[b][:, blk * BLK:(blk + 1) * BLK], src[:, blk * BLK:(blk + 1) * BLK], ref,
                              -clip[0], ALU.subtract, ALU.min if d == 0 else ALU.max)
                    if blk < NB - 1:
                        step(last)
                last.then_inc(S["kvarg_ready"], 1)

            def mults(n):
                c, d = divmod(n, 2)
                b = n % 2
                v.wait_ge(S["exp_ready"], 4 * (n + 1))
                kn = k_fm[:, c, 0:P] if d == 0 else k_fm[:, c, P:2 * P]
                near = kv[n][:, 0:KNEAR].rearrange("p (b j) -> p b j", b=NPT)
                far = kv[n][:, KNEAR:KV].rearrange("p (b j) -> p b j", b=NPT)
                step(TT(near, near, bc(kn.rearrange("p (a j) -> p a j", a=1), [P, NPT, P]), ALU.mult))
                step(TT(far, far, bc(k_fm[:, c, 0:T].rearrange("p (a j) -> p a j", a=1), [P, NPT, T]), ALU.mult))
                step(TT(qv[b], qv[b], q_fm[:, c, :], ALU.mult))
                step(TT(qd[n], qd[n], q_fm[:, c, :], ALU.mult))
                TT(kx[b], kx[b], k_fm[:, c, T:T + TX], ALU.mult).then_inc(S["kvmul_ready"], 1)

            def scores(n):
                c, d = divmod(n, 2)
                if n == 0:
                    v.wait_ge(S["kvarg_ready"], 1)
                if n >= 2:
                    v.wait_ge(S["o_done"], 1)
                for e in range(2):
                    v.wait_ge(S["score_done"], 2 * n + e + 1)
                    TT(pt[:, d, e, :], bank[e][:, 0:SPAN], mask[d], ALU.mult).then_inc(S["pt_ready"], 1)
                v.wait_ge(S["misc_read"], M_GLA[n])
                misc_read(V.tensor_copy(kxT, misc_wait(M_GLA[n])[:, 0:256]))
                misc_read(V.tensor_copy(gS[:, d, :], misc_wait(M_GLA[n] + 1)[:, 0:DV]))

            args(0)
            v.wait_ge(S["negA_ready"], 1)
            v.wait_ge(S["dt_sp"], 1)
            step.settle()
            step(TT(dta, dta, dtt, ALU.add))
            step.settle()
            for d in range(2):
                step(TT(a_tm[:, :, d, :], dta[:, :, d, :], bc(negA3[:, d:d + 1, :], [P, 4, SH]), ALU.mult))
            step.settle()
            TS(a_tm, a_tm, -1.0, None, ALU.mult).then_inc(S["dt_exp"], 1)
            args(1)
            for g in range(SG):
                b = misc_wait(M_CB + g)
                step(TT(cbm[:, 0, g, 0:256], b[:, 0:256], mask[0][:, 0:256], ALU.mult))
                step(TT(cbm[:, 0, g, 256:384], b[:, 384:512], mask[0][:, 256:384], ALU.mult))
                step(TT(cbm[:, 1, g, 0:128], b[:, 0:128], mask[1][:, 0:128], ALU.mult))
                misc_read(TT(cbm[:, 1, g, 128:384], b[:, 256:512], mask[1][:, 128:384], ALU.mult))
            misc_read(V.tensor_copy(b_tm.rearrange("p t g s -> p (t g s)"), misc_wait(M_B)))
            misc_read(V.tensor_copy(acol.rearrange("p t d h -> p (t d h)"), misc_wait(M_ACOL)[:, 0:64]))
            mults(0)
            scores(0)
            args(2)
            mults(1)
            scores(1)
            args(3)
            mults(2)
            scores(2)
            mults(3)
            scores(3)

            v.wait_ge(S["tm_done"], len(TM))
            for i in range(2):
                misc_read(V.tensor_copy(xs_tm[:, X_ORDER[i], :], misc_wait(M_X + i)))
            v.wait_ge(S["misc_read"], M_X + 2)
            v.wait_ge(S["eac_ready"], 1)
            step(TT(dta[:, 2:4], dta[:, 2:4], eac[:, 2:4], ALU.mult))
            step.settle()
            hp = lambda ap: ap.rearrange("p (h q) -> p h q", h=SH)
            for d in range(2):
                for t in range(2):
                    last = TT(hp(xw[:, t, d, :]), hp(xs_tm[:, 2 + t, :]),
                              bc(dta[:, 2 + t, d, :].rearrange("p (h q) -> p h q", q=1), [P, SH, HP]), ALU.mult)
                    if t == 0:
                        step(last)
                last.then_inc(S["xw_ready"], 1)
            for i in range(2, 4):
                misc_read(V.tensor_copy(xs_tm[:, X_ORDER[i], :], misc_wait(M_X + i)))
            v.wait_ge(S["misc_read"], M_X + 4)
            for d in range(2):
                for t in range(2):
                    step(TT(hp(xdt[:, t, d, :]), hp(xs_tm[:, t, :]),
                            bc(dta[:, t, d, :].rearrange("p (h q) -> p h q", q=1), [P, SH, HP]), ALU.mult))
            ya = y_acc.rearrange("p (t c) -> p t c", t=2)
            for t in range(2):
                step(TT(hp(ya[:, t, :]), hp(xs_tm[:, t, :]),
                        bc(d_row.rearrange("p (h q) -> p h q", q=1), [P, SH, HP]), ALU.mult))
            for d in range(2):
                misc_read(V.tensor_copy(sS[:, d, :], misc_wait(M_ST + d)))
            v.wait_ge(S["xw_ready"], 2)
            ytmp = hA[:, 0:512]
            for t in range(2):
                for d in range(2):
                    b = misc_wait(M_YOFF + 2 * t + d)
                    v.wait_ge(S["misc_read"], M_YOFF + 2 * t + d)
                    step.settle()
                    misc_read(TT(hp(ytmp), hp(b), bc(eac[:, t, d, :].rearrange("p (h q) -> p h q", q=1), [P, SH, HP]),
                                 ALU.mult))
                    v.wait_ge(S["misc_read"], M_YOFF + 2 * t + d + 1)
                    step(TT(ya[:, t, :], ya[:, t, :], ytmp, ALU.add))
            step.settle()

            v.wait_ge(S["gla_sq"], 1)
            step(TS(stat[:, 0:8], stat[:, 0:8], 1.0 / DV, EPS, ALU.mult, ALU.add))
            step.settle()
            V.reciprocal(stat[:, 0:8], stat[:, 0:8]).then_inc(S["gst"], 1)

            def seg_arg(i):
                h, d = divmod(i, 2)
                s = seg[i % 4]
                b = rb_bank(i)
                v.wait_ge(S["rb_done"], i + 1)
                if i >= 4:
                    v.wait_ge(S["ydiag_done"], (i - 4) // 2 + 1)
                spans = [(0, 0, 256, 0), (256, 128, 256, 1)] if d == 0 else [(0, 0, 128, 0), (128, 0, 256, 1)]
                for x, (to, c0, c1, jt) in enumerate(spans):
                    ins = TS(s[:, to:to + c1 - c0], b[:, c0:c1], acol[:, jt, d, h:h + 1], 0.0, ALU.subtract, ALU.min)
                    if x == 0:
                        step(ins)
                        step.settle()
                    else:
                        ins.then_inc(S["arg_ready"], 1)

            def seg_mult(i):
                h, d = divmod(i, 2)
                v.wait_ge(S["segexp_ready"], i + 1)
                TT(seg[i % 4], seg[i % 4], cbm[:, d, h // HPG, :], ALU.mult).then_inc(S["segm_ready"], 1)

            v.wait_ge(S["o_done"], 2)
            seg_arg(0)
            for i in range(2 * SH):
                if i + 1 < 2 * SH:
                    seg_arg(i + 1)
                seg_mult(i)
                if i == 4:
                    v.wait_ge(S["gsq"], 1)
                    v.wait_ge(S["silu_ready"], 1)
                    for a in range(8):
                        o = o_sb[:, a * DV:(a + 1) * DV]
                        step(STT(out=o, in0=o, scalar=stat[:, a:a + 1], in1=gnrow, op0=ALU.mult, op1=ALU.mult))
                if i == 6:
                    step.settle()
                    gv = vgz[:, :, 512:1024]
                    TT(gv, gv, o_sb.rearrange("p (t c) -> p t c", t=2), ALU.mult).then_inc(S["mix_ready"], 1)
            v.wait_ge(S["segm_ready"], 2 * SH)

            v.wait_ge(S["ydiag_done"], SH)
            for t in range(2):
                step(TT(ya[:, t, :], ya[:, t, :], bank[5 + t], ALU.add))
            step.settle()
            for t in range(2):
                TT(ya[:, t, :], ya[:, t, :], vgz[:, t, 1024:1536], ALU.mult).then_inc(S["yz_ready"], 1)
            v.wait_ge(S["ssd_sq"], 1)
            step(TS(stat[:, 8:12], stat[:, 8:12], SG / SI, EPS, ALU.mult, ALU.add))
            step.settle()
            V.reciprocal(stat[:, 8:12], stat[:, 8:12]).then_inc(S["sst"], 1)
            v.wait_ge(S["ssq"], 1)
            v.wait_ge(S["sn_in"], 16)
            for t in range(2):
                for g in range(SG):
                    c = slice(256 * g, 256 * (g + 1))
                    last = STT(out=vgz[:, t, 1024 + 256 * g:1024 + 256 * (g + 1)], in0=ya[:, t, c],
                               scalar=stat[:, 8 + 2 * t + g:9 + 2 * t + g], in1=snrow[:, c], op0=ALU.mult, op1=ALU.mult)
            last.then_inc(S["mix_ready"], 1)
            v.wait_ge(S["late_in"], 64)
            v.wait_ge(S["misc_read"], M_ROWS[5] + 1)
            step(TT(w2b, w2b, n2row, ALU.mult))
            step(V.memset(RT, -1.0))
            step(V.memset(GT, 0.0))
            for t in range(2):
                for half in range(2):
                    r = 2 * t + half
                    v.wait_ge(S["op_done"], 5 + r)
                    cols = slice(512 * half, 512 * half + 512)
                    tm_ = fB[:, 3072 + 512 * half:3584 + 512 * half] if t else fB[:, cols]
                    TT(tm_, op_bank(r), g1b[:, cols], ALU.mult).then_inc(S["op_read"], 1)
                    v.wait_ge(S["op_read"], r + 1)
                    TT(x_tm[:, t, cols], x_tm[:, t, cols], tm_, ALU.add).then_inc(S["xnew_ready"], 1)
                st = stat[:, 22 + t:23 + t]
                v.wait_ge(S["nsq"], 3 * t + 1)
                step(TS(st, stat[:, 20 + t:21 + t], 1.0 / D, EPS, ALU.mult, ALU.add))
                v.wait_ge(S["nsq"], 3 * t + 2)
                step.settle()
                step(STT(out=st, in0=stat[:, 24 + t:25 + t], scalar=1.0 / D, in1=st, op0=ALU.mult, op1=ALU.add))
                step.settle()
                V.reciprocal(st, st).then_inc(S["nst"], 1)
                v.wait_ge(S["nsq"], 3 * t + 3)
                halves = [slice(512 * half, 512 * half + 512) for half in range(2)]
                for c in halves:
                    step(STT(out=h2[:, t, c], in0=x_tm[:, t, c], scalar=st, in1=w2b[:, c], op0=ALU.mult, op1=ALU.mult))
                step.settle()
                for c in halves:
                    TT(h2[:, t, c], h2[:, t, c], sh2b[:, c], ALU.add).then_inc(S["h2_ready"], 1)
                if t == 0:
                    v.wait_ge(S["misc_read"], M_ROWS[7] + 1)
                    V.memset(ysb, 0.0).then_inc(S["y_ready"], 1)
            TS(job_sel, part_no[0:PARTS * NE, :], 0.0, None, ALU.is_equal).then_inc(S["sel_ready"], 1)
            v.wait_ge(S["log_done"], 2)
            b = bank[5][:, 0:2 * NE].rearrange("p (t e) -> p t e", t=2)
            step(TT(lg, b, bc(brrow.rearrange("p (a e) -> p a e", a=1), [P, 2, NE]), ALU.add))
            step.settle()
            for t in range(2):
                step(V.max(top8[:, t, :], lg[:, t, :]))
            step.settle()
            sel, eq, ce, ex = rt
            for t in range(2):
                m4 = top8[:, t, 3:4]
                step(TS(sel[:, t, :], lg[:, t, :], m4, None, ALU.is_gt))
                step(TS(eq[:, t, :], lg[:, t, :], m4, None, ALU.is_equal))
            step.settle()
            for t in range(2):
                last = TS(ex[:, t, :], lg[:, t, :], top8[:, t, 0:1], None, ALU.subtract)
                if t == 0:
                    step(last)
            last.then_inc(S["ex_ready"], 1)
            for t in range(2):
                step(V.tensor_tensor_scan(ce[:, t, :], bc(ones[:, 0:1], [P, NE]), eq[:, t, :], 0.0, ALU.mult, ALU.add))
            step(V.tensor_reduce(stat[:, 28:30], sel, AX.X, ALU.add))
            step.settle()
            for t in range(2):
                step(TS(ce[:, t, :], ce[:, t, :], stat[:, 28 + t:29 + t], 4.5, ALU.add, ALU.is_lt))
            step.settle()
            step(TT(eq, eq, ce, ALU.mult))
            step.settle()
            TT(sel, sel, eq, ALU.add).then_inc(S["sel_made"], 1)
            v.wait_ge(S["sel_made"], 1)
            v.wait_ge(S["ex_done"], 1)
            step(TT(ex, ex, sel, ALU.mult))
            step.settle()
            step(V.tensor_reduce(stat[:, 28:30], ex, AX.X, ALU.add))
            step.settle()
            step(V.reciprocal(stat[:, 28:30], stat[:, 28:30]))
            step.settle()
            for t in range(2):
                step(TS(GT[:, t, 0:NE], ex[:, t, :], stat[:, 28 + t:29 + t], None, ALU.mult))
            v.wait_ge(S["rank_done"], 1)
            b = bank[6][:, 0:3 * NE].rearrange("p (i e) -> p i e", i=3)
            step(STT(out=eq, in0=b[:, 0:2, :], scalar=1.0, in1=sel, op0=ALU.add, op1=ALU.mult))
            step.settle()
            step(TS(RT[:, :, 0:NE], eq, -1.0, None, ALU.add))
            step.settle()


            def select_tokens(slots, own):
                for t in range(2):
                    last = TS(S_j[:, t, :], slots, own[:, t, :], None, ALU.is_equal)
                last.then_inc(S["s_ready"], 1)

            def select_gates(slots2, own, gate):
                for t in range(2):
                    last = TS(SG_j[:, t, :], slots2, own[:, t, :], gate[:, t, :], ALU.is_equal, ALU.mult)
                last.then_inc(S["sg_ready"], 1)

            def select_expert(j):
                TS(job_sel, part_no[0:PARTS * NE, :], JE[0:PARTS * NE, bass.ds(j, 1)], None, ALU.is_equal
                   ).then_inc(S["sel_ready"], 1)

            def xg_copy(j):
                v.wait_ge(S["gather_done"], j + 1)
                V.tensor_copy(xg.rearrange("p k s -> p (k s)"), bank[3]).then_inc(S["xg_ready"], 1)

            def job(j):
                v.wait_ge(S["gather_done"], j + 1)
                e = v.value_load(int_e(j + 1), min_val=0, max_val=NE)
                q = v.value_load(int_q(j + 1), min_val=0, max_val=T // SLOTS - 1)
                select_tokens(slot_q[:, bass.ds(q * (2 * SLOTS), SLOTS)], RT[:, :, bass.ds(e, 1)])
                v.wait_ge(S["moe_used"], NSLOT * j + KC)
                TS(gm, bank[0], LIMIT, None, ALU.min).then_inc(S["gm_ready"], 1)
                TS(act, bank[1], LIMIT, -LIMIT, ALU.min, ALU.max).then_inc(S["up_read"], 1)
                v.wait_ge(S["up_read"], 2 * j + 1)
                v.wait_ge(S["gm_ready"], j + 1)
                STT(out=act, in0=act, scalar=1.0, in1=gm, op0=ALU.add, op1=ALU.mult).then_inc(S["up_read"], 1)
                v.wait_ge(S["up_read"], 2 * j + 2)
                v.wait_ge(S["sig_ready"], j + 1)
                TT(act, act, sig, ALU.mult).then_inc(S["act_ready"], 1)
                v.wait_ge(S["sgt_done"], j + 1)
                v.wait_ge(S["scat_done"], j + 1)
                V.tensor_copy(SGT, bank[2][:, 0:256].rearrange("p (t c) -> p t c", t=2)).then_inc(S["sgt_ready"], 1)
                v.wait_ge(S["actT_done"], j + 1)
                V.tensor_copy(actT, bank[0].rearrange("p (q c) -> p q c", q=4)).then_inc(S["actT_ready"], 1)
                xg_copy(j + 1)
                select_gates(slot_q[:, bass.ds(q * (2 * SLOTS), 2 * SLOTS)], RT[:, :, bass.ds(e, 1)],
                             GT[:, :, bass.ds(e, 1)])
                v.wait_ge(S["sel_used"], j + 1)
                select_expert(j + 1)
                v.wait_ge(S["moe_used"], NSLOT * (j + 1))
                V.tensor_copy(ysb, bank[2]).then_inc(S["y_ready"], 1)

            select_tokens(slot_no[:, 0:SLOTS], RT[:, :, 0:1])
            step(V.tensor_copy(cnt[:, 2, :], b[:, 2, :]))
            select_gates(slot_no, RT[:, :, 0:1], GT[:, :, 0:1])
            V.memset(SGT, 0.0).then_inc(S["sgt_ready"], 1)
            step.settle()
            last_jobs(nc, S, step, cnt[:, 2, :], cnt[:, 0, :], cnt[:, 1, :], ints[:, 2 * (NJ + 1):], ones)
            xg_copy(0)
            v.wait_ge(S["slots_ready"], 2)
            job_tables(nc, S, step, cnt[:, 0, :], cnt[:, 1, :], job_no, jobs_w, JE, JQ, ints)
            v.wait_ge(S["job_tables"], 1)
            job(0)
            with v.Fori(1, NE) as j:
                job(j)
            last = v.value_load(int_last(NE - 1), min_val=NE - 1, max_val=NJ - 1)
            with v.Fori(NE, NE + FEW) as j:
                with v.If(last > j - 1):
                    job(j)
            with v.If(last > NE + FEW - 1):
                with v.Fori(NE + FEW, NJ) as j:
                    with v.If(last > j - 1):
                        job(j)
            for r in range(4):
                t, half = divmod(r, 2)
                cols = slice(512 * half, 512 * half + 512)
                part = fB[:, 512 * r:512 * (r + 1)]
                v.wait_ge(S["moe_done"], r + 1)
                step(TT(part, bank[4 + r], g2b[:, cols], ALU.mult))
                step.settle()
                TT(x_tm[:, t, cols], x_tm[:, t, cols], part, ALU.add).then_inc(S["fsq"], 1)
            for t in range(NT):
                v.wait_ge(S["fst"], 2 * t + 2)
                st = stat[:, 26 + t:27 + t]
                step(TS(st, stat[:, 24 + t:25 + t], stat[:, 28 + t:29 + t], 1.0 / D, ALU.add, ALU.mult))
                step.settle()
                step(TS(st, st, EPS, None, ALU.add))
                step.settle()
                V.reciprocal(st, st).then_inc(S["fsq"], 1)
            for t in range(NT):
                v.wait_ge(S["fst"], 2 * NT + t + 1)
                STT(out=x_tm[:, t, :], in0=x_tm[:, t, :], scalar=stat[:, 26 + t:27 + t], in1=fnrow, op0=ALU.mult,
                    op1=ALU.mult).then_inc(S["out_ready"], 1)


def kernel(**inputs):
    import numpy as np
    import concourse.bacc as bacc
    from concourse.bass_utils import run_bass_kernel_spmd

    g = {k: np.asarray(v) for k, v in inputs.items()}
    w_in = g["w_in"][0]
    off = np.cumsum([0, 256, 256, 512, 512, RANK, 512, 1024, SH])
    q, k, v, gg, gk, z, xbc, dt = (w_in[:, off[i]:off[i + 1]] for i in range(8))
    units = np.concatenate([xbc, k, q, v, gg, z], axis=1)
    arr = {
        "x": g["x"][0],
        "xT": g["x"][0].T.reshape(KC, P, T),
        "ctxT": g["ctx"][0].T.reshape(KC, P, TX),
        "c2": np.stack([g["c"][0], g["c_ctx"]], axis=1).reshape(KC, P, 2),
        "w_mod": g["w_mod"][0],
        "bmodT": g["b_mod"][0][:2048].reshape(16, P).T,
        "b_mod2": g["b_mod"][0][2048:].reshape(2, 4, 512),
        "n1T": g["norm1"][0].reshape(KC, P).T,
        "w_in": units.reshape(KC, P, N_IN, 256).transpose(2, 1, 0, 3).reshape(N_IN, P, UNIT),
        "wgk": gk.reshape(KC, P, RANK),
        "wdt": dt.reshape(KC, P, SH),
        "wup": g["gla_w_gk_up"][0].transpose(1, 0, 2),
        "bgk": g["gla_b_gk"][0].reshape(2, 2, P).transpose(2, 1, 0).reshape(P, 4),
        "convw": g["ssd_conv_w"][0].reshape(9, 8, P).transpose(2, 1, 0),
        "convb": g["ssd_conv_b"][0].reshape(8, P).T,
        "gla_norm": g["gla_norm"][0],
        "ssd_norm": g["ssd_norm"][0],
        "ssd_D": g["ssd_D"][0],
        "dtb": g["ssd_dt_bias"][0].reshape(16),
        "alog": g["ssd_A_log"][0].reshape(16),
        "w_out": g["w_out"][0],
        "norm2": g["norm2"][0],
        "final_norm": g["final_norm"],
        "w_router": g["w_router"][0],
        "b_router": g["b_router"][0],
        "w_gate_up": g["w_gate_up"][0],
        "w_down": g["w_down"][0],
        "b_moe": np.concatenate([g["b_gate_up"][0], g["b_down"][0]], axis=1),
    }
    nc = bacc.Bacc("TRN2", target_bir_lowering=False, num_devices=1)
    arrays, A = {}, {}
    for name, a in arr.items():
        a = np.ascontiguousarray(a)
        arrays[f"in_{name}"] = a
        A[name] = nc.dram_tensor(f"in_{name}", a.shape, mybir.dt.from_np(a.dtype), kind="ExternalInput").ap()
    out = nc.dram_tensor("out_0", (1, T, D), F32, kind="ExternalOutput").ap()
    layer_kernel(nc, A, out)
    return run_bass_kernel_spmd(nc, [arrays], core_ids=[0]).results[0]["out_0"]
```
